# Optimizing a Trainium2 kernel written in Bass

```python
import math, functools
import jax, jax.numpy as jnp
from jax import lax
import numpy as np

D_MODEL = 1024
BATCH = 1
SEQ = 128
DEPTH = 2
DEC_BATCH = 1
DEC_SEQ = 512
PAST_LEN = 128

GRID_W = 64
N_MIXERS = 2
N_ATTN_LAYERS = (DEPTH + 1) // 2
N_SSM_LAYERS = DEPTH // 2
N_HEADS = 16
N_KV_HEADS = 4
HEAD_DIM = 64
Q_WIDTH = N_HEADS * HEAD_DIM
KV_WIDTH = N_KV_HEADS * HEAD_DIM
WINDOW = 128
BLOCK = 128
ROPE_BASE = 10000.0
SSM_WIDTH = D_MODEL
SSM_GROUP = 16
N_GROUPS = SSM_WIDTH // SSM_GROUP
STATE = 64
SSM_CHUNK = 128
D_FF = -(-8 * D_MODEL // (3 * 256)) * 256
DN_ALPHA = (2 * DEPTH) ** 0.25
DN_BETA = (8 * DEPTH) ** -0.25
LN_EPS = 1e-5
NEG_INF = -1e30

kernel_name = "hybrid_swa_s5_diffusion_step"

def layer_norm(x, g, b):
    xf = x.astype(jnp.float32)
    mu = jnp.mean(xf, -1, keepdims=True)
    var = jnp.mean(jnp.square(xf - mu), -1, keepdims=True)
    return ((xf - mu) * lax.rsqrt(var + LN_EPS) * g + b).astype(x.dtype)

def ada_params(cvec, w, b):
    m = (jax.nn.silu(cvec) @ w + b).reshape(cvec.shape[0], 6, 1, D_MODEL)
    return [m[:, i] for i in range(6)]

def modulate(x, shift, scale):
    return x * (1 + scale) + shift

def swiglu(h, w1, w3, w2):
    return (jax.nn.silu(h @ w1) * (h @ w3)) @ w2

def trunk_layer(x, mods, mixer, ln_g, ln_b, w1, w3, w2):
    sh1, sc1, g1, sh2, sc2, g2 = mods
    out, extra = mixer(modulate(x, sh1, sc1))
    x = layer_norm(DN_ALPHA * x + g1 * out, ln_g[0], ln_b[0])
    x = layer_norm(DN_ALPHA * x + g2 * swiglu(modulate(x, sh2, sc2), w1, w3, w2), ln_g[1], ln_b[1])
    return x, extra

def split_qkv(h, w):
    n, t, _ = h.shape
    qkv = h @ w
    q = qkv[..., :Q_WIDTH].reshape(n, t, N_HEADS, HEAD_DIM)
    k = qkv[..., Q_WIDTH:Q_WIDTH + KV_WIDTH].reshape(n, t, N_KV_HEADS, HEAD_DIM)
    v = qkv[..., Q_WIDTH + KV_WIDTH:].reshape(n, t, N_KV_HEADS, HEAD_DIM)
    return q, k, v

def sink_softmax(s, sink):
    m = jnp.maximum(jnp.max(s, -1, keepdims=True), sink)
    p = jnp.exp(s - m)
    return p / (jnp.sum(p, -1, keepdims=True) + jnp.exp(sink - m))

def axial_rope_angles(t):
    n_rows = t // GRID_W
    row = jnp.repeat(jnp.arange(n_rows, dtype=jnp.float32), GRID_W)
    col = (jnp.arange(t) % GRID_W).astype(jnp.float32)
    nfreq = HEAD_DIM // 4
    inv = jnp.power(ROPE_BASE, -jnp.arange(nfreq, dtype=jnp.float32) / nfreq)
    return row[:, None] * inv, col[:, None] * inv

def rotate_half(x, ang):
    x1, x2 = jnp.split(x, 2, -1)
    c = jnp.cos(ang)[None, :, None, :].astype(x.dtype)
    s = jnp.sin(ang)[None, :, None, :].astype(x.dtype)
    return jnp.concatenate([x1 * c - x2 * s, x1 * s + x2 * c], -1)

def apply_axial_rope(x, ang_row, ang_col):
    xr, xc = jnp.split(x, 2, -1)
    return jnp.concatenate([rotate_half(xr, ang_row), rotate_half(xc, ang_col)], -1)

def context_attention(q, k, v, sink):
    n, L = q.shape[:2]
    g = N_HEADS // N_KV_HEADS
    qb = q.reshape(n, L // BLOCK, BLOCK, N_KV_HEADS, g, HEAD_DIM).swapaxes(0, 1)
    sink_b = sink.astype(jnp.float32).reshape(1, N_KV_HEADS, g, 1, 1)
    scale = HEAD_DIM ** -0.5

    def one_block(qj):
        s = jnp.einsum('nqkgd,nskd->nkgqs', qj, k, preferred_element_type=jnp.float32) * scale
        p = sink_softmax(s, sink_b).astype(v.dtype)
        return jnp.einsum('nkgqs,nskd->nqkgd', p, v)

    o = lax.map(one_block, qb)
    return o.swapaxes(0, 1).reshape(n, L, Q_WIDTH)

def latent_attention(q_rot, q_plain, k_rot, v, k_ctx, v_ctx, sink):
    n, t = q_rot.shape[:2]
    g = N_HEADS // N_KV_HEADS
    L = k_ctx.shape[1]
    kp = jnp.pad(k_rot, ((0, 0), (BLOCK, BLOCK), (0, 0), (0, 0)))
    vp = jnp.pad(v, ((0, 0), (BLOCK, BLOCK), (0, 0), (0, 0)))
    sink_b = sink.astype(jnp.float32).reshape(1, N_KV_HEADS, g, 1, 1)
    scale = HEAD_DIM ** -0.5
    q_offs = jnp.arange(BLOCK)
    k_offs = jnp.arange(3 * BLOCK) - BLOCK

    def one_block(j):
        start = j * BLOCK
        qr = lax.dynamic_slice_in_dim(q_rot, start, BLOCK, axis=1).reshape(n, BLOCK, N_KV_HEADS, g, HEAD_DIM)
        qp = lax.dynamic_slice_in_dim(q_plain, start, BLOCK, axis=1).reshape(n, BLOCK, N_KV_HEADS, g, HEAD_DIM)
        kj = lax.dynamic_slice_in_dim(kp, start, 3 * BLOCK, axis=1)
        vj = lax.dynamic_slice_in_dim(vp, start, 3 * BLOCK, axis=1)
        qpos = start + q_offs
        kpos = start + k_offs
        valid = (kpos[None, :] >= 0) & (kpos[None, :] < t) & (jnp.abs(qpos[:, None] - kpos[None, :]) <= WINDOW)
        s_loc = jnp.einsum('nqkgd,nskd->nkgqs', qr, kj, preferred_element_type=jnp.float32) * scale
        s_loc = jnp.where(valid, s_loc, NEG_INF)
        s_ctx = jnp.einsum('nqkgd,nskd->nkgqs', qp, k_ctx, preferred_element_type=jnp.float32) * scale
        p = sink_softmax(jnp.concatenate([s_ctx, s_loc], -1), sink_b).astype(v.dtype)
        return (jnp.einsum('nkgqs,nskd->nqkgd', p[..., :L], v_ctx)
                + jnp.einsum('nkgqs,nskd->nqkgd', p[..., L:], vj))

    o = lax.map(one_block, jnp.arange(t // BLOCK))
    return o.swapaxes(0, 1).reshape(n, t, Q_WIDTH)

def ctx_attn_mixer(h, w_qkv_a, w_o_a, sink_a):
    q, k, v = split_qkv(h, w_qkv_a)
    return context_attention(q, k, v, sink_a) @ w_o_a, (k, v)

def lat_attn_mixer(h, k_ctx, v_ctx, ang_row, ang_col, w_qkv_a, w_o_a, sink_a):
    q, k, v = split_qkv(h, w_qkv_a)
    o = latent_attention(apply_axial_rope(q, ang_row, ang_col), q,
                         apply_axial_rope(k, ang_row, ang_col), v, k_ctx, v_ctx, sink_a)
    return o @ w_o_a, None

def s5_discretise(lam_re, lam_im, log_dt, b_re, b_im):
    lam_re = lam_re.astype(jnp.float32)
    lam_im = lam_im.astype(jnp.float32)
    dt = jnp.exp(log_dt.astype(jnp.float32))[:, None]
    mag = jnp.exp(lam_re * dt)
    a_re = mag * jnp.cos(lam_im * dt)
    a_im = mag * jnp.sin(lam_im * dt)
    den = lam_re ** 2 + lam_im ** 2
    nr, ni = a_re - 1.0, a_im
    coef_re = ((nr * lam_re + ni * lam_im) / den)[..., None]
    coef_im = ((ni * lam_re - nr * lam_im) / den)[..., None]
    b_re = b_re.astype(jnp.float32)
    b_im = b_im.astype(jnp.float32)
    bb_re = coef_re * b_re - coef_im * b_im
    bb_im = coef_re * b_im + coef_im * b_re
    return a_re, a_im, bb_re, bb_im

def complex_linear_combine(e1, e2):
    a1r, a1i, b1r, b1i = e1
    a2r, a2i, b2r, b2i = e2
    return (a2r * a1r - a2i * a1i, a2r * a1i + a2i * a1r,
            a2r * b1r - a2i * b1i + b2r, a2r * b1i + a2i * b1r + b2i)

def s5_direction(u, h0_re, h0_im, lam_re, lam_im, log_dt, b_re, b_im, c_re, c_im, reverse):
    a_re, a_im, bb_re, bb_im = s5_discretise(lam_re, lam_im, log_dt, b_re, b_im)
    c_re = c_re.astype(jnp.float32)
    c_im = c_im.astype(jnp.float32)
    n, t = u.shape[:2]
    if reverse:
        u = jnp.flip(u, 1)
    uc = u.reshape(n, t // SSM_CHUNK, SSM_CHUNK, N_GROUPS, SSM_GROUP).swapaxes(0, 1)
    a_r = jnp.broadcast_to(a_re[None, None], (SSM_CHUNK, 1, N_GROUPS, STATE))
    a_i = jnp.broadcast_to(a_im[None, None], (SSM_CHUNK, 1, N_GROUPS, STATE))

    def chunk(carry, u_blk):
        hr, hi = carry
        bu_r = jnp.einsum('ncgm,gpm->cngp', u_blk, bb_re)
        bu_i = jnp.einsum('ncgm,gpm->cngp', u_blk, bb_im)
        bu_r = bu_r.at[0].add(a_re * hr - a_im * hi)
        bu_i = bu_i.at[0].add(a_re * hi + a_im * hr)
        _, _, sr, si = lax.associative_scan(complex_linear_combine, (a_r, a_i, bu_r, bu_i), axis=0)
        y = jnp.einsum('cngp,gmp->ncgm', sr, c_re) - jnp.einsum('cngp,gmp->ncgm', si, c_im)
        return (sr[-1], si[-1]), y

    (hr, hi), ys = lax.scan(chunk, (h0_re.astype(jnp.float32), h0_im.astype(jnp.float32)), uc)
    y = ys.swapaxes(0, 1).reshape(n, t, N_GROUPS, SSM_GROUP)
    if reverse:
        y = jnp.flip(y, 1)
    return y, hr, hi

def s5_mixer(h, h0_re, h0_im, w_in, lam_re, lam_im, log_dt, b_re, b_im, c_re, c_im, d_skip, w_glu, w_out):
    n, t, _ = h.shape
    u = (h @ w_in).astype(jnp.float32).reshape(n, t, N_GROUPS, SSM_GROUP)
    y_f, hfr, hfi = s5_direction(u, h0_re[:, 0], h0_im[:, 0], lam_re[0], lam_im[0], log_dt[0],
                                 b_re[0], b_im[0], c_re[0], c_im[0], False)
    y_b, hbr, hbi = s5_direction(u, h0_re[:, 1], h0_im[:, 1], lam_re[1], lam_im[1], log_dt[1],
                                 b_re[1], b_im[1], c_re[1], c_im[1], True)
    y = y_f + y_b + d_skip.astype(jnp.float32).reshape(N_GROUPS, SSM_GROUP) * u
    y = jax.nn.gelu(y.reshape(n, t, SSM_WIDTH)).astype(h.dtype)
    val, gate = jnp.split(y @ w_glu, 2, -1)
    out = (val * jax.nn.sigmoid(gate)) @ w_out
    return out, (jnp.stack([hfr, hbr], 1), jnp.stack([hfi, hbi], 1))

def setup_inputs(seed: int = 0) -> dict:
    key = jax.random.key(seed)
    ks = jax.random.split(key, 32)
    f32 = jnp.float32

    def nrm(k, shape, std):
        return std * jax.random.normal(k, shape, f32)

    n_idx = jnp.arange(STATE, dtype=f32)
    lam_shape = (N_SSM_LAYERS, 2, N_GROUPS, STATE)
    return {
        "x_prompt": nrm(ks[0], (BATCH, SEQ, D_MODEL), 1.0),
        "x_sample": nrm(ks[1], (DEC_BATCH, DEC_SEQ, D_MODEL), 1.0),
        "cache_k": nrm(ks[2], (DEC_BATCH, N_ATTN_LAYERS, PAST_LEN, N_KV_HEADS, HEAD_DIM), 1.0),
        "cache_v": nrm(ks[3], (DEC_BATCH, N_ATTN_LAYERS, PAST_LEN, N_KV_HEADS, HEAD_DIM), 1.0),
        "state_ssm_re": nrm(ks[4], (DEC_BATCH, N_SSM_LAYERS, 2, N_GROUPS, STATE), 0.3),
        "state_ssm_im": nrm(ks[5], (DEC_BATCH, N_SSM_LAYERS, 2, N_GROUPS, STATE), 0.3),
        "c": nrm(ks[6], (DEC_BATCH, D_MODEL), 1.0),
        "c_ctx": nrm(ks[7], (D_MODEL,), 1.0),
        "w_ada": nrm(ks[8], (DEPTH, D_MODEL, 6 * D_MODEL), 0.5 * D_MODEL ** -0.5),
        "b_ada": nrm(ks[9], (DEPTH, 6 * D_MODEL), 0.02),
        "ln_g": 1.0 + nrm(ks[10], (DEPTH, 2, D_MODEL), 0.02),
        "ln_b": nrm(ks[11], (DEPTH, 2, D_MODEL), 0.02),
        "w_qkv": nrm(ks[12], (N_ATTN_LAYERS, D_MODEL, Q_WIDTH + 2 * KV_WIDTH), D_MODEL ** -0.5),
        "w_o": nrm(ks[13], (N_ATTN_LAYERS, Q_WIDTH, D_MODEL), DN_BETA * Q_WIDTH ** -0.5),
        "attn_sink": nrm(ks[14], (N_ATTN_LAYERS, N_HEADS), 0.5),
        "ssm_w_in": nrm(ks[15], (N_SSM_LAYERS, D_MODEL, SSM_WIDTH), D_MODEL ** -0.5),
        "ssm_lam_re": -0.5 + nrm(ks[16], lam_shape, 0.01),
        "ssm_lam_im": math.pi * n_idx + nrm(ks[17], lam_shape, 0.01),
        "ssm_log_dt": jax.random.uniform(ks[18], (N_SSM_LAYERS, 2, N_GROUPS), f32,
                                         minval=math.log(1e-3), maxval=math.log(1e-1)),
        "ssm_b_re": nrm(ks[19], (N_SSM_LAYERS, 2, N_GROUPS, STATE, SSM_GROUP), (2 * SSM_GROUP) ** -0.5),
        "ssm_b_im": nrm(ks[20], (N_SSM_LAYERS, 2, N_GROUPS, STATE, SSM_GROUP), (2 * SSM_GROUP) ** -0.5),
        "ssm_c_re": nrm(ks[21], (N_SSM_LAYERS, 2, N_GROUPS, SSM_GROUP, STATE), STATE ** -0.5),
        "ssm_c_im": nrm(ks[22], (N_SSM_LAYERS, 2, N_GROUPS, SSM_GROUP, STATE), STATE ** -0.5),
        "ssm_d": nrm(ks[23], (N_SSM_LAYERS, SSM_WIDTH), 1.0),
        "ssm_w_glu": nrm(ks[24], (N_SSM_LAYERS, SSM_WIDTH, 2 * SSM_WIDTH), SSM_WIDTH ** -0.5),
        "ssm_w_out": nrm(ks[25], (N_SSM_LAYERS, SSM_WIDTH, D_MODEL), DN_BETA * SSM_WIDTH ** -0.5),
        "ffn_w1": nrm(ks[26], (DEPTH, D_MODEL, D_FF), D_MODEL ** -0.5),
        "ffn_w3": nrm(ks[27], (DEPTH, D_MODEL, D_FF), D_MODEL ** -0.5),
        "ffn_w2": nrm(ks[28], (DEPTH, D_FF, D_MODEL), DN_BETA * D_FF ** -0.5),
    }

def reference(x_prompt, x_sample, cache_k, cache_v, state_ssm_re, state_ssm_im, c, c_ctx,
              w_ada, b_ada, ln_g, ln_b, w_qkv, w_o, attn_sink,
              ssm_w_in, ssm_lam_re, ssm_lam_im, ssm_log_dt, ssm_b_re, ssm_b_im,
              ssm_c_re, ssm_c_im, ssm_d, ssm_w_glu, ssm_w_out,
              ffn_w1, ffn_w3, ffn_w2):
    def ssm_params(s):
        return (ssm_w_in[s], ssm_lam_re[s], ssm_lam_im[s], ssm_log_dt[s], ssm_b_re[s], ssm_b_im[s],
                ssm_c_re[s], ssm_c_im[s], ssm_d[s], ssm_w_glu[s], ssm_w_out[s])

    y = x_prompt
    zeros_state = jnp.zeros((x_prompt.shape[0], 2, N_GROUPS, STATE), jnp.float32)
    new_k, new_v, new_sr, new_si = [], [], [], []
    for l in range(DEPTH):
        mods = ada_params(c_ctx[None, :], w_ada[l], b_ada[l])
        if l % N_MIXERS == 0:
            a = l // N_MIXERS
            mixer = functools.partial(ctx_attn_mixer, w_qkv_a=w_qkv[a], w_o_a=w_o[a], sink_a=attn_sink[a])
        else:
            s = l // N_MIXERS
            mixer = functools.partial(s5_mixer, h0_re=zeros_state, h0_im=zeros_state,
                                      **dict(zip(('w_in', 'lam_re', 'lam_im', 'log_dt', 'b_re', 'b_im',
                                                  'c_re', 'c_im', 'd_skip', 'w_glu', 'w_out'), ssm_params(s))))
        y, extra = trunk_layer(y, mods, mixer, ln_g[l], ln_b[l], ffn_w1[l], ffn_w3[l], ffn_w2[l])
        if l % N_MIXERS == 0:
            new_k.append(extra[0])
            new_v.append(extra[1])
        else:
            new_sr.append(extra[0])
            new_si.append(extra[1])
    y_prompt = y

    z = x_sample
    ang_row, ang_col = axial_rope_angles(x_sample.shape[1])
    for l in range(DEPTH):
        mods = ada_params(c, w_ada[l], b_ada[l])
        if l % N_MIXERS == 0:
            a = l // N_MIXERS
            mixer = functools.partial(lat_attn_mixer, k_ctx=cache_k[:, a], v_ctx=cache_v[:, a],
                                      ang_row=ang_row, ang_col=ang_col,
                                      w_qkv_a=w_qkv[a], w_o_a=w_o[a], sink_a=attn_sink[a])
        else:
            s = l // N_MIXERS
            mixer = functools.partial(s5_mixer, h0_re=state_ssm_re[:, s], h0_im=state_ssm_im[:, s],
                                      **dict(zip(('w_in', 'lam_re', 'lam_im', 'log_dt', 'b_re', 'b_im',
                                                  'c_re', 'c_im', 'd_skip', 'w_glu', 'w_out'), ssm_params(s))))
        z, _ = trunk_layer(z, mods, mixer, ln_g[l], ln_b[l], ffn_w1[l], ffn_w3[l], ffn_w2[l])
    y_sample = z

    new_cache_k = jnp.stack(new_k, axis=1)
    new_cache_v = jnp.stack(new_v, axis=1)
    new_state_re = jnp.stack(new_sr, axis=1)
    new_state_im = jnp.stack(new_si, axis=1)
    return (y_prompt, y_sample, new_cache_k, new_cache_v, new_state_re, new_state_im)


_drawn_inputs = setup_inputs


def setup_inputs(seed=0):
    import zlib

    import numpy as np

    out = dict(_drawn_inputs(seed))
    spreads = {}
    factors = {'cache_k': 8.0,
     'cache_v': 8.0,
     'state_ssm_re': 7.498,
     'state_ssm_im': 7.562,
     'attn_sink': 45.435,
     'ssm_lam_re': 19.71,
     'ssm_c_re': 6.615,
     'ssm_c_im': 6.737}
    for name, (base, spread) in spreads.items():
        noise = np.random.default_rng([zlib.crc32(name.encode()), seed]).standard_normal(out[name].shape)
        drawn = base * np.exp(spread * noise) if base else spread * noise
        out[name] = __import__('jax').numpy.asarray(drawn.astype(out[name].dtype))
    for name, factor in factors.items():
        out[name] = (out[name] * factor).astype(out[name].dtype)
    return out
```

```python
from contextlib import ExitStack, nullcontext

import numpy as np

import concourse.bass as bass
from concourse import mybir

ACT = mybir.ActivationFunctionType
ALU = mybir.AluOpType
AXIS_X = mybir.AxisListType.X
F32 = mybir.dt.float32
F32R = mybir.dt.float32r

P = 128
D = 1024
KT = D // P
CTX = 128
LAT = 512
TOK = CTX + LAT
HALF = TOK // 2
FF = 2816
FF_TILES = FF // P
HEADS = 16
KV_HEADS = 4
HD = 64
GROUPS = 64
GCH = 16
STATE = 64
CHUNK = 8
NCHUNK = TOK // CHUNK
CCH = CTX // CHUNK
LCH = LAT // CHUNK
ALPHA = 4.0 ** 0.25
LN_EPS = 1e-5
SCALE = HD ** -0.5
NEG = -1e30
SLOTS = 4
MODQ = 6 * KT

PHASES = [(0, 8), (8, 8), (16, 6)]
STAGES = [("ada0", 48), ("qkv", 12), ("wo", 8)]
for _ph, (_f0, _n) in enumerate(PHASES):
    STAGES += [(f"up0{_ph}", 2 * _n), (f"down0{_ph}", 8)]
LAYERS = 2
if LAYERS == 2:
  STAGES += [("ada1", 48), ("win", 8), ("glu", 16), ("wout", 8)]
  for _ph, (_f0, _n) in enumerate(PHASES):
    STAGES += [(f"up1{_ph}", 2 * _n), (f"down1{_ph}", 8)]
BASE, COUNT = {}, {}
_at = 0
for _name, _n in STAGES:
    BASE[_name], COUNT[_name] = _at, _n
    _at += _n
PANELS = _at
PAIRS_BEFORE, _at = {}, 0
for _name, _n in STAGES:
    PAIRS_BEFORE[_name] = _at
    if _name.startswith("up") or _name == "glu":
        _at += _n // 2


def host_constants():
    ident = np.eye(P, dtype=np.float32)
    sel = np.zeros((P, 2), np.float32)
    for r in range(4):
        sel[r, r % 2] = 1.0
    masks = np.zeros((4, P, 4 * P), np.float32)
    q = np.arange(P)[:, None]
    k = np.arange(P)[None, :]
    masks[:, :, P:2 * P] = np.where(k >= q, 0.0, NEG)
    masks[:, :, 3 * P:] = np.where(k <= q, 0.0, NEG)
    masks[0, :, P:2 * P] = NEG
    masks[3, :, 3 * P:] = NEG
    t = np.arange(LAT)
    nf = HD // 4
    inv = np.power(np.float32(10000.0), -np.arange(nf, dtype=np.float32) / np.float32(nf)).astype(np.float32)
    ang = np.stack([(t // 64).astype(np.float32)[:, None] * inv, (t % 64).astype(np.float32)[:, None] * inv])
    rope = np.zeros((2, P, LAT), np.float32)
    for p in range(P):
        axis, half, f = (p % HD) // 32, (p % 32) // 16, p % 16
        rope[0, p] = np.cos(ang[axis, :, f])
        rope[1, p] = np.sin(ang[axis, :, f]) * (1.0 if half else -1.0)
    return {"k_ident": ident, "k_sel": sel, "k_masks": masks, "k_rope": rope}


class Chain:

    def __init__(self, eng, sem):
        self.eng, self.sem, self.n, self.i, self.per = eng, sem, 0, None, 0

    def value(self):
        return self.n if self.i is None else self.n + self.i * self.per

    def link(self, ins):
        self.n += 1
        ins.then_inc(self.sem, 1)
        self.eng.wait_ge(self.sem, self.value())

    def enter(self, i, per):
        self.i, self.per, self.start = i, per, self.n

    def leave(self, trips):
        assert self.n - self.start == self.per, (self.n - self.start, self.per)
        self.n, self.i = self.start + self.per * trips, None


def hybrid_step(nc, I, O):
    ctx = ExitStack()
    with ctx:
        def psum(name, shape):
            return ctx.enter_context(nc.psum_tensor(name, shape, F32))

        def sem(name):
            return ctx.enter_context(nc.semaphore(name))

        top = [((nc.sbuf_base + 63) // 64) * 64]

        def place(name, shape, dt=F32, at=None):
            size = int(np.prod(shape[1:])) * 4
            size = (size + 31) // 32 * 32
            where = top[0] if at is None else at
            t = nc.alloc_sbuf_tensor_at(name, shape, dt, offset=where)
            if at is None:
                top[0] += size
            return t, where + size

        def sb(name, shape, dt=F32):
            return place(name, shape, dt)[0]

        X = sb("X", [P, KT, TOK])
        RAW = sb("RAW", [P, SLOTS, KT, P])
        WH = sb("WH", [P, SLOTS, KT, P], F32R)
        WL = sb("WL", [P, SLOTS, KT, P], F32R)
        IDENT = sb("IDENT", [P, P])
        MEANW = sb("MEANW", [P, P])
        SEL = sb("SEL", [P, 2])
        EPS = sb("EPS", [P, 1])
        PV1 = sb("PV1", [P, P])
        PV2 = sb("PV2", [P, 56])
        MODS = sb("MODS", [P, 2, MODQ, 2])
        CS = sb("CS", [P, KT, 4], F32R)
        CS2 = sb("CS2", [P, KT, 4], F32R)
        SC = sb("SC", [P, 2, KT])
        XH = sb("XH", [P, KT, TOK], F32R)
        XL = sb("XL", [P, KT, TOK], F32R)
        AR, AI = sb("AR", [P, 2, GROUPS]), sb("AI", [P, 2, GROUPS])
        H0, FINS = sb("H0", [P, 2, GROUPS]), sb("FINS", [P, 2, GROUPS])
        common_end = top[0]
        HH, e = place("HH", [P, KT, TOK], F32R, at=common_end)
        HL, e = place("HL", [P, KT, TOK], F32R, at=e)
        GT, e = place("GT", [P, 2, TOK], at=e)
        HT, ffn_end = place("HT", [P, 2, TOK], at=e)
        ACC, e = place("ACC", [P, TOK], at=common_end)
        SQ, e = place("SQ", [P, 2, TOK], at=e)
        YT, e = place("YT", [P, 2, TOK], at=e)
        XM, e = place("XM", [P, 2, TOK], at=e)
        RSTD, e = place("RSTD", [P, TOK], at=e)
        RT, e = place("RT", [P, TOK], at=e)
        STD, ln_end = place("STD", [P, TOK], at=e)
        XN, e = place("XN", [P, 5, D], at=ln_end)
        SV, e = place("SV", [P, 2, P], at=e)
        ROWS, _e = place("ROWS", [4, 2, 2 * P], at=max(e, ffn_end))
        QKVT, e = place("QKVT", [P, 12, TOK], at=common_end)
        VN, e = place("VN", [P, 7, 2 * P], at=e)
        KR, e = place("KR", [P, 2, LAT + 2 * P], at=e)
        KCT, e = place("KCT", [P, 2, P], at=e)
        QB, e = place("QB", [P, 2, 4, P], at=e)
        VW, e = place("VW", [P, 3, 2 * P], at=e)
        KW, e = place("KW", [P, 3 * P], at=e)
        S, e = place("S", [P, 8, 4 * P], at=e)
        PT, e = place("PT", [P, 4, 4, P], at=e)
        MASK, e = place("MASK", [P, 4, 4 * P], at=e)
        ROPE, e = place("ROPE", [P, 2, LAT], at=e)
        SWAP, e = place("SWAP", [P, LAT], at=e)
        CK, e = place("CK", [P, 2 * P], at=e)
        CV, e = place("CV", [P, 2 * P], at=e)
        KN, e = place("KN", [P, 2 * P], at=e)
        SINK, e = place("SINK", [P, HEADS], at=e)
        STAT, e = place("STAT", [P, 8, 8], at=e)
        xh_at = common_end - 4 * 512 - 2 * KT * TOK * 4
        STRIP, e = place("STRIP", [P, 2, 8, 15 * GCH], at=xh_at)
        G, e = place("G", [P, 2, 9, 8, GCH], at=e)
        BTS, e = place("BTS", [P, 8, 2, P], at=e)
        KS, e = place("KS", [GCH, 8, 15 * GCH], at=e)
        assert e <= common_end - 4 * 512
        LAM, e = place("LAM", [GROUPS, 2, 2, STATE], at=common_end)
        GM, e = place("GM", [GROUPS, 6, 2, STATE], at=e)
        LDT, e = place("LDT", [GROUPS, 2], at=e)
        ZR, e = place("ZR", [GROUPS, P], at=e)
        ZI, e = place("ZI", [GROUPS, P], at=e)
        MAG, e = place("MAG", [GROUPS, P], at=e)
        SIN, e = place("SIN", [GROUPS, P], at=e)
        SINH, e = place("SINH", [GROUPS, P], at=e)
        T1, e = place("T1", [GROUPS, P], at=e)
        T2, e = place("T2", [GROUPS, P], at=e)
        T3, e = place("T3", [GROUPS, P], at=e)
        DB, small_end = place("DB", [GCH, D], at=e)
        CP, e = place("CP", [P, 2, 8, P], at=common_end)
        BBS, e = place("BBS", [P, 2, 8, GCH], at=e)
        assert e <= small_end
        BN, e = place("BN", [P, 2, GROUPS, GCH], at=small_end)
        BP, e = place("BP", [P, 2, 8, P], at=small_end)
        CN, e2 = place("CN", [P, 2, KT, 2, STATE], at=e)
        Q1, e = place("Q1", [P, 8, 8, GCH], at=e)
        Q2, e = place("Q2", [P, 8, 8, GCH], at=e)
        AC, e = place("AC", [P, 6, GROUPS], at=e2)
        CT, e = place("CT", [P, 2, KT, P], at=e)
        POW, e = place("POW", [P, 2, 9, GROUPS], at=e)
        POWB, e = place("POWB", [P, 2, 8, GROUPS], at=e)
        BB, e = place("BB", [P, 2, GROUPS, GCH], at=e)
        DI, e = place("DI", [GCH, GROUPS, GCH], at=e)
        W1, e = place("W1", [P, 9 * P], at=e)
        W2, e = place("W2", [P, 9 * P], at=e)
        assert e <= nc.sbuf_usable_end
        SSM_DMAS = 15
        ENT, e = place("ENT", [P, 2, GROUPS, NCHUNK], at=xh_at)
        U8, e = place("U8", [P, GROUPS, NCHUNK], at=common_end)
        YIN, e = place("YIN", [P, KT, TOK], at=common_end)
        ST, st_end = place("ST", [P, TOK // CHUNK + 2, 2, GROUPS], at=e)
        UT, _e = place("UT", [P, KT, TOK], at=e)
        Y8, _e = place("Y8", [P, GROUPS, NCHUNK], at=e)
        BT, _e = place("BT", [P, 2, 8, 2, P], at=st_end)
        CPL, e = place("CPL", [P, 2, 2, 8, P], at=st_end)
        TOEP, e = place("TOEP", [P, 2, 8, P], at=e)
        SC1, e = place("SC1", [P, 2, 2, GROUPS], at=e)
        SC2, e = place("SC2", [P, 2, 2, GROUPS], at=e)
        FIN, e = place("FIN", [GROUPS, 2, P], at=e)
        assert e <= nc.sbuf_usable_end, (e, nc.sbuf_usable_end)
        B_SCR = nc.dram_tensor("b_scratch", (KT, P, 16 * P), F32, kind="Internal").ap()
        C_SCR = nc.dram_tensor("c_scratch", (KT, P, 16 * P), F32, kind="Internal").ap()
        K_SCR = nc.dram_tensor("k_scratch", (GROUPS, GCH, 15 * GCH), F32, kind="Internal").ap()
        U_SCR = nc.dram_tensor("u_scratch", (D, TOK), F32, kind="Internal").ap()
        OUTN, _e = place("OUTN", [P, 2, D], at=common_end)
        assert e <= nc.sbuf_usable_end, (e, nc.sbuf_usable_end)

        PS = psum("PS", [P, 8, 512])
        PSF = PS[:, :, :].rearrange("p b n -> p (b n)")

        def halves(bank):
            return PS[:, bank:bank + 2, 0:HALF]

        def by_half(ap):
            return ap.rearrange("p (h t) -> p h t", h=2)

        raw_in = [sem(f"raw_in{u}") for u in range(SLOTS)]
        hi_ready = sem("hi_ready")
        lo_ready = sem("lo_ready")
        pe_done = sem("pe_done")
        psum_free = sem("psum_free")
        silu_done = sem("silu_done")
        hid_hi = sem("hid_hi")
        hid_lo = sem("hid_lo")
        dve_chain = sem("dve_chain")
        pool_chain = sem("pool_chain")
        act_chain = sem("act_chain")
        sink_in = sem("sink_in")
        small_in = sem("small_in")
        const_in = sem("const_in")
        x_in = sem("x_in")
        attn_in = sem("attn_in")
        memset_done = sem("memset_done")
        sv_t = sem("sv_t")
        pv_ready = sem("pv_ready")
        silu_c = sem("silu_c")
        cs_ready = sem("cs_ready")
        cs_lo = sem("cs_lo")
        rows_ready = sem("rows_ready")
        mods_ps = sem("mods_ps")
        mods_ready = sem("mods_ready")
        x_t = sem("x_t")
        x_ready = sem("x_ready")
        xm_ready = sem("xm_ready")
        xh_ready = sem("xh_ready")
        xl_ready = sem("xl_ready")
        ln_sum, ln_mean, ln_cent = sem("ln_sum"), sem("ln_mean"), sem("ln_cent")
        ln_sq, ln_sqsum, ln_std = sem("ln_sq"), sem("ln_sqsum"), sem("ln_std")
        ln_y, ln_x = sem("ln_y"), sem("ln_x")
        out_t, out_a, out_v = sem("out_t"), sem("out_a"), sem("out_v")
        out_dma = [sem(f"out_dma{u}") for u in range(2)]
        kv_out = sem("kv_out")
        (att_t, att_kv, att_qplain, att_qrot, att_vw, att_s, att_max, att_stat, att_exp, att_p, att_tr, att_pt,
         att_pv, att_oh, att_ol) = [sem("att_" + x) for x in (
             "t", "kv", "qplain", "qrot", "vw", "s", "max", "stat", "exp", "p", "tr", "pt", "pv", "oh", "ol")]
        ATTN_DMAS = 8
        (ssm_in, ssm_a, ssm_v, ssm_t, g_ready, cp_ready, kern_ps, ks_ready, ks_out, bp_ready, bt_ps, bt_ready, bt_out,
         cp_out, u_out, u_in, inc_ps, inc_a, inc_v, scan_t, scan_done, ent_a, ent_v, y_ps, y_ready, y_out, fin_ps,
         fin_ready, fin_out, gelu_done, gelu_hi, gelu_lo) = [sem("s5_" + x) for x in (
             "in", "a", "v", "t", "g", "cp", "kern_ps", "ks", "ks_out", "bp", "bt_ps", "bt", "bt_out", "cp_out",
             "u_out", "u_in", "inc_ps", "inc_a", "inc_v", "scan_t", "scan", "ent_a", "ent_v", "y_ps", "y", "y_out",
             "fin_ps", "fin", "fin_out", "gelu", "gelu_hi", "gelu_lo")]
        bt_in = [sem(f"s5_bt_in{u}") for u in range(2)]
        cp_in = [sem(f"s5_cp_in{u}") for u in range(2)]
        y_in = [sem(f"s5_y_in{m}") for m in range(KT)]
        pchain = Chain(nc.gpsimd, pool_chain)

        def loop(eng, trips):
            return eng.Fori(0, trips) if trips > 1 else nullcontext(0)

        def w_view(name, layer=0):
            return I[name][layer]

        def panel_parts(name, i, u):
            full = RAW[:, u, :, :]
            if name.startswith("ada"):
                w = I["w_ada"][int(name[3])].rearrange("(h k p) n -> p h k n", p=P, h=2)
                dst = full.rearrange("p k m -> p (k m)").rearrange("p (k m) -> p k m", k=4)
                return [(dst, w[:, u % 2, :, bass.ds(512 * i + 256 * (u // 2), 256)])]
            if name == "qkv":
                w = I["w_qkv"][0].rearrange("(k p) n -> p k n", p=P)
                if isinstance(i, int) and i == 2:
                    return [(full, w[:, :, D + P * u:D + P * u + P])]
                return [(RAW[:, u, :, HD * h:HD * h + HD], w[:, :, bass.ds(512 * i + 256 * h + HD * u, HD)])
                        for h in range(2)]
            if name == "wo":
                w = I["w_o"][0].rearrange("(b h j d) n -> b h d j n", b=2, h=2, j=4)
                return [(RAW[HD * h:HD * h + HD, u, 4 * b:4 * b + 4, :], w[b, h][:, :, bass.ds(512 * i + P * u, P)])
                        for b in range(2) for h in range(2)]
            if name.startswith("up"):
                layer, ph = int(name[2]), int(name[3])
                w = I["ffn_w1" if u % 2 == 0 else "ffn_w3"][layer].rearrange("(k p) n -> p k n", p=P)
                return [(full, w[:, :, bass.ds(PHASES[ph][0] * P + 256 * i + P * (u // 2), P)])]
            if name.startswith("down"):
                layer, ph = int(name[4]), int(name[5])
                f0, n = PHASES[ph]
                w = I["ffn_w2"][layer].rearrange("(k p) n -> p k n", p=P)
                return [(RAW[:, u, 0:n, :], w[:, f0:f0 + n, bass.ds(512 * i + P * u, P)])]
            if name == "glu":
                w = I["ssm_w_glu"][0].rearrange("(k p) (v c n) -> p k v c n", p=P, v=2, n=P)
                src = w[:, :, 1 - u % 2, bass.ds(2 * i + u // 2, 1), :]
                return [(full, src.rearrange("p k a n -> p k (a n)"))]
            w = I["ssm_w_in" if name == "win" else "ssm_w_out"][0].rearrange("(k p) n -> p k n", p=P)
            return [(full, w[:, :, bass.ds(512 * i + P * u, P)])]

        def load_panels(sp, name):
            base, trips = BASE[name], COUNT[name] // SLOTS

            def body(i, first=False):
                for u in range(SLOTS):
                    if not first:
                        sp.wait_ge(hi_ready, base + SLOTS * i + u - SLOTS + 1)
                        sp.wait_ge(lo_ready, base + SLOTS * i + u - SLOTS + 1)
                    parts = panel_parts(name, i, u)
                    for dst, src in parts:
                        sp.dma_start(dst, src).then_inc(raw_in[u], 64 // len(parts))

            if name == "qkv":
                with loop(sp, 2) as i:
                    body(i)
                body(2)
            elif name == "glu":
                for i in range(trips):
                    body(i)
            elif base == 0:
                body(0, first=True)
                with sp.Fori(1, trips) as i:
                    body(i)
            else:
                with loop(sp, trips) as i:
                    body(i)

        def split_hi(n, u, first=False):
            nc.scalar.wait_ge(raw_in[u], (n - u) * 16 + 64)
            if not first:
                nc.scalar.wait_ge(pe_done, n - SLOTS + 1)
            nc.scalar.activation(WH[:, u], RAW[:, u], ACT.Copy).then_inc(hi_ready, 1)

        def split_lo(n, u):
            nc.vector.wait_ge(hi_ready, n + 1)
            nc.vector.tensor_tensor(WL[:, u], RAW[:, u], WH[:, u].bitcast(F32), ALU.subtract).then_inc(lo_ready, 1)

        def stage_loop(eng, name, body):
            trips = COUNT[name] // SLOTS
            if BASE[name] + COUNT[name] == PANELS:
                with loop(eng, trips - 1) as i:
                    body(i, False)
                body(trips - 1, True)
            else:
                with loop(eng, trips) as i:
                    body(i, False)

        def pe_stage(pe, name, moving_h, moving_l, kt=KT):
            base = BASE[name]

            def body(i, last):
                for u in range(SLOTS):
                    n = base + SLOTS * i + u
                    pe.wait_ge(psum_free, n - SLOTS + 1)
                    pe.wait_ge(hi_ready, n + 1)
                    pe.wait_ge(lo_ready, n + 1)
                    for k in range(kt):
                        for w, m, first, end in ((WH, moving_h, k == 0, False), (WH, moving_l, False, False),
                                                 (WL, moving_h, False, k == kt - 1)):
                            for h in range(2):
                                ins = nc.tensor.matmul(PS[:, 2 * u + h, 0:HALF], w[:, u, k, :],
                                                       m[:, k, HALF * h:HALF * h + HALF], start=first, stop=end)
                    ins.then_inc(pe_done, 1)

            stage_loop(pe, name, body)

        def pe_ada(pe, layer):
            name = f"ada{layer}"
            base = BASE[name]

            def body(i, first=False):
                for c in range(2):
                    for h in range(2):
                        u = 2 * c + h
                        n = base + SLOTS * i + u
                        if not first and h == 0:
                            pe.wait_ge(psum_free, n - SLOTS + 2)
                        pe.wait_ge(hi_ready, n + 1)
                        pe.wait_ge(lo_ready, n + 1)
                        for k in range(4):
                            wide = [W[:, u].rearrange("p k m -> p (k m)")[:, 256 * k:256 * k + 256] for W in (WH, WL)]
                            nc.tensor.matmul(PS[0:4, 4 * c, 0:256], CS[:, 4 * h + k, :], wide[0],
                                             start=(h == 0 and k == 0), stop=False)
                            ins = nc.tensor.matmul(PS[0:4, 4 * c, 0:256], CS2[:, 4 * h + k, :], wide[1],
                                                   start=False, stop=(h == 1 and k == 3))
                        ins.then_inc(pe_done, 1)
                    pe.wait_ge(rows_ready, (base - BASE["ada0"] if layer == 0 else 48) // 2 + 2 * i + c + 1)
                    for q in range(2):
                        ins = nc.tensor.matmul(PS[:, 4 * c + 2, 2 * q:2 * q + 2], ROWS[0:4, c, P * q:P * q + P],
                                               SEL[0:4, :], start=True, stop=True)
                    ins.then_inc(mods_ps, 1)

            if base == 0:
                body(0, first=True)
                with pe.Fori(1, COUNT[name] // SLOTS) as i:
                    body(i)
            else:
                with pe.Fori(0, COUNT[name] // SLOTS) as i:
                    body(i)

        def pe_norm(pe, q):
            pe.wait_ge(ln_sum, q + 1)
            for h in range(2):
                ins = nc.tensor.matmul(PS[:, h, 0:HALF], MEANW[:, :], ACC[:, HALF * h:HALF * h + HALF],
                                       start=True, stop=True)
            ins.then_inc(ln_mean, 1)
            for k in range(KT):
                pe.wait_ge(ln_sq, KT * q + k + 1)
                for h in range(2):
                    ins = nc.tensor.matmul(PS[:, 2 + h, 0:HALF], MEANW[:, :], SQ[:, k % 2, HALF * h:HALF * h + HALF],
                                           start=(k == 0), stop=(k == KT - 1))
                ins.then_inc(ln_sqsum, 1)

        def act_gated(name, func, pairs_before):
            base = BASE[name]

            def body(i, last):
                for c in range(2):
                    n = base + SLOTS * i + 2 * c
                    nc.scalar.wait_ge(pe_done, n + 1)
                    nc.scalar.activation(by_half(GT[:, c, :]), halves(4 * c), func).then_inc(silu_done, 1)
                    if not last:
                        split_hi(n + SLOTS, 2 * c)
                        split_hi(n + SLOTS + 1, 2 * c + 1)
                    nc.scalar.wait_ge(psum_free, n + 2)
                    nc.scalar.activation(HH[:, bass.ds(2 * i + c, 1), :].rearrange("p a t -> p (a t)"),
                                         HT[:, c, :], ACT.Copy).then_inc(hid_hi, 1)

            stage_loop(nc.scalar, name, body)

        def dve_gated(name, pairs_before):
            base = BASE[name]

            def body(i, last):
                for c in range(2):
                    n = base + SLOTS * i + 2 * c
                    pair = pairs_before + 2 * i + c
                    nc.vector.wait_ge(silu_done, pair + 1)
                    nc.vector.wait_ge(pe_done, n + 2)
                    if pairs_before:
                        nc.vector.wait_ge(hid_lo, pair - 1)
                    nc.vector.tensor_tensor(by_half(HT[:, c, :]), halves(4 * c + 2), by_half(GT[:, c, :]),
                                            ALU.mult).then_inc(psum_free, 2)
                    if not last:
                        split_lo(n + SLOTS, 2 * c)
                        split_lo(n + SLOTS + 1, 2 * c + 1)
                    nc.vector.wait_ge(hid_hi, pair + 1)
                    one = bass.ds(2 * i + c, 1)
                    nc.vector.tensor_tensor(HL[:, one, :].rearrange("p a t -> p (a t)"), HT[:, c, :],
                                            HH[:, one, :].rearrange("p a t -> p (a t)").bitcast(F32),
                                            ALU.subtract).then_inc(hid_lo, 1)

            stage_loop(nc.vector, name, body)

        def act_split_only(name):
            base = BASE[name]

            def body(i, last):
                for u in range(SLOTS):
                    if not last:
                        split_hi(base + SLOTS * i + u + SLOTS, u)

            stage_loop(nc.scalar, name, body)

        def stream_parts(permuted):
            if not permuted:
                return [(0, 0, slice(0, CTX), slice(0, CTX)), (1, 0, slice(CTX, HALF), slice(CTX, HALF)),
                        (1, 1, slice(0, HALF), slice(HALF, TOK))]
            return [(s, h, cs, h) for h in range(2) for s, cs in ((0, slice(0, CCH)), (1, slice(CCH, NCHUNK)))]

        def dve_residual(name, layer, gate):
            base = BASE[name]

            def body(i, last):
                for u in range(SLOTS):
                    n = base + SLOTS * i + u
                    nc.vector.wait_ge(pe_done, n + 1)
                    tile = X[:, bass.ds(SLOTS * i + u, 1), :].rearrange("p a t -> p (a t)")
                    col = MODS[:, layer, bass.ds(gate * KT + SLOTS * i + u, 1), :].rearrange("p a s -> p (a s)")
                    for s, b, cols, where in stream_parts(layer == 1):
                        if layer == 0:
                            src, dst = PS[:, 2 * u + b, cols], tile[:, where]
                        else:
                            src = PS[:, 2 * u + b, 0:HALF].rearrange("p (t c) -> p t c", c=NCHUNK)[:, :, cols]
                            dst = tile[:, HALF * b:HALF * b + HALF].rearrange("p (t c) -> p t c", c=NCHUNK)[:, :, cols]
                        ins = nc.vector.scalar_tensor_tensor(out=dst, in0=src, scalar=col[:, s:s + 1], in1=dst,
                                                             op0=ALU.mult, op1=ALU.add)
                    ins.then_inc(psum_free, 1)
                    if not last:
                        split_lo(n + SLOTS, u)

            stage_loop(nc.vector, name, body)

        def dve_store(name, dest):
            base = BASE[name]

            def body(i, last):
                for u in range(SLOTS):
                    n = base + SLOTS * i + u
                    nc.vector.wait_ge(pe_done, n + 1)
                    nc.vector.tensor_copy(by_half(dest[:, bass.ds(SLOTS * i + u, 1), :].rearrange("p a t -> p (a t)")),
                                          halves(2 * u)).then_inc(psum_free, 1)
                    if not last:
                        split_lo(n + SLOTS, u)

            stage_loop(nc.vector, name, body)

        def act_ada(name):
            act_split_only(name)

        vchain = Chain(nc.vector, dve_chain)
        v_link = vchain.link

        def dve_ada(layer):
            base = BASE[f"ada{layer}"]
            chunks = 24 * layer

            def body(i):
                for c in range(2):
                    n = base + SLOTS * i + 2 * c
                    nc.vector.wait_ge(pe_done, n + 2)
                    nc.vector.tensor_copy(ROWS[0:4, c, :], PS[0:4, 4 * c, 0:256]).then_inc(rows_ready, 1)
                    split_lo(n + SLOTS, 2 * c)
                    split_lo(n + SLOTS + 1, 2 * c + 1)
                    nc.vector.wait_ge(mods_ps, chunks + 2 * i + c + 1)
                    nc.vector.tensor_tensor(
                        MODS[:, layer, bass.ds(4 * i + 2 * c, 2), :],
                        PS[:, 4 * c + 2, 0:4].rearrange("p (q s) -> p q s", s=2),
                        PV1[:, bass.ds(MODQ * layer + 4 * i + 2 * c, 2)].unsqueeze(2).to_broadcast([P, 2, 2]),
                        ALU.add).then_inc(psum_free, 2)

            with nc.vector.Fori(0, COUNT[f"ada{layer}"] // SLOTS) as i:
                body(i)
            nc.vector.wait_ge(psum_free, base + COUNT[f"ada{layer}"])
            for q in (1, 4):
                cols = MODS[:, layer, q * KT:(q + 1) * KT, :]
                v_link(nc.vector.tensor_scalar(cols, cols, 1.0, None, ALU.add))
            for q in (2, 5):
                cols = MODS[:, layer, q * KT:(q + 1) * KT, :]
                v_link(nc.vector.tensor_scalar(cols, cols, 1.0 / ALPHA, None, ALU.mult))

        def perm_view(tile):
            return tile.rearrange("p (t c) -> p t c", c=NCHUNK)

        norm_after = [BASE["wo"] + 8, BASE["down02"] + 8, BASE.get("wout", 0) + 8, BASE.get("down12", 0) + 8]

        def dve_norm(q):
            v = nc.vector
            v.wait_ge(psum_free, norm_after[q])
            v.tensor_reduce(ACC[:, :], X[:, :, :].rearrange("p k t -> p t k"), AXIS_X, ALU.add).then_inc(ln_sum, 1)
            v.wait_ge(ln_mean, q + 1)
            for k in range(KT):
                v.tensor_tensor(by_half(X[:, k, :]), by_half(X[:, k, :]), halves(0), ALU.subtract).then_inc(ln_cent, 1)
            v.wait_ge(ln_std, q + 1)
            v_link(v.reciprocal(RSTD[:, :], STD[:, :]))
            v_link(v.tensor_tensor(RT[:, :], RSTD[:, :], RSTD[:, :], ALU.mult))
            v_link(v.scalar_tensor_tensor(out=by_half(RT[:, :]), in0=halves(2), scalar=LN_EPS / ALPHA ** 2,
                                          in1=by_half(RT[:, :]), op0=ALU.add, op1=ALU.mult))
            v_link(v.tensor_scalar(RT[:, :], RT[:, :], -0.5, 1.5, ALU.mult, ALU.add))
            v_link(v.tensor_tensor(RSTD[:, :], RSTD[:, :], RT[:, :], ALU.mult))

        def dve_norm_scale(q, k):
            v = nc.vector
            if k >= 2:
                v.wait_ge(ln_x, KT * q + k - 1)
            v.wait_ge(ln_cent, KT * q + k + 1)
            v.scalar_tensor_tensor(out=YT[:, k % 2, :], in0=X[:, k, :], scalar=PV1[:, 2 * MODQ + KT * q + k:2 * MODQ + KT * q + k + 1],
                                   in1=RSTD[:, :], op0=ALU.mult, op1=ALU.mult).then_inc(ln_y, 1)

        def act_norm(q):
            a = nc.scalar
            for k in range(KT):
                a.wait_ge(ln_cent, KT * q + k + 1)
                if k >= 2:
                    a.wait_ge(ln_sqsum, KT * q + k - 1)
                a.activation(SQ[:, k % 2, :], X[:, k, :], ACT.Square).then_inc(ln_sq, 1)
            a.wait_ge(ln_sqsum, KT * q + KT)
            a.activation(by_half(STD[:, :]), halves(2), ACT.Sqrt, bias=EPS[:, :]).then_inc(ln_std, 1)

        def act_norm_shift(q, k):
            a = nc.scalar
            a.wait_ge(ln_y, KT * q + k + 1)
            src, dst = YT[:, k % 2, :], X[:, k, :]
            if q == 1 and LAYERS == 2:
                src, dst = src.rearrange("p (c t) -> p t c", t=CHUNK), perm_view(dst)
            if q == 3:
                src, dst = perm_view(src), dst.rearrange("p (c t) -> p t c", t=CHUNK)
            a.activation(dst, src, ACT.Identity, bias=PV2[:, KT * q + k:KT * q + k + 1]).then_inc(ln_x, 1)

        def dve_modulate(r, layer, shift, before):
            v = nc.vector

            def low(k):
                v.wait_ge(xh_ready, KT * r + k + 1)
                v.tensor_tensor(XL[:, k, :], XM[:, k % 2, :], XH[:, k, :].bitcast(F32), ALU.subtract).then_inc(xl_ready, 1)

            for k in range(KT):
                before(k)
                if k >= 2:
                    v.wait_ge(xl_ready, KT * r + k - 1)
                sc = MODS[:, layer, (shift + 1) * KT + k, :]
                sh = MODS[:, layer, shift * KT + k, :]
                for s in range(2):
                    if r < 2:
                        cols = slice(0, CTX) if s == 0 else slice(CTX, TOK)
                        src, dst = X[:, k, cols], XM[:, k % 2, cols]
                    else:
                        cols = slice(0, CCH) if s == 0 else slice(CCH, NCHUNK)
                        src = perm_view(X[:, k, :])[:, :, cols]
                        dst = perm_view(XM[:, k % 2, :])[:, :, cols]
                    ins = v.tensor_scalar(dst, src, sc[:, s:s + 1], sh[:, s:s + 1], ALU.mult, ALU.add)
                ins.then_inc(xm_ready, 1)
                if k:
                    low(k - 1)
            low(KT - 1)

        def act_high(r, k):
            a = nc.scalar
            a.wait_ge(xm_ready, KT * r + k + 1)
            a.activation(XH[:, k, :], XM[:, k % 2, :], ACT.Copy).then_inc(xh_ready, 1)

        def dve_norm_modulate(q, r, layer, shift):
            dve_norm(q)

            def before(k):
                if k == 0:
                    dve_norm_scale(q, 0)
                if k < KT - 1:
                    dve_norm_scale(q, k + 1)
                nc.vector.wait_ge(ln_x, KT * q + k + 1)

            dve_modulate(r, layer, shift, before)

        def act_norm_modulate(q, r):
            act_norm(q)
            act_norm_shift(q, 0)
            for k in range(KT):
                if k < KT - 1:
                    act_norm_shift(q, k + 1)
                act_high(r, k)

        qkv_end = BASE["wo"]

        def turn_number(block, B):
            return B if block is None else 2 + 2 * block + B

        def key_tiles(block):
            return 1 if block is None else 4

        def pe_attention_start(pe):
            pe.wait_ge(psum_free, qkv_end)
            pe.wait_ge(attn_in, 16 * ATTN_DMAS)
            t = lambda bank, col, src: nc.tensor.transpose(PS[:, bank, P * col:P * col + P], src, IDENT[:, :])
            for bank in range(2):
                for b in range(2):
                    for d in range(2):
                        c0 = CTX + P * (2 * bank + b)
                        ins = t(bank, 2 * b + d, QKVT[:, 10 + d, c0:c0 + P])
                ins.then_inc(att_t, 1)
            for d in range(2):
                t(2, d, QKVT[:, 10 + d, 0:CTX])
                ins = t(2, 2 + d, QKVT[:, 8 + d, 0:CTX])
            ins.then_inc(att_t, 1)
            for d in range(2):
                ins = t(3, d, CK[:, P * d:P * d + P])
            ins.then_inc(att_t, 1)

        def act_attention_start():
            a = nc.scalar
            for bank in range(2):
                a.wait_ge(att_t, bank + 1)
                a.activation(VN[:, 2 + 2 * bank:4 + 2 * bank, :].rearrange("p b d -> p (b d)"), PS[:, bank, :],
                             ACT.Copy).then_inc(att_kv, 1)
            a.wait_ge(att_t, 3)
            a.activation(VN[:, 0, :], PS[:, 2, 0:2 * P], ACT.Copy).then_inc(att_kv, 1)
            a.activation(KN[:, :], PS[:, 2, 2 * P:4 * P], ACT.Copy).then_inc(att_kv, 1)
            a.wait_ge(att_t, 4)
            a.activation(KCT[:, :, :].rearrange("p b d -> p (b d)"), PS[:, 3, 0:2 * P], ACT.Copy).then_inc(att_kv, 1)

        SWAP_HALVES = [(p + 16) % 32 for p in range(32)]

        def dve_rotate(out, src, cos, sin, swap):
            v = nc.vector
            v_link(v.stream_shuffle(swap, src, SWAP_HALVES))
            v_link(v.tensor_tensor(swap, swap, sin, ALU.mult))
            v_link(v.tensor_tensor(out, src, cos, ALU.mult))
            return v.tensor_tensor(out, out, swap, ALU.add)

        def dve_attention_start():
            v = nc.vector
            v.wait_ge(psum_free, qkv_end)
            v.wait_ge(attn_in, 16 * ATTN_DMAS)
            v.wait_ge(sink_in, 16)
            v_link(v.memset(VN[:, 1, :], 0.0))
            v_link(v.memset(VN[:, 6, :], 0.0))
            for B in range(2):
                v_link(v.memset(KR[:, B, 0:P], 0.0))
                v_link(v.memset(KR[:, B, P + LAT:], 0.0))
                v_link(dve_rotate(KR[:, B, P:P + LAT], QKVT[:, 8 + B, CTX:TOK], ROPE[:, 0, :], ROPE[:, 1, :], SWAP[:, :]))

        def queries(block, B):
            first = 0 if block is None else block * P + CTX
            return QKVT[:, 4 * B:4 * B + 4, bass.ds(first, P)]

        def dve_turn(block, B):
            v = nc.vector
            g = turn_number(block, B)
            width = P * key_tiles(block)
            if block is not None:
                tok = bass.ds(block * P, P)
                cos = ROPE[:, 0, tok].unsqueeze(1).to_broadcast([P, 4, P])
                sin = ROPE[:, 1, tok].unsqueeze(1).to_broadcast([P, 4, P])
                swap = SWAP[:, :].rearrange("p (a t) -> p a t", a=4)
                v.wait_ge(att_s, 8 * g)
                v_link(v.tensor_copy(KW[:, :], KR[:, B, bass.ds(block * P, 3 * P)]))
                dve_rotate(QB[:, 1, :, :], queries(block, B), cos, sin, swap).then_inc(att_qrot, 1)
            for n in range(8):
                v.wait_ge(att_s, 8 * g + n + 1)
                if g_positive(block, B):
                    v.wait_ge(att_tr, 8 * g)
                mask = MASK[:, 0, 0:P] if block is None else MASK[:, block, :]
                v.tensor_tensor_reduce(out=S[:, n, 0:width], in0=PS[:, n % 4, 0:width], in1=mask, scale=1.0,
                                       scalar=-3.0e38, op0=ALU.add, op1=ALU.max,
                                       accum_out=STAT[:, 0, n:n + 1]).then_inc(att_max, 1)
            v.wait_ge(att_max, 8 * g + 8)
            pair = lambda r: STAT[:, r, :].rearrange("p (j h) -> p j h", h=2)
            sink = SINK[:, 8 * B:8 * B + 8].rearrange("p (h j) -> p j h", h=2)
            v_link(v.scalar_tensor_tensor(out=pair(1), in0=pair(0), scalar=SCALE, in1=sink, op0=ALU.mult, op1=ALU.max))
            v_link(v.tensor_scalar(STAT[:, 2, :], STAT[:, 1, :], -1.0, None, ALU.mult))
            v.tensor_tensor(pair(3), sink, pair(1), ALU.subtract).then_inc(att_stat, 1)
            v.wait_ge(att_exp, 9 * g + 9)
            v_link(v.tensor_tensor(STAT[:, 6, :], STAT[:, 4, :], STAT[:, 5, :], ALU.add))
            v_link(v.reciprocal(STAT[:, 7, :], STAT[:, 6, :]))
            for h in range(2):
                for j in range(4):
                    n = 2 * j + h
                    v.tensor_scalar(S[:, n, 0:width], S[:, n, 0:width], STAT[:, 7, n:n + 1], None,
                                    ALU.mult).then_inc(att_p, 1)
            for h in range(2):
                rows = slice(HD * h, HD * h + HD)
                v.wait_ge(att_oh, 2 * g + h + 1)
                v.tensor_tensor(attended(XL, block, B, rows), pv_out(h), attended(XH, block, B, rows).bitcast(F32),
                                ALU.subtract).then_inc(att_ol, 1)

        def attended(T, block, B, rows):
            first = 0 if block is None else block * P + CTX
            return T[rows, 4 * B:4 * B + 4, bass.ds(first, P)]

        def pv_out(h):
            return PS[HD * h:HD * h + HD, 6 + h, :].rearrange("p (j q) -> p j q", j=4)

        def g_positive(block, B):
            return block is not None or B > 0

        def act_turn(block, B):
            a = nc.scalar
            g = turn_number(block, B)
            width = P * key_tiles(block)
            if g_positive(block, B):
                a.wait_ge(att_s, 8 * g)
            a.activation(QB[:, 0, :, :], queries(block, B), ACT.Copy).then_inc(att_qplain, 1)
            if block is not None and B == 0:
                a.wait_ge(att_pv, 2 * g)
                a.activation(VW[:, :, :].rearrange("p b d -> p (b d)"),
                             VN[:, bass.ds(block + 1, 3), :].rearrange("p b d -> p (b d)"), ACT.Copy).then_inc(att_vw, 1)
            a.wait_ge(att_stat, g + 1)
            a.activation(STAT[:, 5, :], STAT[:, 3, :], ACT.Exp).then_inc(att_exp, 1)
            for n in range(8):
                a.activation(S[:, n, 0:width], S[:, n, 0:width], ACT.Exp, bias=STAT[:, 2, n:n + 1], scale=SCALE,
                             accum_out=STAT[:, 4, n:n + 1]).then_inc(att_exp, 1)
            for h in range(2):
                for j in range(4):
                    idx = 4 * h + j
                    a.wait_ge(att_tr, 8 * g + idx + 1)
                    if h == 0:
                        if g_positive(block, B):
                            a.wait_ge(att_pv, 2 * g)
                    else:
                        a.wait_ge(att_pv, 2 * g + 1)
                    kt = key_tiles(block)
                    a.activation(PT[:, 0:kt, j, :], PS[:, 4 + idx % 2, 0:width].rearrange("p (k q) -> p k q", k=kt),
                                 ACT.Copy).then_inc(att_pt, 1)
                    if h == 1 and j == 0:
                        act_attended(block, B, 0)
            act_attended(block, B, 1)

        def act_attended(block, B, h):
            rows = slice(HD * h, HD * h + HD)
            nc.scalar.wait_ge(att_pv, 2 * turn_number(block, B) + h + 1)
            nc.scalar.activation(attended(XH, block, B, rows), pv_out(h), ACT.Copy).then_inc(att_oh, 1)

        def pe_turn(pe, block, B):
            g = turn_number(block, B)
            kt = key_tiles(block)
            if block is None:
                pe.wait_ge(att_kv, 5)
            pe.wait_ge(att_qplain, g + 1)
            if block is not None:
                pe.wait_ge(att_qrot, 2 * block + B + 1)
            for j in range(4):
                for h in range(2):
                    n = 2 * j + h
                    rows = slice(HD * h, HD * h + HD)
                    if g_positive(block, B) or n >= 4:
                        pe.wait_ge(att_max, 8 * g + n - 3)
                    keys = QKVT[rows, 8 + B, 0:CTX] if block is None else KCT[rows, B, :]
                    ins = nc.tensor.matmul(PS[:, n % 4, 0:P], QB[rows, 0, j, :], keys, start=True, stop=True)
                    if block is not None:
                        ins = nc.tensor.matmul(PS[:, n % 4, P:4 * P], QB[rows, 1, j, :],
                                               KW[rows, :], start=True, stop=True)
                    ins.then_inc(att_s, 1)
            if block is not None and B == 0:
                pe.wait_ge(att_vw, block + 1)
            for h in range(2):
                for j in range(4):
                    idx = 4 * h + j
                    pe.wait_ge(att_p, 8 * g + idx + 1)
                    if g_positive(block, B) or idx >= 2:
                        pe.wait_ge(att_pt, 8 * g + idx - 1)
                    for k in range(kt):
                        ins = nc.tensor.transpose(PS[:, 4 + idx % 2, P * k:P * k + P],
                                                  S[:, 2 * j + h, P * k:P * k + P], IDENT[:, :])
                    ins.then_inc(att_tr, 1)
                pe.wait_ge(att_pt, 8 * g + 4 * h + 4)
                if g_positive(block, B):
                    pe.wait_ge(att_ol, 2 * g - 1 + h)
                for k in range(kt):
                    if block is None:
                        val = VN[:, 0, :]
                    else:
                        val = CV[:, :] if k == 0 else VW[:, k - 1, :]
                    c0 = P * B + HD * h
                    ins = nc.tensor.matmul(PS[HD * h:HD * h + HD, 6 + h, :], val[:, c0:c0 + HD],
                                           PT[:, k, :, :].rearrange("p j q -> p (j q)"), start=(k == 0), stop=(k == kt - 1))
                ins.then_inc(att_pv, 1)


        NB = GROUPS // 8

        def complex_mult(eng, chn, out_re, out_im, ar, ai, br, bi, t1, t2, negate_im=False):
            chn.link(eng.tensor_tensor(t1, ar, br, ALU.mult))
            chn.link(eng.tensor_tensor(t2, ai, bi, ALU.mult))
            chn.link(eng.tensor_tensor(out_re, t1, t2, ALU.subtract))
            chn.link(eng.tensor_tensor(t1, ar, bi, ALU.mult))
            chn.link(eng.tensor_tensor(t2, ai, br, ALU.mult))
            if negate_im:
                chn.link(eng.tensor_scalar(t1, t1, -1.0, None, ALU.mult))
            return eng.tensor_tensor(out_im, t1, t2, ALU.subtract if negate_im else ALU.add)

        def sp_ssm_start(sp):
            sp.wait_ge(psum_free, BASE["ada1"])
            by_group = lambda a: a.rearrange("d g p -> g d p")
            sp.dma_start(LAM[:, 0], by_group(I["ssm_lam_re"][0])).then_inc(ssm_in, 16)
            sp.dma_start(LAM[:, 1], by_group(I["ssm_lam_im"][0])).then_inc(ssm_in, 16)
            sp.dma_start(GM[:, 4], by_group(I["state_ssm_re"][0, 0])).then_inc(ssm_in, 16)
            sp.dma_start(GM[:, 5], by_group(I["state_ssm_im"][0, 0])).then_inc(ssm_in, 16)
            for d in range(2):
                sp.dma_start(LDT[:, d:d + 1], I["ssm_log_dt"][0, d].rearrange("(g a) -> g a", a=1)).then_inc(ssm_in, 16)
            for r, nm in enumerate(("re", "im")):
                for d in range(2):
                    rows = slice(STATE * d, STATE * d + STATE)
                    sp.dma_start(BN[rows, r], I["ssm_b_" + nm][0, d].rearrange("g p m -> p g m")).then_inc(ssm_in, 16)
                    sp.dma_start(CN[:, r, :, d, :], I["ssm_c_" + nm][0, d].rearrange("g n p -> (g n) p")
                                 .rearrange("(T q) p -> q T p", q=P)).then_inc(ssm_in, 16)
            sp.dma_start(DB[:, :], I["ssm_d"][0:1, :].to_broadcast([GCH, D])).then_inc(ssm_in, 16)

        TWO_PI = (6.28125, 0.0019350051879882812, 3.0199161e-07)
        ROUND = 12582912.0

        def act_ssm_start():
            a = nc.scalar
            a.wait_ge(ssm_in, 16 * SSM_DMAS)
            a.activation(LDT[:, :], LDT[:, :], ACT.Exp).then_inc(ssm_a, 1)
            a.wait_ge(ssm_v, 1)
            a.activation(MAG[:, :], ZR[:, :], ACT.Exp).then_inc(ssm_a, 1)
            a.wait_ge(ssm_v, 2)
            a.activation(SINH[:, :], ZI[:, :], ACT.Sin, scale=0.5).then_inc(ssm_a, 1)
            a.activation(SIN[:, :], ZI[:, :], ACT.Sin).then_inc(ssm_a, 1)
            a.wait_ge(ssm_t, 1)
            a.activation(AC[:, :, :], PS[:, 0, 0:6 * GROUPS].rearrange("p (a g) -> p a g", g=GROUPS), ACT.Copy).then_inc(ssm_a, 1)
            for n in range(4):
                a.wait_ge(ssm_t, 2 + n)
                a.activation(CT[:, n // 2, 4 * (n % 2):4 * (n % 2) + 4, :].rearrange("p a n -> p (a n)"),
                             PS[:, 4 + n, :], ACT.Copy).then_inc(ssm_a, 1)
            a.wait_ge(ssm_v, 4)
            a.activation(POWB[0:64], POW[0:64, :, 0:8, :][:, :, ::-1, :], ACT.Copy).then_inc(ssm_a, 1)
            a.activation(POWB[64:P], POW[64:P, :, 0:8, :], ACT.Copy).then_inc(ssm_a, 1)

        def dve_ssm_start():
            v = nc.vector
            chn = vchain
            tt, ts = v.tensor_tensor, v.tensor_scalar
            v.wait_ge(ssm_in, 16 * SSM_DMAS)
            v.wait_ge(ssm_a, 1)
            dp = lambda t: t[:, :].rearrange("g (d p) -> g d p", d=2)
            dt = LDT[:, :].unsqueeze(2).to_broadcast([GROUPS, 2, STATE])
            tt(dp(ZR), LAM[:, 0], dt, ALU.mult).then_inc(ssm_v, 1)
            chn.link(tt(dp(ZI), LAM[:, 1], dt, ALU.mult))
            chn.link(ts(T1[:, :], ZI[:, :], 1.0 / (2 * np.pi), None, ALU.mult))
            chn.link(ts(T1[:, :], T1[:, :], ROUND, None, ALU.add))
            chn.link(ts(T1[:, :], T1[:, :], -ROUND, None, ALU.add))
            for part in TWO_PI:
                chn.link(v.scalar_tensor_tensor(out=ZI[:, :], in0=T1[:, :], scalar=-part, in1=ZI[:, :], op0=ALU.mult, op1=ALU.add))
            ts(ZI[:, :], ZI[:, :], 3.1415925, -3.1415925, ALU.min, ALU.max).then_inc(ssm_v, 1)
            v.wait_ge(ssm_a, 4)
            chn.link(tt(T1[:, :], SINH[:, :], SINH[:, :], ALU.mult))
            chn.link(ts(T1[:, :], T1[:, :], -2.0, 1.0, ALU.mult, ALU.add))
            gm = lambda r: GM[:, r].rearrange("g d p -> g (d p)")
            lam = lambda r: LAM[:, r].rearrange("g d p -> g (d p)")
            chn.link(tt(gm(0), MAG[:, :], T1[:, :], ALU.mult))
            chn.link(tt(gm(1), MAG[:, :], SIN[:, :], ALU.mult))
            chn.link(ts(T1[:, :], gm(0), -1.0, None, ALU.add))
            chn.link(tt(T2[:, :], lam(0), lam(0), ALU.mult))
            chn.link(tt(T3[:, :], lam(1), lam(1), ALU.mult))
            chn.link(tt(T2[:, :], T2[:, :], T3[:, :], ALU.add))
            chn.link(v.reciprocal(T2[:, :], T2[:, :]))
            chn.link(tt(gm(2), T1[:, :], lam(0), ALU.mult))
            chn.link(tt(T3[:, :], gm(1), lam(1), ALU.mult))
            chn.link(tt(gm(2), gm(2), T3[:, :], ALU.add))
            chn.link(tt(gm(2), gm(2), T2[:, :], ALU.mult))
            chn.link(tt(gm(3), gm(1), lam(0), ALU.mult))
            chn.link(tt(T3[:, :], T1[:, :], lam(1), ALU.mult))
            chn.link(tt(gm(3), gm(3), T3[:, :], ALU.subtract))
            tt(gm(3), gm(3), T2[:, :], ALU.mult).then_inc(ssm_v, 1)
            v.wait_ge(ssm_a, 5)
            chn.link(v.memset(POW[:, 0, 0, :], 1.0))
            chn.link(v.memset(POW[:, 1, 0, :], 0.0))
            chn.link(v.tensor_copy(POW[:, :, 1, :], AC[:, 0:2, :]))
            for have in (1, 2, 4):
                pw = lambda r: POW[:, r, 1:have + 1, :]
                by = lambda r: POW[:, r, have:have + 1, :].to_broadcast([P, have, GROUPS])
                tmp = [W1[:, 0:have * GROUPS].rearrange("p (k g) -> p k g", g=GROUPS),
                       W2[:, 0:have * GROUPS].rearrange("p (k g) -> p k g", g=GROUPS)]
                out = lambda r: POW[:, r, have + 1:2 * have + 1, :]
                ins = complex_mult(v, chn, out(0), out(1), pw(0), pw(1), by(0), by(1), *tmp)
                if have < 4:
                    chn.link(ins)
                else:
                    ins.then_inc(ssm_v, 1)
            v.wait_ge(ssm_v, 4)
            for r in range(2):
                chn.link(v.tensor_copy(AR[:, r, :], POW[:, 0, 8, :]))
            chn.link(v.tensor_copy(AI[:, 0, :], POW[:, 1, 8, :]))
            chn.link(ts(AI[:, 1, :], POW[:, 1, 8, :], -1.0, None, ALU.mult))
            chn.link(v.tensor_copy(H0[:, :, :], AC[:, 4:6, :]))
            wide = [t[:, 0:1024].rearrange("p (g m) -> p g m", m=GCH) for t in (W1, W2)]
            coef = lambda r: AC[:, 2 + r, :].unsqueeze(2).to_broadcast([P, GROUPS, GCH])
            complex_mult(v, chn, BB[:, 0], BB[:, 1], BN[:, 0], BN[:, 1], coef(0), coef(1), *wide).then_inc(ssm_v, 1)
            v.tensor_tensor(DI[:, :, :], DB[:, :].rearrange("p (g n) -> p g n", n=GCH),
                            IDENT[0:GCH, 0:GCH].unsqueeze(1).to_broadcast([GCH, GROUPS, GCH]), ALU.mult).then_inc(ssm_v, 1)
            v.memset(STRIP[0:64, :, :, 0:7 * GCH], 0.0).then_inc(ssm_v, 1)
            v.memset(STRIP[64:P, :, :, 8 * GCH:15 * GCH], 0.0).then_inc(ssm_v, 1)
            v.wait_ge(ssm_v, 8)
            v.wait_ge(ssm_a, 9)

        def pe_ssm_start(pe):
            pe.wait_ge(ssm_in, 16 * SSM_DMAS)
            pe.wait_ge(ssm_v, 3)
            for r in range(6):
                ins = nc.tensor.transpose(PS[:, 0, GROUPS * r:GROUPS * r + GROUPS], GM[:, r].rearrange("g d p -> g (d p)"),
                                          IDENT[0:GROUPS, 0:GROUPS])
            ins.then_inc(ssm_t, 1)
            for n in range(4):
                for T in range(4):
                    ins = nc.tensor.transpose(PS[:, 4 + n, P * T:P * T + P],
                                              CN[:, n // 2, 4 * (n % 2) + T].rearrange("q d p -> q (d p)"), IDENT[:, :])
                ins.then_inc(ssm_t, 1)

        def k_g_n(ap, k):
            return ap.unsqueeze(1).to_broadcast([P, k, 8, GCH])

        def dve_prep(T, first):
            v = nc.vector
            tmp = [t[:, 0:9 * P].rearrange("p (k g n) -> p k g n", k=9, g=8) for t in (W1, W2)]
            c = lambda r: k_g_n(CT[:, r, bass.ds(T, 1), :].rearrange("p a (g n) -> p (a g) n", n=GCH), 9)
            pw = lambda r: POW[:, r, :, bass.ds(8 * T, 8)].unsqueeze(3).to_broadcast([P, 9, 8, GCH])
            if not first:
                v.wait_ge(cp_ready, 9 * T)
            complex_mult(v, vchain, G[:, 0], G[:, 1], c(0), c(1), pw(0), pw(1), *tmp, negate_im=True).then_inc(g_ready, 1)
            v.wait_ge(kern_ps, T + 1)
            if not first:
                v.wait_ge(ks_out, 16 * T)
            v.tensor_copy(KS[:, :, :], PS[0:GCH, 4:8, :].rearrange("m b (g n) -> m (b g) n", g=2)[:, :, 0:15 * GCH]).then_inc(ks_ready, 1)
            v.wait_ge(ks_ready, 2 * T + 1)
            mid = KS[:, :, 7 * GCH:8 * GCH]
            v.tensor_tensor(mid, mid, DI[:, bass.ds(8 * T, 8), :], ALU.add).then_inc(ks_ready, 1)

        def pool_prep(T, first):
            g = nc.gpsimd
            tmp = [t[:, :, :, :] for t in (Q1, Q2)]
            b = lambda r: BB[:, r, bass.ds(8 * T, 8), :].unsqueeze(1).to_broadcast([P, 8, 8, GCH])
            pw = lambda r: POWB[:, r, :, bass.ds(8 * T, 8)].unsqueeze(3).to_broadcast([P, 8, 8, GCH])
            out = lambda r: BP[:, r, :, :].rearrange("p g (t m) -> p t g m", m=GCH)
            if not first:
                g.wait_ge(bt_ps, 4 * T)
            complex_mult(g, pchain, out(0), out(1), b(0), b(1), pw(0), pw(1), *tmp).then_inc(bp_ready, 1)

        def act_prep(T, first):
            a = nc.scalar
            a.wait_ge(g_ready, T + 1)
            if not first:
                a.wait_ge(cp_out, 16 * T)
                a.wait_ge(kern_ps, T)
            a.activation(BBS[:, :, :, :], BB[:, :, bass.ds(8 * T, 8), :], ACT.Copy).then_inc(cp_ready, 1)
            for r in range(2):
                for d in range(2):
                    rows = slice(64 * d, 64 * d + 64)
                    ks = slice(1, 9)
                    src = G[rows, r, ks] if d == 0 else G[rows, r, ks][:, ::-1]
                    dst = CP[rows, r, :, :].rearrange("p g (t n) -> p t g n", n=GCH)
                    a.activation(dst, src, ACT.Copy).then_inc(cp_ready, 1)
                    src = G[rows, r, 0:8] if d == 0 else G[rows, r, 0:8][:, ::-1]
                    dst = STRIP[rows, r, :, 7 * GCH * (1 - d):7 * GCH * (1 - d) + 8 * GCH].rearrange("p g (t n) -> p t g n", n=GCH)
                    a.activation(dst, src, ACT.Copy).then_inc(cp_ready, 1)
            store_cp(a, T)
            if not first:
                a.wait_ge(bt_out, 16 * T)
            for n in range(4):
                a.wait_ge(bt_ps, 4 * T + n + 1)
                a.activation(BTS[:, 2 * n:2 * n + 2, :, :].rearrange("p g r n -> p (g r n)"), PS[:, n, :], ACT.Copy).then_inc(bt_ready, 1)
            store_bt_ks(a, T)

        def pe_prep(pe, T, first):
            pe.wait_ge(cp_ready, 9 * T + 9)
            if not first:
                pe.wait_ge(ks_ready, 2 * T)
            for g in range(8):
                for r in range(2):
                    ins = nc.tensor.matmul(PS[0:GCH, 4 + g // 2, 256 * (g % 2):256 * (g % 2) + 15 * GCH],
                                           BBS[:, r, g, :], STRIP[:, r, g, :], start=(r == 0), stop=(r == 1))
            ins.then_inc(kern_ps, 1)
            pe.wait_ge(bp_ready, T + 1)
            if not first:
                pe.wait_ge(bt_ready, 4 * T)
            for n in range(4):
                for g in range(2):
                    for r in range(2):
                        ins = nc.tensor.transpose(PS[:, n, P * (2 * g + r):P * (2 * g + r) + P], BP[:, r, 2 * n + g, :], IDENT[:, :])
                ins.then_inc(bt_ps, 1)

        def store_cp(sp, T):
            sp.wait_ge(cp_ready, 9 * T + 9)
            sp.dma_start(C_SCR[bass.ds(T, 1)].rearrange("a p n -> p (a n)"), CP[:, :, :, :].rearrange("p r g n -> p (r g n)")).then_inc(cp_out, 16)

        def store_bt_ks(sp, T):
            sp.wait_ge(bt_ready, 4 * T + 4)
            sp.dma_start(B_SCR[bass.ds(T, 1)].rearrange("a p n -> p (a n)"), BTS[:, :, :, :].rearrange("p g r n -> p (g r n)")).then_inc(bt_out, 16)
            sp.wait_ge(ks_ready, 2 * T + 2)
            sp.dma_start(K_SCR[bass.ds(8 * T, 8)].rearrange("g m n -> m g n"), KS[:, :, :]).then_inc(ks_out, 16)

        def over_batches(eng, body, chn=None, per=0):
            body(0, True)
            with eng.Fori(1, NB) as T:
                if chn is not None:
                    chn.enter(T - 1, per)
                body(T, False)
                if chn is not None:
                    chn.leave(NB - 1)

        FWD, BWD = slice(0, STATE), slice(STATE, P)

        def scan_views(T, r_major=False):
            return [(FWD, slice(0, CCH), slice(1, 1 + CCH)), (FWD, slice(CCH, NCHUNK), slice(CCH + 2, CCH + 2 + LCH)),
                    (BWD, slice(0, CCH), slice(CCH, 0, -1)), (BWD, slice(CCH, NCHUNK), slice(CCH + 1 + LCH, CCH + 1, -1))]

        def entering_views():
            return [(FWD, slice(0, CCH), slice(0, CCH)), (FWD, slice(CCH, NCHUNK), slice(CCH + 1, CCH + 1 + LCH)),
                    (BWD, slice(0, CCH), slice(CCH - 1, None, -1)), (BWD, slice(CCH, NCHUNK), slice(CCH + LCH, CCH, -1))]

        def sp_ssm(sp):
            for m in range(KT):
                sp.wait_ge(psum_free, BASE["win"] + m + 1)
                sp.dma_start(U_SCR[P * m:P * m + P, :], UT[:, m, :]).then_inc(u_out, 16)
            sp.wait_ge(u_out, 16 * KT)
            for t in range(CHUNK):
                sp.dma_start(U8[GCH * t:GCH * t + GCH, :, :], U_SCR.rearrange("(g c) n -> c g n", c=GCH)[:, :, NCHUNK * t:NCHUNK * t + NCHUNK]).then_inc(u_in, 16)
            for T in range(NB):
                if T >= 2:
                    sp.wait_ge(inc_ps, T - 1)
                sp.dma_start(BT[:, T % 2].rearrange("p g r n -> p (g r n)"), B_SCR[T]).then_inc(bt_in[T % 2], 16)
            for T in range(NB):
                sp.wait_ge(inc_ps, NB)
                if T >= 2:
                    sp.wait_ge(y_ps, T - 1)
                sp.dma_start(CPL[:, T % 2].rearrange("p r g n -> p (r g n)"), C_SCR[T]).then_inc(cp_in[T % 2], 16)
                for t in range(CHUNK):
                    src = K_SCR[8 * T:8 * T + 8].rearrange("g m n -> m g n")[:, :, GCH * (7 - t):GCH * (7 - t) + P]
                    sp.dma_start(TOEP[GCH * t:GCH * t + GCH, T % 2, :, :], src).then_inc(cp_in[T % 2], 16)
            sp.wait_ge(fin_ready, 1)
            for r, nm in enumerate(("new_re", "new_im")):
                sp.dma_start(O[nm][0, 0].rearrange("d g p -> g d p"), FIN[:, r, :].rearrange("g (d p) -> g d p", d=2)).then_inc(fin_out, 16)
            sp.wait_ge(y_ready, NB)
            for t in range(CHUNK):
                sp.dma_start(U_SCR.rearrange("(g c) n -> c g n", c=GCH)[:, :, NCHUNK * t:NCHUNK * t + NCHUNK], Y8[GCH * t:GCH * t + GCH, :, :]).then_inc(y_out, 16)
            sp.wait_ge(y_out, 16 * CHUNK)
            for m in range(KT):
                sp.dma_start(YIN[:, m, :], U_SCR[P * m:P * m + P, :]).then_inc(y_in[m], 16)

        def pe_ssm(pe):
            pe.wait_ge(u_in, 16 * CHUNK)
            pe.wait_ge(psum_free, BASE["win"] + KT)
            for T in range(NB):
                pe.wait_ge(bt_in[T % 2], 16 * (T // 2 + 1))
                if T >= 2:
                    pe.wait_ge(inc_a, 2 * T - 2)
                    pe.wait_ge(inc_v, 2 * T - 2)
                for g in range(8):
                    for r in range(2):
                        c0 = 256 * (g % 2) + P * r
                        ins = nc.tensor.matmul(PS[:, 4 * (T % 2) + g // 2, c0:c0 + NCHUNK], BT[:, T % 2, g, r, :],
                                               U8[:, 8 * T + g, :], start=True, stop=True)
                ins.then_inc(inc_ps, 1)
            for T in range(NB):
                pe.wait_ge(cp_in[T % 2], 16 * 9 * (T // 2 + 1))
                pe.wait_ge(ent_a, 2 * T + 2)
                pe.wait_ge(ent_v, 2 * T + 2)
                if T >= 4:
                    pe.wait_ge(y_ready, T - 3)
                for g in range(8):
                    out = PS[:, 2 * (T % 4) + g // 4, P * (g % 4):P * (g % 4) + NCHUNK]
                    nc.tensor.matmul(out, TOEP[:, T % 2, g, :], U8[:, 8 * T + g, :], start=True, stop=False)
                    for r in range(2):
                        ins = nc.tensor.matmul(out, CPL[:, T % 2, r, g, :], ENT[:, r, 8 * T + g, :], start=False, stop=(r == 1))
                ins.then_inc(y_ps, 1)
            pe.wait_ge(y_ready, NB)
            for r in range(2):
                ins = nc.tensor.transpose(PS[0:GROUPS, 0, P * r:P * r + P], FINS[:, r, :], IDENT[:, :])
            ins.then_inc(fin_ps, 1)

        def scan_inputs(engine, T, parts, done):
            engine.wait_ge(inc_ps, T + 1)
            for rows, chunks, slots in parts:
                src = PS[rows, 4 * (T % 2):4 * (T % 2) + 4, :].rearrange("p b (g r c) -> p (b g) r c", g=2, r=2)[:, :, :, chunks]
                dst = ST[rows, slots, :, 8 * T:8 * T + 8].rearrange("p c r g -> p g r c")
                if engine is nc.scalar:
                    ins = engine.activation(dst, src, ACT.Copy)
                else:
                    ins = engine.tensor_copy(dst, src)
                ins.then_inc(done, 1)

        def entering(engine, T, parts, done):
            for rows, chunks, slots in parts:
                src = ST[rows, slots, :, 8 * T:8 * T + 8].rearrange("p c r g -> p r g c")
                dst = ENT[rows, :, 8 * T:8 * T + 8, chunks]
                if engine is nc.scalar:
                    ins = engine.activation(dst, src, ACT.Copy)
                else:
                    ins = engine.tensor_copy(dst, src)
                ins.then_inc(done, 1)

        def act_ssm():
            a = nc.scalar
            for T in range(NB):
                scan_inputs(a, T, scan_views(T)[0:2], inc_a)
            a.wait_ge(scan_done, 1)
            for T in range(NB):
                entering(a, T, entering_views()[0:2], ent_a)
            a.wait_ge(ent_a, 2 * NB)
            a.wait_ge(ent_v, 2 * NB)
            for T in range(NB):
                a.wait_ge(y_ps, T + 1)
                a.activation(Y8[:, 8 * T:8 * T + 8, :], PSF[:, 1024 * (T % 4):1024 * (T % 4) + 1024]
                             .rearrange("p (g c) -> p g c", g=8)[:, :, 0:NCHUNK], ACT.Copy).then_inc(y_ready, 1)
            a.wait_ge(fin_ps, 1)
            a.activation(FIN[:, :, :].rearrange("g r n -> g (r n)"), PS[0:GROUPS, 0, 0:2 * P], ACT.Copy).then_inc(fin_ready, 1)
            for m in range(KT):
                a.wait_ge(y_in[m], 16)
                if m >= 2:
                    a.wait_ge(gelu_lo, m - 1)
                a.activation(GT[:, m % 2, :], YIN[:, m, :], ACT.Gelu_apprx_tanh).then_inc(gelu_done, 1)
                a.wait_ge(gelu_done, m + 1)
                a.activation(XH[:, m, :], GT[:, m % 2, :], ACT.Copy).then_inc(gelu_hi, 1)

        def dve_ssm():
            v = nc.vector
            v.wait_ge(u_out, 16 * KT)
            v_link(v.memset(ST[:, 0, :, :], 0.0))
            v_link(v.tensor_copy(ST[:, CCH + 1, :, :], H0[:, :, :]))
            for T in range(NB):
                scan_inputs(v, T, scan_views(T)[2:4], inc_v)
            v.wait_ge(inc_a, 2 * NB)
            v.wait_ge(inc_v, 2 * NB)

            both = ST[:, 0:2 * (CCH + 1)].rearrange("p (a s) r g -> p a s (r g)", s=CCH + 1)

            def run(trips, first, n, count0):
                with v.Fori(0, trips) as i:
                    for u in range(UN):
                        c = count0 + 4 * UN * i + 4 * u
                        s = first + UN * i + u
                        if n == 2:
                            last = both[:, :, bass.ds(s - 1, 1), :].rearrange("p a s (r g) -> p (a s) r g", r=2)
                            now = both[:, :, bass.ds(s, 1), :].rearrange("p a s (r g) -> p (a s) r g", r=2)
                        else:
                            last, now = ST[:, bass.ds(s - 1, 1)], ST[:, bass.ds(s, 1)]
                        shape = [P, n, 2, GROUPS]
                        ar = AR[:, :, :].unsqueeze(1).to_broadcast(shape)
                        ai = AI[:, :, :].unsqueeze(1).to_broadcast(shape)
                        t1, t2 = SC1[:, 0:n], SC2[:, 0:n]
                        v.tensor_tensor(t1, last, ar, ALU.mult).then_inc(scan_t, 1)
                        v.tensor_tensor(t2[:, :, ::-1, :], last, ai, ALU.mult).then_inc(scan_t, 1)
                        v.wait_ge(scan_t, c + 1)
                        v.tensor_tensor(now, now, t1, ALU.add).then_inc(scan_t, 1)
                        v.wait_ge(scan_t, c + 3)
                        v.tensor_tensor(now, now, t2, ALU.add).then_inc(scan_t, 1)
                        v.wait_ge(scan_t, c + 4)
                return count0 + 4 * UN * trips

            UN = 4
            c = run(CCH // UN, 1, 2, 0)
            run((LCH - CCH) // UN, 2 * CCH + 2, 1, c)
            v.tensor_copy(FINS[:, :, :], ST[:, CCH, :, :]).then_inc(scan_done, 1)
            for T in range(NB):
                entering(v, T, entering_views()[2:4], ent_v)
            for m in range(KT):
                v.wait_ge(gelu_hi, m + 1)
                v.tensor_tensor(XL[:, m, :], GT[:, m % 2, :], XH[:, m, :].bitcast(F32), ALU.subtract).then_inc(gelu_lo, 1)

        def XBANK(k):
            return 4 + 2 * (k % 2)

        def act_out(a):
            for b in range(5):
                a.wait_ge(out_t, 2 * b + 1)
                if b >= 2:
                    a.wait_ge(out_dma[b % 2], 16 * (b // 2))
                a.activation(OUTN[:, b % 2, 0:512], PS[:, 2 * (b % 4), :], ACT.Copy).then_inc(out_a, 1)

        def dve_out(v):
            for b in range(5):
                v.wait_ge(out_t, 2 * b + 2)
                if b >= 2:
                    v.wait_ge(out_dma[b % 2], 16 * (b // 2))
                nc.vector.tensor_copy(OUTN[:, b % 2, 512:1024], PS[:, 2 * (b % 4) + 1, :]).then_inc(out_v, 1)

        def pe_out(pe, q):
            pe.wait_ge(ln_x, KT * q + KT)
            for b in range(5):
                if b >= 4:
                    pe.wait_ge(out_a, b - 3)
                    pe.wait_ge(out_v, b - 3)
                for k in range(KT):
                    ins = nc.tensor.transpose(PS[:, 2 * (b % 4) + k // 4, P * (k % 4):P * (k % 4) + P],
                                              X[:, k, P * b:P * b + P], IDENT[:, :])
                    if k % 4 == 3:
                        ins.then_inc(out_t, 1)

        block = ctx.enter_context(nc.Block())

        @block.sync
        def _(sp):
            rows = [(0, 0, I["b_ada"].rearrange("l (q p) -> (l q) p", p=P)),
                    (0, 96, I["ln_g"].rearrange("l i (k p) -> (l i k) p", p=P)),
                    (1, 0, I["ln_b"].rearrange("l i (k p) -> (l i k) p", p=P)),
                    (1, 32, I["c_ctx"].rearrange("(k p) -> k p", p=P)),
                    (1, 40, I["c"].rearrange("b (k p) -> (b k) p", p=P)),
                    (1, 48, I["ssm_d"].rearrange("b (k p) -> (b k) p", p=P))]
            for t, r, src in rows:
                sp.dma_start(SV[r:r + src.shape[0], t, :], src).then_inc(small_in, 16)
            sp.dma_start(IDENT[:, :], I["k_ident"]).then_inc(const_in, 16)
            sp.dma_start(SEL[:, :], I["k_sel"]).then_inc(const_in, 16)
            load_panels(sp, "ada0")
            for name, _n in STAGES[1:]:
                load_panels(sp, name)
            for b in range(5):
                sp.wait_ge(out_a, b + 1)
                sp.wait_ge(out_v, b + 1)
                dst = O["y_prompt"][0] if b == 0 else O["y_sample"][0][P * (b - 1):P * b, :]
                sp.dma_start(dst, OUTN[:, b % 2, :]).then_inc(out_dma[b % 2], 16)
            sp.wait_ge(out_dma[0], 48)
            sp.wait_ge(out_dma[1], 32)
            sp.wait_ge(kv_out, 32)

        @block.scalar
        def _(a):
            for b in range(5):
                src = I["x_prompt"][0] if b == 0 else I["x_sample"][0][P * (b - 1):P * b, :]
                a.dma_start(XN[:, b, :], src).then_inc(x_in, 16)
            for n in range(4):
                a.dma_start(MASK[:, n, :], I["k_masks"][n]).then_inc(attn_in, 16)
            a.dma_start(ROPE[:, 0, :], I["k_rope"][0]).then_inc(attn_in, 16)
            a.dma_start(ROPE[:, 1, :], I["k_rope"][1]).then_inc(attn_in, 16)
            a.dma_start(CK[:, :], I["cache_k"][0, 0].rearrange("s h d -> s (h d)")).then_inc(attn_in, 16)
            a.dma_start(CV[:, :], I["cache_v"][0, 0].rearrange("s h d -> s (h d)")).then_inc(attn_in, 16)
            a.dma_start(SINK[:, :], I["attn_sink"][0:1, :].to_broadcast([P, HEADS])).then_inc(sink_in, 16)
            a.wait_ge(sv_t, 1)
            a.activation(PV1[:, :], PS[:, 0, 0:P], ACT.Copy).then_inc(pv_ready, 1)
            a.activation(PV2[:, :], PS[:, 1, 0:56], ACT.Copy).then_inc(pv_ready, 1)
            a.wait_ge(pv_ready, 2)
            a.activation(SC[:, :, :].rearrange("p s k -> p (s k)"), PV2[:, 32:48], ACT.Silu).then_inc(silu_c, 1)
            a.wait_ge(silu_c, 1)
            a.wait_ge(memset_done, 3)
            sc = SC[:, :, :].rearrange("p s k -> p k s")
            a.activation(CS[:, :, 0:2], sc, ACT.Copy).then_inc(cs_ready, 1)
            a.activation(CS2[:, :, 0:2], sc, ACT.Copy).then_inc(cs_ready, 1)
            for u in range(SLOTS):
                split_hi(u, u, first=True)
            for k in range(KT):
                a.wait_ge(x_t, k + 1)
                a.activation(X[:, k, :], PSF[:, XBANK(k) * 512:XBANK(k) * 512 + TOK], ACT.Copy).then_inc(x_ready, 1)
            act_split_only("ada0")
            for k in range(KT):
                act_high(0, k)
            act_split_only("qkv")
            act_attention_start()
            for B in range(2):
                act_turn(None, B)
            for j in range(4):
                for B in range(2):
                    act_turn(j, B)
            act_split_only("wo")
            a.wait_ge(kv_out, 32)
            act_norm_modulate(0, 1)
            for ph in range(3):
                act_gated(f"up0{ph}", ACT.Silu, 0)
                act_split_only(f"down0{ph}")
            if LAYERS == 2:
                act_split_only("ada1")
                act_ssm_start()
                over_batches(a, act_prep)
                act_norm_modulate(1, 2)
                act_split_only("win")
                act_ssm()
                act_gated("glu", ACT.Sigmoid, 0)
                act_split_only("wout")
                act_norm_modulate(2, 3)
                for ph in range(3):
                    act_gated(f"up1{ph}", ACT.Silu, 0)
                    act_split_only(f"down1{ph}")
            last = 2 * LAYERS - 1
            act_norm(last)
            for k in range(KT):
                act_norm_shift(last, k)
            act_out(a)

        @block.vector
        def _(v):
            nc.vector.memset(MEANW[:, :], 1.0 / D).then_inc(memset_done, 1)
            nc.vector.memset(EPS[:, :], LN_EPS / ALPHA ** 2).then_inc(memset_done, 1)
            nc.vector.memset(CS2[:, :, 2:4].bitcast(F32), 0.0).then_inc(memset_done, 1)
            v.wait_ge(cs_ready, 1)
            v.wait_ge(silu_c, 1)
            nc.vector.tensor_tensor(CS[:, :, 2:4], SC[:, :, :].rearrange("p s k -> p k s"), CS[:, :, 0:2].bitcast(F32),
                                    ALU.subtract).then_inc(cs_lo, 1)
            v.wait_ge(pv_ready, 2)
            for u in range(SLOTS):
                split_lo(u, u)
            dve_ada(0)
            dve_modulate(0, 0, 0, lambda k: nc.vector.wait_ge(x_ready, k + 1))
            dve_store("qkv", QKVT)
            dve_attention_start()
            for B in range(2):
                dve_turn(None, B)
            for j in range(4):
                for B in range(2):
                    dve_turn(j, B)
            dve_residual("wo", 0, 2)
            v.wait_ge(kv_out, 32)
            dve_norm_modulate(0, 1, 0, 3)
            for ph in range(3):
                dve_gated(f"up0{ph}", PAIRS_BEFORE[f"up0{ph}"])
                dve_residual(f"down0{ph}", 0, 5)
            if LAYERS == 2:
                dve_ada(1)
                dve_ssm_start()
                over_batches(v, dve_prep, vchain, 6)
                for done in (cp_out, bt_out, ks_out):
                    v.wait_ge(done, 16 * NB)
                dve_norm_modulate(1, 2, 1, 0)
                dve_store("win", UT)
                dve_ssm()
                dve_gated("glu", PAIRS_BEFORE["glu"])
                dve_residual("wout", 1, 2)
                dve_norm_modulate(2, 3, 1, 3)
                for ph in range(3):
                    dve_gated(f"up1{ph}", PAIRS_BEFORE[f"up1{ph}"])
                    dve_residual(f"down1{ph}", 1, 5)
            last = 2 * LAYERS - 1
            dve_norm(last)
            for k in range(KT):
                dve_norm_scale(last, k)
            dve_out(v)

        @block.gpsimd
        def _(g):
            g.wait_ge(att_kv, 4)
            g.dma_start(O["new_k"][0, 0].rearrange("s h d -> s (h d)"), KN[:, :]).then_inc(kv_out, 16)
            g.dma_start(O["new_v"][0, 0].rearrange("s h d -> s (h d)"), VN[:, 0, :]).then_inc(kv_out, 16)
            if LAYERS == 2:
                sp_ssm_start(g)
                g.wait_ge(ssm_v, 5)
                g.wait_ge(ssm_a, 11)
                g.wait_ge(ssm_t, 5)

                for T in range(NB):
                    pool_prep(T, T == 0)
                sp_ssm(g)
                g.wait_ge(fin_out, 32)

        @block.tensor
        def _(pe):
            pe.wait_ge(small_in, 96)
            pe.wait_ge(const_in, 32)
            nc.tensor.transpose(PS[:, 0, 0:P], SV[:, 0, :], IDENT[:, :])
            nc.tensor.transpose(PS[:, 1, 0:56], SV[0:56, 1, :], IDENT[0:56, 0:56]).then_inc(sv_t, 1)
            pe.wait_ge(x_in, 80)
            for k in range(KT):
                if k >= 2:
                    pe.wait_ge(x_ready, k - 1)
                for b in range(5):
                    ins = nc.tensor.transpose(PSF[:, XBANK(k) * 512 + P * b:XBANK(k) * 512 + P * b + P],
                                              XN[:, b, P * k:P * k + P], IDENT[:, :])
                ins.then_inc(x_t, 1)
            pe.wait_ge(cs_ready, 2)
            pe.wait_ge(cs_lo, 1)
            pe.wait_ge(x_ready, KT)
            pe_ada(pe, 0)
            pe.wait_ge(xl_ready, KT)
            pe_stage(pe, "qkv", XH, XL)
            pe_attention_start(pe)
            for B in range(2):
                pe_turn(pe, None, B)
            for j in range(4):
                for B in range(2):
                    pe_turn(pe, j, B)
            pe.wait_ge(att_ol, 20)
            pe_stage(pe, "wo", XH, XL)
            pe_norm(pe, 0)
            pe.wait_ge(xl_ready, 2 * KT)
            for ph in range(3):
                pe_stage(pe, f"up0{ph}", XH, XL)
                pe.wait_ge(hid_lo, PAIRS_BEFORE[f"up0{ph}"] + PHASES[ph][1])
                pe_stage(pe, f"down0{ph}", HH, HL, PHASES[ph][1])
            if LAYERS == 2:
                pe_ada(pe, 1)
                pe_ssm_start(pe)
                over_batches(pe, lambda T, first: pe_prep(pe, T, first))
                pe_norm(pe, 1)
                pe.wait_ge(xl_ready, 3 * KT)
                pe_stage(pe, "win", XH, XL)
                pe_ssm(pe)
                pe.wait_ge(gelu_lo, KT)
                pe_stage(pe, "glu", XH, XL)
                pe.wait_ge(hid_lo, PAIRS_BEFORE["glu"] + 8)
                pe_stage(pe, "wout", HH, HL)
                pe_norm(pe, 2)
                pe.wait_ge(xl_ready, 4 * KT)
                for ph in range(3):
                    pe_stage(pe, f"up1{ph}", XH, XL)
                    pe.wait_ge(hid_lo, PAIRS_BEFORE[f"up1{ph}"] + PHASES[ph][1])
                    pe_stage(pe, f"down1{ph}", HH, HL, PHASES[ph][1])
            pe_norm(pe, 2 * LAYERS - 1)
            pe_out(pe, 2 * LAYERS - 1)


OUTPUTS = {"y_prompt": (1, CTX, D), "y_sample": (1, LAT, D), "new_k": (1, 1, CTX, KV_HEADS, HD),
           "new_v": (1, 1, CTX, KV_HEADS, HD), "new_re": (1, 1, 2, GROUPS, STATE), "new_im": (1, 1, 2, GROUPS, STATE)}


def kernel(**inputs):
    import concourse.bacc as bacc
    from concourse.bass_utils import run_bass_kernel_spmd

    nc = bacc.Bacc("TRN2", target_bir_lowering=False, num_devices=1)
    arrays = {n: np.ascontiguousarray(a) for n, a in inputs.items()}
    arrays.update(host_constants())
    handles = {n: nc.dram_tensor("in_" + n, a.shape, mybir.dt.from_np(a.dtype), kind="ExternalInput").ap()
               for n, a in arrays.items()}
    outs = {n: nc.dram_tensor("out_" + n, s, F32, kind="ExternalOutput").ap() for n, s in OUTPUTS.items()}
    hybrid_step(nc, handles, outs)
    r = run_bass_kernel_spmd(nc, [{"in_" + n: a for n, a in arrays.items()}], core_ids=[0])
    return tuple(r.results[0]["out_" + n] for n in OUTPUTS)
```

```python
from contextlib import ExitStack, nullcontext

import numpy as np

import concourse.bass as bass
from concourse import mybir

ACT = mybir.ActivationFunctionType
ALU = mybir.AluOpType
AXIS_X = mybir.AxisListType.X
F32 = mybir.dt.float32
F32R = mybir.dt.float32r

P = 128
D = 1024
KT = D // P
CTX = 128
LAT = 512
TOK = CTX + LAT
HALF = TOK // 2
FF = 2816
FF_TILES = FF // P
HEADS = 16
KV_HEADS = 4
HD = 64
GROUPS = 64
GCH = 16
STATE = 64
CHUNK = 8
NCHUNK = TOK // CHUNK
CCH = CTX // CHUNK
LCH = LAT // CHUNK
ALPHA = 4.0 ** 0.25
LN_EPS = 1e-5
SCALE = HD ** -0.5
NEG = -1e30
SLOTS = 4
MODQ = 6 * KT

PHASES = [(0, 8), (8, 8), (16, 6)]
STAGES = [("qkv", 12), ("wo", 8)]
for _ph, (_f0, _n) in enumerate(PHASES):
    STAGES += [(f"up0{_ph}", 2 * _n), (f"down0{_ph}", 8)]
LAYERS = 2
STAGES += [("win", 8), ("glu", 16), ("wout", 8)]
for _ph, (_f0, _n) in enumerate(PHASES):
    STAGES += [(f"up1{_ph}", 2 * _n), (f"down1{_ph}", 8)]
BASE, COUNT = {}, {}
_at = 0
for _name, _n in STAGES:
    BASE[_name], COUNT[_name] = _at, _n
    _at += _n
PANELS = _at
ADA = 2 * MODQ
ADA_FIRST, ADA_SECOND = 2 * KT, MODQ + 2 * KT
ADA_SECOND_AT, ADA_THIRD_AT = BASE["wo"] + SLOTS, BASE["glu"] + SLOTS


def ada_before(name):
    return ADA_FIRST if name == "qkv" else ADA_SECOND if BASE[name] < BASE["glu"] else ADA
PAIRS_BEFORE, _at = {}, 0
for _name, _n in STAGES:
    PAIRS_BEFORE[_name] = _at
    if _name.startswith("up") or _name == "glu":
        _at += _n // 2


def host_constants():
    ident = np.eye(P, dtype=np.float32)
    masks = np.zeros((4, P, 4 * P), np.float32)
    q = np.arange(P)[:, None]
    k = np.arange(P)[None, :]
    masks[:, :, P:2 * P] = np.where(k >= q, 0.0, NEG)
    masks[:, :, 3 * P:] = np.where(k <= q, 0.0, NEG)
    masks[0, :, P:2 * P] = NEG
    masks[3, :, 3 * P:] = NEG
    t = np.arange(LAT)
    nf = HD // 4
    inv = np.power(np.float32(10000.0), -np.arange(nf, dtype=np.float32) / np.float32(nf)).astype(np.float32)
    ang = np.stack([(t // 64).astype(np.float32)[:, None] * inv, (t % 64).astype(np.float32)[:, None] * inv])
    rope = np.zeros((2, P, LAT), np.float32)
    for p in range(P):
        axis, half, f = (p % HD) // 32, (p % 32) // 16, p % 16
        rope[0, p] = np.cos(ang[axis, :, f])
        rope[1, p] = np.sin(ang[axis, :, f]) * (1.0 if half else -1.0)
    return {"k_ident": ident, "k_masks": masks, "k_rope": rope}


class Chain:

    def __init__(self, eng, sem):
        self.eng, self.sem, self.n, self.i, self.per = eng, sem, 0, None, 0

    def value(self):
        return self.n if self.i is None else self.n + self.i * self.per

    def link(self, ins):
        self.n += 1
        ins.then_inc(self.sem, 1)
        self.eng.wait_ge(self.sem, self.value())

    def enter(self, i, per):
        self.i, self.per, self.start = i, per, self.n

    def leave(self, trips):
        assert self.n - self.start == self.per, (self.n - self.start, self.per)
        self.n, self.i = self.start + self.per * trips, None


def hybrid_step(nc, I, O):
    ctx = ExitStack()
    with ctx:
        def psum(name, shape):
            return ctx.enter_context(nc.psum_tensor(name, shape, F32))

        def sem(name):
            return ctx.enter_context(nc.semaphore(name))

        top = [((nc.sbuf_base + 63) // 64) * 64]

        def place(name, shape, dt=F32, at=None):
            size = int(np.prod(shape[1:])) * 4
            size = (size + 31) // 32 * 32
            where = top[0] if at is None else at
            t = nc.alloc_sbuf_tensor_at(name, shape, dt, offset=where)
            if at is None:
                top[0] += size
            return t, where + size

        def sb(name, shape, dt=F32):
            return place(name, shape, dt)[0]

        X = sb("X", [P, KT, TOK])
        RAW = sb("RAW", [P, SLOTS, KT, P])
        WH = sb("WH", [P, SLOTS, KT, P], F32R)
        WL = sb("WL", [P, SLOTS, KT, P], F32R)
        IDENT = sb("IDENT", [P, P])
        MEANW = sb("MEANW", [P, P])
        EPS = sb("EPS", [P, 1])
        PV1 = sb("PV1", [P, P])
        PV2 = sb("PV2", [P, 56])
        MODS = sb("MODS", [P, 2, MODQ, 2])
        SC = sb("SC", [P, KT, 2])
        ROWS = sb("ROWS", [2, 2, SLOTS * P])
        MT = sb("MT", [2 * MODQ, 2, P])
        XH = sb("XH", [P, KT, TOK], F32R)
        XL = sb("XL", [P, KT, TOK], F32R)
        AR, AI = sb("AR", [P, 2, GROUPS]), sb("AI", [P, 2, GROUPS])
        H0, FINS = sb("H0", [P, 2, GROUPS]), sb("FINS", [P, 2, GROUPS])
        common_end = top[0]
        HH, e = place("HH", [P, KT, TOK], F32R, at=common_end)
        HL, e = place("HL", [P, KT, TOK], F32R, at=e)
        GT, e = place("GT", [P, 2, TOK], at=e)
        HT, ffn_end = place("HT", [P, 2, TOK], at=e)
        ACC, e = place("ACC", [P, TOK], at=common_end)
        SQ, e = place("SQ", [P, 2, TOK], at=e)
        YT, e = place("YT", [P, 2, TOK], at=e)
        XM, e = place("XM", [P, 2, TOK], at=e)
        RSTD, e = place("RSTD", [P, TOK], at=e)
        RT, e = place("RT", [P, TOK], at=e)
        STD, ln_end = place("STD", [P, TOK], at=e)
        XN, e = place("XN", [P, 5, D], at=ln_end)
        SV, e = place("SV", [P, 2, P], at=e)
        QKVT, e = place("QKVT", [P, 12, TOK], at=common_end)
        VN, e = place("VN", [P, 7, 2 * P], at=e)
        KR, e = place("KR", [P, 2, LAT + 2 * P], at=e)
        KCT, e = place("KCT", [P, 2, P], at=e)
        QR, e = place("QR", [P, 2, 4, P], at=e)
        S, e = place("S", [P, 8, 4 * P], at=e)
        PT, e = place("PT", [P, 4, 4, P], at=e)
        MASK, e = place("MASK", [P, 4, 4 * P], at=e)
        ROPE, e = place("ROPE", [P, 2, LAT], at=e)
        SWAP, e = place("SWAP", [P, LAT], at=e)
        CK, e = place("CK", [P, 2 * P], at=e)
        CV, e = place("CV", [P, 2 * P], at=e)
        KN, e = place("KN", [P, 2 * P], at=e)
        SINK, e = place("SINK", [P, HEADS], at=e)
        STAT, e = place("STAT", [P, 8, 8], at=e)
        xh_at = common_end - 4 * 512 - 2 * KT * TOK * 4
        G, e = place("G", [P, 2, 2, 8, 9, GCH], at=xh_at)
        BTS, e = place("BTS", [P, 2, 8, 2, P], at=e)
        BBS, e = place("BBS", [P, 2, 2, 8, GCH], at=e)
        assert e <= common_end - 4 * 512
        LAM, e = place("LAM", [GROUPS, 2, 2, STATE], at=common_end)
        GM, e = place("GM", [GROUPS, 6, 2, STATE], at=e)
        LDT, e = place("LDT", [GROUPS, 2], at=e)
        ZR, e = place("ZR", [GROUPS, P], at=e)
        ZI, e = place("ZI", [GROUPS, P], at=e)
        MAG, e = place("MAG", [GROUPS, P], at=e)
        SIN, e = place("SIN", [GROUPS, P], at=e)
        SINH, e = place("SINH", [GROUPS, P], at=e)
        T1, e = place("T1", [GROUPS, P], at=e)
        T2, e = place("T2", [GROUPS, P], at=e)
        T3, e = place("T3", [GROUPS, P], at=e)
        DB, small_end = place("DB", [GCH, D], at=e)
        KS, e = place("KS", [GCH, 2, 8, 15 * GCH], at=common_end)
        KM, e = place("KM", [GCH, 2, 8, GCH], at=e)
        BN, e = place("BN", [P, 2, GROUPS, GCH], at=max(e, small_end))
        CN, e = place("CN", [P, 2, KT, 2, STATE], at=e)
        BP, e = place("BP", [P, 2, 2, 8, P], at=e - 4 * 2 * 2 * 8 * P)
        Q1, e = place("Q1", [P, 8, 6, GCH], at=e)
        Q2, e = place("Q2", [P, 8, 6, GCH], at=e)
        AC, e = place("AC", [P, 6, GROUPS], at=e)
        CT, e = place("CT", [P, 2, KT, P], at=e)
        POW, e = place("POW", [P, 2, 9, GROUPS], at=e)
        POWB, e = place("POWB", [P, 2, 8, GROUPS], at=e)
        POWC, e = place("POWC", [P, 3, 9, GROUPS], at=e)
        BB, e = place("BB", [P, 2, GROUPS, GCH], at=e)
        DI, e = place("DI", [GCH, GROUPS, GCH], at=e)
        W1, e = place("W1", [P, 9 * P], at=e)
        W2, e = place("W2", [P, 9 * P], at=e)
        assert e <= nc.sbuf_usable_end
        SSM_DMAS = 15
        ENT, e = place("ENT", [P, 2, GROUPS, NCHUNK], at=xh_at)
        U8, e = place("U8", [P, GROUPS, NCHUNK], at=common_end)
        ST, st_end = place("ST", [P, TOK // CHUNK + 2, 2, GROUPS], at=common_end + 4 * KT * TOK)
        UT, _e = place("UT", [P, KT, TOK], at=common_end + 4 * KT * TOK)
        Y8, e = place("Y8", [P, GROUPS, NCHUNK], at=common_end + 4 * KT * TOK)
        YIN, e = place("YIN", [P, KT, TOK], at=e)
        assert e <= st_end
        BT, _e = place("BT", [P, 2, 8, 2, P], at=st_end)
        CPL, e = place("CPL", [P, 2, 2, 8, P], at=st_end)
        TOEP, e = place("TOEP", [P, 2, 8, P], at=e)
        SC1, e = place("SC1", [P, 2, 2, GROUPS], at=e)
        SC2, e = place("SC2", [P, 2, 2, GROUPS], at=e)
        FIN, e = place("FIN", [GROUPS, 2, P], at=e)
        assert e <= nc.sbuf_usable_end, (e, nc.sbuf_usable_end)
        B_SCR = nc.dram_tensor("b_scratch", (KT, P, 16 * P), F32, kind="Internal").ap()
        C_SCR = nc.dram_tensor("c_scratch", (KT, P, 16 * P), F32, kind="Internal").ap()
        M_SCR = nc.dram_tensor("m_scratch", (2, 2, MODQ * P), F32, kind="Internal").ap()
        K_SCR = nc.dram_tensor("k_scratch", (GROUPS, GCH, 15 * GCH), F32, kind="Internal").ap()
        U_SCR = nc.dram_tensor("u_scratch", (D, TOK), F32, kind="Internal").ap()
        OUTN, _e = place("OUTN", [P, 2, D], at=common_end)
        assert e <= nc.sbuf_usable_end, (e, nc.sbuf_usable_end)

        PS = psum("PS", [P, 8, 512])
        PSF = PS[:, :, :].rearrange("p b n -> p (b n)")

        def halves(bank):
            return PS[:, bank:bank + 2, 0:HALF]

        def by_half(ap):
            return ap.rearrange("p (h t) -> p h t", h=2)

        raw_in = [sem(f"raw_in{u}") for u in range(SLOTS)]
        hi_ready = sem("hi_ready")
        lo_ready = sem("lo_ready")
        pe_done = sem("pe_done")
        psum_free = sem("psum_free")
        silu_done = sem("silu_done")
        hid_hi = sem("hid_hi")
        hid_lo = sem("hid_lo")
        dve_chain = sem("dve_chain")
        pool_chain = sem("pool_chain")
        act_chain = sem("act_chain")
        sink_in = sem("sink_in")
        small_in = sem("small_in")
        const_in = sem("const_in")
        x_in = sem("x_in")
        attn_in = sem("attn_in")
        memset_done = sem("memset_done")
        sv_t = sem("sv_t")
        pv_ready = sem("pv_ready")
        silu_c = sem("silu_c")
        rows_read = sem("rows_read")
        rows_out = [sem(f"rows_out{u}") for u in range(2)]
        mt_in = sem("mt_in")
        mods_ps = sem("mods_ps")
        mods_read = sem("mods_read")
        ada_done = sem("ada_done")
        x_t = sem("x_t")
        x_ready = sem("x_ready")
        xm_ready = sem("xm_ready")
        xh_ready = sem("xh_ready")
        xl_ready = sem("xl_ready")
        ln_sum, ln_mean, ln_cent = sem("ln_sum"), sem("ln_mean"), sem("ln_cent")
        ln_sq, ln_sqsum, ln_std = sem("ln_sq"), sem("ln_sqsum"), sem("ln_std")
        ln_y, ln_x = sem("ln_y"), sem("ln_x")
        out_t, out_a, out_v = sem("out_t"), sem("out_a"), sem("out_v")
        out_dma = [sem(f"out_dma{u}") for u in range(2)]
        kv_out = sem("kv_out")
        (att_t, att_kv, att_qrot, att_s, att_max, att_stat, att_exp, att_p, att_tr, att_pt,
         att_pv, att_oh, att_ol) = [sem("att_" + x) for x in (
             "t", "kv", "qrot", "s", "max", "stat", "exp", "p", "tr", "pt", "pv", "oh", "ol")]
        ATTN_DMAS = 8
        (ssm_in, ssm_a, ssm_v, ssm_t, g_ready, kern_ps, ks_copied, ks_ready, bp_ready, bpv_ready, bt_ps, bt_ready,
         u_out, u_in, inc_ps, inc_a, inc_v, scan_t, scan_done, ent_a, ent_v, y_ps, y_ready, fin_ps,
         fin_ready, fin_out, gelu_done, gelu_hi, gelu_lo) = [sem("s5_" + x) for x in (
             "in", "a", "v", "t", "g", "kern_ps", "ks_copied", "ks", "bp", "bpv", "bt_ps", "bt",
             "u_out", "u_in", "inc_ps", "inc_a", "inc_v", "scan_t", "scan", "ent_a", "ent_v", "y_ps", "y", 
             "fin_ps", "fin", "fin_out", "gelu", "gelu_hi", "gelu_lo")]
        cp_out, bt_out, ks_out = [[sem(f"s5_{x}_out{u}") for u in range(2)] for x in ("cp", "bt", "ks")]
        bt_in = [sem(f"s5_bt_in{u}") for u in range(2)]
        cp_in = [sem(f"s5_cp_in{u}") for u in range(2)]
        y_out = [sem(f"s5_y_out{m}") for m in range(KT)]
        y_in = [sem(f"s5_y_in{m}") for m in range(KT)]
        pchain = Chain(nc.gpsimd, pool_chain)

        def loop(eng, trips):
            return eng.Fori(0, trips) if trips > 1 else nullcontext(0)

        def w_view(name, layer=0):
            return I[name][layer]

        def panel_parts(name, i, u):
            full = RAW[:, u, :, :]
            if name == "qkv":
                w = I["w_qkv"][0].rearrange("(k p) n -> p k n", p=P)
                if isinstance(i, int) and i == 2:
                    return [(full, w[:, :, D + P * u:D + P * u + P])]
                return [(RAW[:, u, :, HD * h:HD * h + HD], w[:, :, bass.ds(512 * i + 256 * h + HD * u, HD)])
                        for h in range(2)]
            if name == "wo":
                w = I["w_o"][0].rearrange("(b h j d) n -> b h d j n", b=2, h=2, j=4)
                return [(RAW[HD * h:HD * h + HD, u, 4 * b:4 * b + 4, :], w[b, h][:, :, bass.ds(512 * i + P * u, P)])
                        for b in range(2) for h in range(2)]
            if name.startswith("up"):
                layer, ph = int(name[2]), int(name[3])
                w = I["ffn_w1" if u % 2 == 0 else "ffn_w3"][layer].rearrange("(k p) n -> p k n", p=P)
                return [(full, w[:, :, bass.ds(PHASES[ph][0] * P + 256 * i + P * (u // 2), P)])]
            if name.startswith("down"):
                layer, ph = int(name[4]), int(name[5])
                f0, n = PHASES[ph]
                w = I["ffn_w2"][layer].rearrange("(k p) n -> p k n", p=P)
                return [(RAW[:, u, 0:n, :], w[:, f0:f0 + n, bass.ds(512 * i + P * u, P)])]
            if name == "glu":
                w = I["ssm_w_glu"][0].rearrange("(k p) (v c n) -> p k v c n", p=P, v=2, n=P)
                src = w[:, :, 1 - u % 2, bass.ds(2 * i + u // 2, 1), :]
                return [(full, src.rearrange("p k a n -> p k (a n)"))]
            w = I["ssm_w_in" if name == "win" else "ssm_w_out"][0].rearrange("(k p) n -> p k n", p=P)
            return [(full, w[:, :, bass.ds(512 * i + P * u, P)])]

        def load_turn(sp, name, i, first=False, after_ada=0):
            for u in range(SLOTS):
                n = BASE[name] + SLOTS * i + u
                if after_ada:
                    sp.wait_ge(ada_done, after_ada - SLOTS + 1 + u)
                elif not first:
                    sp.wait_ge(hi_ready, n - SLOTS + 1)
                    sp.wait_ge(lo_ready, n - SLOTS + 1)
                parts = panel_parts(name, i, u)
                for dst, src in parts:
                    sp.dma_start(dst, src).then_inc(raw_in[u], 64 // len(parts))

        def load_stage(sp, name):
            with loop(sp, COUNT[name] // SLOTS) as i:
                load_turn(sp, name, i)

        def load_ada(sp, first, count, dense=None):
            layer, col = divmod(first, MODQ)
            w = I["w_ada"][layer].rearrange("(u k p) n -> u p k n", p=P, u=SLOTS)

            def body(i, peeled=False):
                for u in range(SLOTS):
                    if not peeled:
                        sp.wait_ge(ada_done, first + SLOTS * i + u - SLOTS + 1)
                    elif dense:
                        sp.wait_ge(hi_ready, dense - SLOTS + 1 + u)
                        sp.wait_ge(lo_ready, dense - SLOTS + 1 + u)
                    src = w[u][:, :, bass.ds(SLOTS * P * i + P * col, SLOTS * P)]
                    sp.dma_start(RAW[:, u].rearrange("p k m -> p (k m)").rearrange("p (k n) -> p k n", k=2), src
                                 ).then_inc(raw_in[u], 64)

            if dense is None:
                with sp.Fori(0, count // SLOTS) as i:
                    body(i)
            else:
                body(0, peeled=True)
                with sp.Fori(1, count // SLOTS) as i:
                    body(i)

        def split_hi(n, u, ada, first=False):
            nc.scalar.wait_ge(raw_in[u], (n - u) * 16 + 64 + ada * 16)
            if not first:
                nc.scalar.wait_ge(pe_done, n - SLOTS + 1)
            nc.scalar.activation(WH[:, u], RAW[:, u], ACT.Copy).then_inc(hi_ready, 1)

        def split_lo(n, u):
            nc.vector.wait_ge(hi_ready, n + 1)
            nc.vector.tensor_tensor(WL[:, u], RAW[:, u], WH[:, u].bitcast(F32), ALU.subtract).then_inc(lo_ready, 1)

        def stage_loop(eng, name, body):
            trips = COUNT[name] // SLOTS
            if BASE[name] + COUNT[name] == PANELS:
                with loop(eng, trips - 1) as i:
                    body(i, False)
                body(trips - 1, True)
            else:
                with loop(eng, trips) as i:
                    body(i, False)

        def pe_stage(pe, name, moving_h, moving_l, kt=KT):
            base = BASE[name]

            def body(i, last, first=False):
                for u in range(SLOTS):
                    n = base + SLOTS * i + u
                    if not first:
                        pe.wait_ge(psum_free, n - SLOTS + 1)
                    pe.wait_ge(hi_ready, n + 1)
                    pe.wait_ge(lo_ready, n + 1)
                    for k in range(kt):
                        for w, m, start, stop in ((WH, moving_h, k == 0, False), (WH, moving_l, False, False),
                                                 (WL, moving_h, False, k == kt - 1)):
                            for h in range(2):
                                ins = nc.tensor.matmul(PS[:, 2 * u + h, 0:HALF], w[:, u, k, :],
                                                       m[:, k, HALF * h:HALF * h + HALF], start=start, stop=stop)
                    ins.then_inc(pe_done, 1)

            if base == 0:
                body(0, False, first=True)
                with pe.Fori(1, COUNT[name] // SLOTS) as i:
                    body(i, False)
            else:
                stage_loop(pe, name, body)

        def pe_ada(pe, group, bank):
            a = SLOTS * group
            before = 0 if a < ADA_FIRST else ADA_SECOND_AT if a < ADA_SECOND else ADA_THIRD_AT
            if group:
                pe.wait_ge(rows_read, group)
            for u in range(SLOTS):
                pe.wait_ge(raw_in[u], 64 * (group + 1) + 16 * before)
                for k in range(2):
                    ins = nc.tensor.matmul(PS[0:2, bank, :], SC[:, 2 * u + k, :],
                                           RAW[:, u].rearrange("p k m -> p (k m)")[:, 512 * k:512 * k + 512],
                                           start=(u + k == 0), stop=(u == 3 and k == 1))
                ins.then_inc(ada_done, 1)

        ADA_PARTS = [(0, 0, 2, 3, 0), (0, 2, 6, 7, 0), (1, 0, 2, 7, P), (1, 2, 6, 7, 0)]
        GROUPS_IN = [4, 12, 16, 24]

        def act_rows(group, bank):
            a = nc.scalar
            a.wait_ge(ada_done, SLOTS * group + SLOTS)
            if group >= 2:
                a.wait_ge(rows_out[group % 2], 16 * (group // 2))
            a.activation(ROWS[:, group % 2, :], PS[0:2, bank, :], ACT.Copy).then_inc(rows_read, 1)

        def pool_ada(part):
            g = nc.gpsimd
            layer, first, end, bank, c0 = ADA_PARTS[part]
            for group in range(GROUPS_IN[part - 1] if part else 0, GROUPS_IN[part]):
                g.wait_ge(rows_read, group + 1)
                at = SLOTS * P * group - MODQ * P * layer
                g.dma_start(M_SCR[layer][:, at:at + SLOTS * P], ROWS[:, group % 2, :]).then_inc(rows_out[group % 2], 16)
            for u in range(2):
                g.wait_ge(rows_out[u], 8 * GROUPS_IN[part])
            if part >= 2:
                g.wait_ge(mods_ps, part - 1)
            n = (end - first) * KT
            for s in range(2):
                g.dma_start(MT[n * s:n * s + n, part % 2, :], M_SCR[layer, s].rearrange("(q p) -> q p", p=P)
                            [first * KT:end * KT, :]).then_inc(mt_in, 16)

        def pe_mods(pe, part):
            layer, first, end, bank, c0 = ADA_PARTS[part]
            n = 2 * (end - first) * KT
            pe.wait_ge(mt_in, 32 * part + 32)
            pe.wait_ge(rows_read, GROUPS_IN[max(part, 2) if part else 0])
            nc.tensor.transpose(PS[:, bank, c0:c0 + n], MT[0:n, part % 2, :], IDENT[0:n, 0:n]).then_inc(mods_ps, 1)

        def pe_norm(pe, q):
            pe.wait_ge(ln_sum, q + 1)
            for h in range(2):
                ins = nc.tensor.matmul(PS[:, h, 0:HALF], MEANW[:, :], ACC[:, HALF * h:HALF * h + HALF],
                                       start=True, stop=True)
            ins.then_inc(ln_mean, 1)
            for k in range(KT):
                pe.wait_ge(ln_sq, KT * q + k + 1)
                for h in range(2):
                    ins = nc.tensor.matmul(PS[:, 2 + h, 0:HALF], MEANW[:, :], SQ[:, k % 2, HALF * h:HALF * h + HALF],
                                           start=(k == 0), stop=(k == KT - 1))
                ins.then_inc(ln_sqsum, 1)

        def act_gated(name, func, pairs_before):
            base = BASE[name]

            def body(i, last):
                for c in range(2):
                    n = base + SLOTS * i + 2 * c
                    nc.scalar.wait_ge(pe_done, n + 1)
                    nc.scalar.activation(by_half(GT[:, c, :]), halves(4 * c), func).then_inc(silu_done, 1)
                    if not last:
                        split_hi(n + SLOTS, 2 * c, ada=ada_before(name))
                        split_hi(n + SLOTS + 1, 2 * c + 1, ada=ada_before(name))
                    nc.scalar.wait_ge(psum_free, n + 2)
                    nc.scalar.activation(HH[:, bass.ds(2 * i + c, 1), :].rearrange("p a t -> p (a t)"),
                                         HT[:, c, :], ACT.Copy).then_inc(hid_hi, 1)

            stage_loop(nc.scalar, name, body)

        def dve_gated(name, pairs_before):
            base = BASE[name]

            def body(i, last):
                for c in range(2):
                    n = base + SLOTS * i + 2 * c
                    pair = pairs_before + 2 * i + c
                    nc.vector.wait_ge(silu_done, pair + 1)
                    nc.vector.wait_ge(pe_done, n + 2)
                    if pairs_before:
                        nc.vector.wait_ge(hid_lo, pair - 1)
                    nc.vector.tensor_tensor(by_half(HT[:, c, :]), halves(4 * c + 2), by_half(GT[:, c, :]),
                                            ALU.mult).then_inc(psum_free, 2)
                    if not last:
                        split_lo(n + SLOTS, 2 * c)
                        split_lo(n + SLOTS + 1, 2 * c + 1)
                    nc.vector.wait_ge(hid_hi, pair + 1)
                    one = bass.ds(2 * i + c, 1)
                    nc.vector.tensor_tensor(HL[:, one, :].rearrange("p a t -> p (a t)"), HT[:, c, :],
                                            HH[:, one, :].rearrange("p a t -> p (a t)").bitcast(F32),
                                            ALU.subtract).then_inc(hid_lo, 1)

            stage_loop(nc.vector, name, body)

        def act_split_only(name):
            base = BASE[name]

            def body(i, last):
                for u in range(SLOTS):
                    if not last:
                        split_hi(base + SLOTS * i + u + SLOTS, u, ada=ada_before(name))

            stage_loop(nc.scalar, name, body)

        def stream_parts(permuted):
            if not permuted:
                return [(0, 0, slice(0, CTX), slice(0, CTX)), (1, 0, slice(CTX, HALF), slice(CTX, HALF)),
                        (1, 1, slice(0, HALF), slice(HALF, TOK))]
            return [(s, h, cs, h) for h in range(2) for s, cs in ((0, slice(0, CCH)), (1, slice(CCH, NCHUNK)))]

        def dve_residual(name, layer, gate):
            base = BASE[name]

            def body(i, last):
                for u in range(SLOTS):
                    n = base + SLOTS * i + u
                    nc.vector.wait_ge(pe_done, n + 1)
                    tile = X[:, bass.ds(SLOTS * i + u, 1), :].rearrange("p a t -> p (a t)")
                    col = MODS[:, layer, bass.ds(gate * KT + SLOTS * i + u, 1), :].rearrange("p a s -> p (a s)")
                    for s, b, cols, where in stream_parts(layer == 1):
                        if layer == 0:
                            src, dst = PS[:, 2 * u + b, cols], tile[:, where]
                        else:
                            src = PS[:, 2 * u + b, 0:HALF].rearrange("p (t c) -> p t c", c=NCHUNK)[:, :, cols]
                            dst = tile[:, HALF * b:HALF * b + HALF].rearrange("p (t c) -> p t c", c=NCHUNK)[:, :, cols]
                        ins = nc.vector.scalar_tensor_tensor(out=dst, in0=src, scalar=col[:, s:s + 1], in1=dst,
                                                             op0=ALU.mult, op1=ALU.add)
                    ins.then_inc(psum_free, 1)
                    if not last:
                        split_lo(n + SLOTS, u)

            stage_loop(nc.vector, name, body)

        def dve_store(name, dest):
            base = BASE[name]

            def body(i, last):
                for u in range(SLOTS):
                    n = base + SLOTS * i + u
                    nc.vector.wait_ge(pe_done, n + 1)
                    nc.vector.tensor_copy(by_half(dest[:, bass.ds(SLOTS * i + u, 1), :].rearrange("p a t -> p (a t)")),
                                          halves(2 * u)).then_inc(psum_free, 1)
                    if not last:
                        split_lo(n + SLOTS, u)

            stage_loop(nc.vector, name, body)

        vchain = Chain(nc.vector, dve_chain)
        v_link = vchain.link

        def dve_mods(part):
            v = nc.vector
            layer, first, end, bank, c0 = ADA_PARTS[part]
            q = slice(first * KT, end * KT)
            n = (end - first) * KT
            v.wait_ge(mods_ps, max(part + 1, 3) if part else 1)
            bias = PV1[:, MODQ * layer:MODQ * (layer + 1)][:, q].unsqueeze(2).to_broadcast([P, n, 2])
            v.tensor_tensor(MODS[:, layer, q], PS[:, bank, c0:c0 + 2 * n].rearrange("p (s q) -> p q s", s=2), bias,
                            ALU.add).then_inc(mods_read, 1)
            v.wait_ge(mods_read, part + 1)
            for sixth in range(first, end):
                cols = MODS[:, layer, sixth * KT:(sixth + 1) * KT, :]
                if sixth % 3 == 1:
                    v_link(v.tensor_scalar(cols, cols, 1.0, None, ALU.add))
                if sixth % 3 == 2:
                    v_link(v.tensor_scalar(cols, cols, 1.0 / ALPHA, None, ALU.mult))

        def perm_view(tile):
            return tile.rearrange("p (t c) -> p t c", c=NCHUNK)

        norm_after = [BASE["wo"] + 8, BASE["down02"] + 8, BASE.get("wout", 0) + 8, BASE.get("down12", 0) + 8]

        def dve_norm(q):
            v = nc.vector
            v.wait_ge(psum_free, norm_after[q])
            v.tensor_reduce(ACC[:, :], X[:, :, :].rearrange("p k t -> p t k"), AXIS_X, ALU.add).then_inc(ln_sum, 1)
            v.wait_ge(ln_mean, q + 1)
            for k in range(KT):
                v.tensor_tensor(by_half(X[:, k, :]), by_half(X[:, k, :]), halves(0), ALU.subtract).then_inc(ln_cent, 1)
            v.wait_ge(ln_std, q + 1)
            v_link(v.reciprocal(RSTD[:, :], STD[:, :]))
            v_link(v.tensor_tensor(RT[:, :], RSTD[:, :], RSTD[:, :], ALU.mult))
            v_link(v.scalar_tensor_tensor(out=by_half(RT[:, :]), in0=halves(2), scalar=LN_EPS / ALPHA ** 2,
                                          in1=by_half(RT[:, :]), op0=ALU.add, op1=ALU.mult))
            v_link(v.tensor_scalar(RT[:, :], RT[:, :], -0.5, 1.5, ALU.mult, ALU.add))
            v_link(v.tensor_tensor(RSTD[:, :], RSTD[:, :], RT[:, :], ALU.mult))

        def dve_norm_scale(q, k):
            v = nc.vector
            if k >= 2:
                v.wait_ge(ln_x, KT * q + k - 1)
            v.wait_ge(ln_cent, KT * q + k + 1)
            v.scalar_tensor_tensor(out=YT[:, k % 2, :], in0=X[:, k, :], scalar=PV1[:, 2 * MODQ + KT * q + k:2 * MODQ + KT * q + k + 1],
                                   in1=RSTD[:, :], op0=ALU.mult, op1=ALU.mult).then_inc(ln_y, 1)

        def act_norm(q):
            a = nc.scalar
            for k in range(KT):
                a.wait_ge(ln_cent, KT * q + k + 1)
                if k >= 2:
                    a.wait_ge(ln_sqsum, KT * q + k - 1)
                a.activation(SQ[:, k % 2, :], X[:, k, :], ACT.Square).then_inc(ln_sq, 1)
            a.wait_ge(ln_sqsum, KT * q + KT)
            a.activation(by_half(STD[:, :]), halves(2), ACT.Sqrt, bias=EPS[:, :]).then_inc(ln_std, 1)

        def act_norm_shift(q, k):
            a = nc.scalar
            a.wait_ge(ln_y, KT * q + k + 1)
            src, dst = YT[:, k % 2, :], X[:, k, :]
            if q == 1 and LAYERS == 2:
                src, dst = src.rearrange("p (c t) -> p t c", t=CHUNK), perm_view(dst)
            if q == 3:
                src, dst = perm_view(src), dst.rearrange("p (c t) -> p t c", t=CHUNK)
            a.activation(dst, src, ACT.Identity, bias=PV2[:, KT * q + k:KT * q + k + 1]).then_inc(ln_x, 1)

        def dve_modulate(r, layer, shift, before):
            v = nc.vector

            def low(k):
                v.wait_ge(xh_ready, KT * r + k + 1)
                v.tensor_tensor(XL[:, k, :], XM[:, k % 2, :], XH[:, k, :].bitcast(F32), ALU.subtract).then_inc(xl_ready, 1)

            for k in range(KT):
                before(k)
                if k >= 2:
                    v.wait_ge(xl_ready, KT * r + k - 1)
                sc = MODS[:, layer, (shift + 1) * KT + k, :]
                sh = MODS[:, layer, shift * KT + k, :]
                for s in range(2):
                    if r < 2:
                        cols = slice(0, CTX) if s == 0 else slice(CTX, TOK)
                        src, dst = X[:, k, cols], XM[:, k % 2, cols]
                    else:
                        cols = slice(0, CCH) if s == 0 else slice(CCH, NCHUNK)
                        src = perm_view(X[:, k, :])[:, :, cols]
                        dst = perm_view(XM[:, k % 2, :])[:, :, cols]
                    ins = v.tensor_scalar(dst, src, sc[:, s:s + 1], sh[:, s:s + 1], ALU.mult, ALU.add)
                ins.then_inc(xm_ready, 1)
                if k:
                    low(k - 1)
            low(KT - 1)

        def act_high(r, k):
            a = nc.scalar
            a.wait_ge(xm_ready, KT * r + k + 1)
            a.activation(XH[:, k, :], XM[:, k % 2, :], ACT.Copy).then_inc(xh_ready, 1)

        def dve_norm_modulate(q, r, layer, shift):
            dve_norm(q)

            def before(k):
                if k == 0:
                    dve_norm_scale(q, 0)
                if k < KT - 1:
                    dve_norm_scale(q, k + 1)
                nc.vector.wait_ge(ln_x, KT * q + k + 1)

            dve_modulate(r, layer, shift, before)

        def act_norm_modulate(q, r):
            act_norm(q)
            act_norm_shift(q, 0)
            for k in range(KT):
                if k < KT - 1:
                    act_norm_shift(q, k + 1)
                act_high(r, k)

        qkv_end = BASE["wo"]

        STEPS = [(block, B, h) for block in (None, 0, 1, 2, 3) for B in range(2) for h in range(2)]

        FIRST_ADA_STEP = len(STEPS) - GROUPS_IN[2] + GROUPS_IN[0]

        def key_tiles(block):
            return 1 if block is None else 4

        def pe_attention_start(pe):
            pe.wait_ge(psum_free, qkv_end)
            pe.wait_ge(attn_in, 16 * ATTN_DMAS)
            t = lambda bank, col, src: nc.tensor.transpose(PS[:, bank, P * col:P * col + P], src, IDENT[:, :])
            for bank in range(2):
                for b in range(2):
                    for d in range(2):
                        c0 = CTX + P * (2 * bank + b)
                        ins = t(bank, 2 * b + d, QKVT[:, 10 + d, c0:c0 + P])
                ins.then_inc(att_t, 1)
            for d in range(2):
                t(2, d, QKVT[:, 10 + d, 0:CTX])
                ins = t(2, 2 + d, QKVT[:, 8 + d, 0:CTX])
            ins.then_inc(att_t, 1)
            for d in range(2):
                ins = t(3, d, CK[:, P * d:P * d + P])
            ins.then_inc(att_t, 1)

        def act_attention_start():
            a = nc.scalar
            for bank in range(2):
                a.wait_ge(att_t, bank + 1)
                a.activation(VN[:, 2 + 2 * bank:4 + 2 * bank, :].rearrange("p b d -> p (b d)"), PS[:, bank, :],
                             ACT.Copy).then_inc(att_kv, 1)
            a.wait_ge(att_t, 3)
            a.activation(VN[:, 0, :], PS[:, 2, 0:2 * P], ACT.Copy).then_inc(att_kv, 1)
            a.activation(KN[:, :], PS[:, 2, 2 * P:4 * P], ACT.Copy).then_inc(att_kv, 1)
            a.wait_ge(att_t, 4)
            a.activation(KCT[:, :, :].rearrange("p b d -> p (b d)"), PS[:, 3, 0:2 * P], ACT.Copy).then_inc(att_kv, 1)

        SWAP_HALVES = [(p + 16) % 32 for p in range(32)]

        def dve_rotate(out, src, cos, sin, swap):
            v = nc.vector
            v_link(v.stream_shuffle(swap, src, SWAP_HALVES))
            v_link(v.tensor_tensor(swap, swap, sin, ALU.mult))
            v_link(v.tensor_tensor(out, src, cos, ALU.mult))
            return v.tensor_tensor(out, out, swap, ALU.add)

        def dve_attention_start():
            v = nc.vector
            v.wait_ge(psum_free, qkv_end)
            v.wait_ge(attn_in, 16 * ATTN_DMAS)
            v.wait_ge(sink_in, 16)
            v_link(v.memset(VN[:, 1, :], 0.0))
            v_link(v.memset(VN[:, 6, :], 0.0))
            for B in range(2):
                v_link(v.memset(KR[:, B, 0:P], 0.0))
                v_link(v.memset(KR[:, B, P + LAT:], 0.0))
                v_link(dve_rotate(KR[:, B, P:P + LAT], QKVT[:, 8 + B, CTX:TOK], ROPE[:, 0, :], ROPE[:, 1, :], SWAP[:, :]))

        def queries(block, B):
            first = 0 if block is None else block * P + CTX
            return QKVT[:, 4 * B:4 * B + 4, bass.ds(first, P)]

        def attended(T, block, B, rows):
            first = 0 if block is None else block * P + CTX
            return T[rows, 4 * B:4 * B + 4, first:first + P]

        def pv_out(h):
            return PS[HD * h:HD * h + HD, 6, :].rearrange("p (j q) -> p j q", j=4)

        def dve_queries(t):
            block, B, h = STEPS[t]
            v, turn = nc.vector, t // 2
            tok = slice(block * P, block * P + P)
            cos = ROPE[:, 0, tok].unsqueeze(1).to_broadcast([P, 4, P])
            sin = ROPE[:, 1, tok].unsqueeze(1).to_broadcast([P, 4, P])
            if turn >= 4:
                v.wait_ge(att_s, 8 * (turn - 2) + 8)
            dve_rotate(QR[:, turn % 2, :, :], queries(block, B), cos, sin,
                       SWAP[:, :].rearrange("p (a t) -> p a t", a=4)).then_inc(att_qrot, 1)

        def dve_mask(t):
            block, B, h = STEPS[t]
            v, width, c = nc.vector, P * key_tiles(block), 4 * (t % 2)
            if t >= 2:
                v.wait_ge(att_tr, 4 * (t - 2) + 4)
            for j in range(4):
                v.wait_ge(att_s, 4 * t + j + 1)
                v.tensor_tensor_reduce(out=S[:, c + j, 0:width], in0=PS[:, j, 0:width], in1=MASK[:, block or 0, 0:width],
                                       scale=1.0, scalar=-3.0e38, op0=ALU.add, op1=ALU.max,
                                       accum_out=STAT[:, 0, c + j:c + j + 1]).then_inc(att_max, 1)
            v.wait_ge(att_max, 4 * t + 4)
            row = lambda r: STAT[:, r, c:c + 4]
            sink = SINK[:, 8 * B + 4 * h:8 * B + 4 * h + 4]
            v_link(v.scalar_tensor_tensor(out=row(1), in0=row(0), scalar=SCALE, in1=sink, op0=ALU.mult, op1=ALU.max))
            v_link(v.tensor_scalar(row(2), row(1), -1.0, None, ALU.mult))
            v.tensor_tensor(row(3), sink, row(1), ALU.subtract).then_inc(att_stat, 1)

        def dve_normalize(t):
            block, B, h = STEPS[t]
            v, width, c = nc.vector, P * key_tiles(block), 4 * (t % 2)
            v.wait_ge(att_exp, 5 * t + 5)
            v_link(v.tensor_tensor(STAT[:, 6, c:c + 4], STAT[:, 4, c:c + 4], STAT[:, 5, c:c + 4], ALU.add))
            v_link(v.reciprocal(STAT[:, 7, c:c + 4], STAT[:, 6, c:c + 4]))
            for j in range(4):
                v.tensor_scalar(S[:, c + j, 0:width], S[:, c + j, 0:width], STAT[:, 7, c + j:c + j + 1], None,
                                ALU.mult).then_inc(att_p, 1)

        def dve_attended(t):
            block, B, h = STEPS[t]
            rows = slice(HD * h, HD * h + HD)
            nc.vector.wait_ge(att_oh, t + 1)
            nc.vector.tensor_tensor(attended(XL, block, B, rows), pv_out(h), attended(XH, block, B, rows).bitcast(F32),
                                    ALU.subtract).then_inc(att_ol, 1)

        def dve_attention():
            dve_mask(0)
            for t in range(len(STEPS)):
                if t + 2 < len(STEPS) and t % 2 == 0 and STEPS[t + 2][0] is not None:
                    dve_queries(t + 2)
                if t + 1 < len(STEPS):
                    dve_mask(t + 1)
                dve_normalize(t)
                if t:
                    dve_attended(t - 1)
            dve_attended(len(STEPS) - 1)

        def act_exp(t):
            block, B, h = STEPS[t]
            a, width, c = nc.scalar, P * key_tiles(block), 4 * (t % 2)
            a.wait_ge(att_stat, t + 1)
            a.activation(STAT[:, 5, c:c + 4], STAT[:, 3, c:c + 4], ACT.Exp).then_inc(att_exp, 1)
            for j in range(4):
                a.activation(S[:, c + j, 0:width], S[:, c + j, 0:width], ACT.Exp, bias=STAT[:, 2, c + j:c + j + 1],
                             scale=SCALE, accum_out=STAT[:, 4, c + j:c + j + 1]).then_inc(att_exp, 1)

        def act_attention():
            a = nc.scalar
            act_exp(0)
            for t, (block, B, h) in enumerate(STEPS):
                if t + 1 < len(STEPS):
                    act_exp(t + 1)
                kt = key_tiles(block)
                if t:
                    a.wait_ge(att_pv, t)
                for j in range(4):
                    a.wait_ge(att_tr, 4 * t + j + 1)
                    a.activation(PT[:, 0:kt, j, :], PS[:, 4 + j % 2, 0:P * kt].rearrange("p (k q) -> p k q", k=kt),
                                 ACT.Copy).then_inc(att_pt, 1)
                if t >= FIRST_ADA_STEP:
                    act_rows(GROUPS_IN[0] + t - FIRST_ADA_STEP, 7)
                a.wait_ge(att_pv, t + 1)
                a.activation(attended(XH, block, B, slice(HD * h, HD * h + HD)), pv_out(h), ACT.Copy).then_inc(att_oh, 1)

        def pe_scores(pe, t):
            block, B, h = STEPS[t]
            rows = slice(HD * h, HD * h + HD)
            if h == 0 and block is not None:
                pe.wait_ge(att_qrot, 2 * block + B + 1)
            for j in range(4):
                if t:
                    pe.wait_ge(att_max, 4 * (t - 1) + j + 1)
                keys = QKVT[rows, 8 + B, 0:CTX] if block is None else KCT[rows, B, :]
                ins = nc.tensor.matmul(PS[:, j, 0:P], queries(block, B)[rows, j, :], keys, start=True, stop=True)
                if block is not None:
                    ins = nc.tensor.matmul(PS[:, j, P:4 * P], QR[rows, (t // 2) % 2, j, :],
                                           KR[rows, B, P * block:P * block + 3 * P], start=True, stop=True)
                ins.then_inc(att_s, 1)

        def pe_attention(pe):
            pe.wait_ge(att_kv, 5)
            pe_scores(pe, 0)
            for t, (block, B, h) in enumerate(STEPS):
                if t + 1 < len(STEPS):
                    pe_scores(pe, t + 1)
                kt = key_tiles(block)
                for j in range(4):
                    pe.wait_ge(att_p, 4 * t + j + 1)
                    if 4 * t + j >= 2:
                        pe.wait_ge(att_pt, 4 * t + j - 1)
                    for k in range(kt):
                        ins = nc.tensor.transpose(PS[:, 4 + j % 2, P * k:P * k + P],
                                                  S[:, 4 * (t % 2) + j, P * k:P * k + P], IDENT[:, :])
                    ins.then_inc(att_tr, 1)
                if t >= FIRST_ADA_STEP:
                    pe_ada(pe, GROUPS_IN[0] + t - FIRST_ADA_STEP, 7)
                pe.wait_ge(att_pt, 4 * t + 4)
                if t >= 2:
                    pe.wait_ge(att_ol, t - 1)
                c0 = P * B + HD * h
                for k in range(kt):
                    val = VN[:, 0, :] if block is None else CV[:, :] if k == 0 else VN[:, block + k, :]
                    ins = nc.tensor.matmul(PS[HD * h:HD * h + HD, 6, :], val[:, c0:c0 + HD],
                                           PT[:, k, :, :].rearrange("p j q -> p (j q)"), start=(k == 0), stop=(k == kt - 1))
                ins.then_inc(att_pv, 1)

        NB = GROUPS // 8
        FWD, BWD = slice(0, STATE), slice(STATE, P)

        def complex_mult(eng, chn, out_re, out_im, ar, ai, br, bi, t1, t2, minus_bi=None):
            chn.link(eng.tensor_tensor(t1, ar, br, ALU.mult))
            chn.link(eng.tensor_tensor(t2, ai, bi, ALU.mult))
            chn.link(eng.tensor_tensor(out_re, t1, t2, ALU.subtract))
            chn.link(eng.tensor_tensor(t1, ar, bi if minus_bi is None else minus_bi, ALU.mult))
            chn.link(eng.tensor_tensor(t2, ai, br, ALU.mult))
            return eng.tensor_tensor(out_im, t1, t2, ALU.add if minus_bi is None else ALU.subtract)

        def sp_ssm_start(sp):
            sp.wait_ge(psum_free, BASE["win"])
            by_group = lambda a: a.rearrange("d g p -> g d p")
            sp.dma_start(LAM[:, 0], by_group(I["ssm_lam_re"][0])).then_inc(ssm_in, 16)
            sp.dma_start(LAM[:, 1], by_group(I["ssm_lam_im"][0])).then_inc(ssm_in, 16)
            sp.dma_start(GM[:, 4], by_group(I["state_ssm_re"][0, 0])).then_inc(ssm_in, 16)
            sp.dma_start(GM[:, 5], by_group(I["state_ssm_im"][0, 0])).then_inc(ssm_in, 16)
            for d in range(2):
                sp.dma_start(LDT[:, d:d + 1], I["ssm_log_dt"][0, d].rearrange("(g a) -> g a", a=1)).then_inc(ssm_in, 16)
            for r, nm in enumerate(("re", "im")):
                for d in range(2):
                    rows = slice(STATE * d, STATE * d + STATE)
                    sp.dma_start(BN[rows, r], I["ssm_b_" + nm][0, d].rearrange("g p m -> p g m")).then_inc(ssm_in, 16)
                    sp.dma_start(CN[:, r, :, d, :], I["ssm_c_" + nm][0, d].rearrange("g n p -> (g n) p")
                                 .rearrange("(T q) p -> q T p", q=P)).then_inc(ssm_in, 16)
            sp.dma_start(DB[:, :], I["ssm_d"][0:1, :].to_broadcast([GCH, D])).then_inc(ssm_in, 16)

        TWO_PI = (6.28125, 0.0019350051879882812, 3.0199161e-07)
        ROUND = 12582912.0

        def act_ssm_start():
            a = nc.scalar
            a.wait_ge(ssm_in, 16 * SSM_DMAS)
            a.activation(LDT[:, :], LDT[:, :], ACT.Exp).then_inc(ssm_a, 1)
            a.wait_ge(ssm_v, 1)
            a.activation(MAG[:, :], ZR[:, :], ACT.Exp).then_inc(ssm_a, 1)
            a.wait_ge(ssm_v, 2)
            a.activation(SINH[:, :], ZI[:, :], ACT.Sin, scale=0.5).then_inc(ssm_a, 1)
            a.activation(SIN[:, :], ZI[:, :], ACT.Sin).then_inc(ssm_a, 1)
            a.wait_ge(ssm_t, 1)
            a.activation(AC[:, :, :], PS[:, 0, 0:6 * GROUPS].rearrange("p (a g) -> p a g", g=GROUPS), ACT.Copy).then_inc(ssm_a, 1)
            for n in range(4):
                a.wait_ge(ssm_t, 2 + n)
                a.activation(CT[:, n // 2, 4 * (n % 2):4 * (n % 2) + 4, :].rearrange("p a n -> p (a n)"),
                             PS[:, 4 + n, :], ACT.Copy).then_inc(ssm_a, 1)
            a.wait_ge(ssm_v, 4)
            a.activation(POWB[0:64], POW[0:64, :, 0:8, :][:, :, ::-1, :], ACT.Copy).then_inc(ssm_a, 1)
            a.activation(POWB[64:P], POW[64:P, :, 0:8, :], ACT.Copy).then_inc(ssm_a, 1)
            a.activation(POWC[0:64, 0:2], POW[0:64], ACT.Copy).then_inc(ssm_a, 1)
            a.activation(POWC[0:64, 2], POW[0:64, 1], ACT.Copy, scale=-1.0).then_inc(ssm_a, 1)
            a.activation(POWC[64:P, 0:2], POW[64:P][:, :, ::-1, :], ACT.Copy).then_inc(ssm_a, 1)
            a.activation(POWC[64:P, 2], POW[64:P, 1][:, ::-1, :], ACT.Copy, scale=-1.0).then_inc(ssm_a, 1)

        def dve_ssm_start():
            v = nc.vector
            chn = vchain
            tt, ts = v.tensor_tensor, v.tensor_scalar
            v.wait_ge(ssm_in, 16 * SSM_DMAS)
            v.wait_ge(ssm_a, 1)
            dp = lambda t: t[:, :].rearrange("g (d p) -> g d p", d=2)
            dt = LDT[:, :].unsqueeze(2).to_broadcast([GROUPS, 2, STATE])
            tt(dp(ZR), LAM[:, 0], dt, ALU.mult).then_inc(ssm_v, 1)
            chn.link(tt(dp(ZI), LAM[:, 1], dt, ALU.mult))
            chn.link(ts(T1[:, :], ZI[:, :], 1.0 / (2 * np.pi), None, ALU.mult))
            chn.link(ts(T1[:, :], T1[:, :], ROUND, None, ALU.add))
            chn.link(ts(T1[:, :], T1[:, :], -ROUND, None, ALU.add))
            for part in TWO_PI:
                chn.link(v.scalar_tensor_tensor(out=ZI[:, :], in0=T1[:, :], scalar=-part, in1=ZI[:, :], op0=ALU.mult, op1=ALU.add))
            ts(ZI[:, :], ZI[:, :], 3.1415925, -3.1415925, ALU.min, ALU.max).then_inc(ssm_v, 1)
            v.wait_ge(ssm_a, 4)
            chn.link(tt(T1[:, :], SINH[:, :], SINH[:, :], ALU.mult))
            chn.link(ts(T1[:, :], T1[:, :], -2.0, 1.0, ALU.mult, ALU.add))
            gm = lambda r: GM[:, r].rearrange("g d p -> g (d p)")
            lam = lambda r: LAM[:, r].rearrange("g d p -> g (d p)")
            chn.link(tt(gm(0), MAG[:, :], T1[:, :], ALU.mult))
            chn.link(tt(gm(1), MAG[:, :], SIN[:, :], ALU.mult))
            chn.link(ts(T1[:, :], gm(0), -1.0, None, ALU.add))
            chn.link(tt(T2[:, :], lam(0), lam(0), ALU.mult))
            chn.link(tt(T3[:, :], lam(1), lam(1), ALU.mult))
            chn.link(tt(T2[:, :], T2[:, :], T3[:, :], ALU.add))
            chn.link(v.reciprocal(T2[:, :], T2[:, :]))
            chn.link(tt(gm(2), T1[:, :], lam(0), ALU.mult))
            chn.link(tt(T3[:, :], gm(1), lam(1), ALU.mult))
            chn.link(tt(gm(2), gm(2), T3[:, :], ALU.add))
            chn.link(tt(gm(2), gm(2), T2[:, :], ALU.mult))
            chn.link(tt(gm(3), gm(1), lam(0), ALU.mult))
            chn.link(tt(T3[:, :], T1[:, :], lam(1), ALU.mult))
            chn.link(tt(gm(3), gm(3), T3[:, :], ALU.subtract))
            tt(gm(3), gm(3), T2[:, :], ALU.mult).then_inc(ssm_v, 1)
            v.wait_ge(ssm_a, 5)
            chn.link(v.memset(POW[:, 0, 0, :], 1.0))
            chn.link(v.memset(POW[:, 1, 0, :], 0.0))
            chn.link(v.tensor_copy(POW[:, :, 1, :], AC[:, 0:2, :]))
            for have in (1, 2, 4):
                pw = lambda r: POW[:, r, 1:have + 1, :]
                by = lambda r: POW[:, r, have:have + 1, :].to_broadcast([P, have, GROUPS])
                tmp = [W1[:, 0:have * GROUPS].rearrange("p (k g) -> p k g", g=GROUPS),
                       W2[:, 0:have * GROUPS].rearrange("p (k g) -> p k g", g=GROUPS)]
                out = lambda r: POW[:, r, have + 1:2 * have + 1, :]
                ins = complex_mult(v, chn, out(0), out(1), pw(0), pw(1), by(0), by(1), *tmp)
                if have < 4:
                    chn.link(ins)
                else:
                    ins.then_inc(ssm_v, 1)
            v.wait_ge(ssm_v, 4)
            for r in range(2):
                chn.link(v.tensor_copy(AR[:, r, :], POW[:, 0, 8, :]))
            chn.link(v.tensor_copy(AI[:, 0, :], POW[:, 1, 8, :]))
            chn.link(ts(AI[:, 1, :], POW[:, 1, 8, :], -1.0, None, ALU.mult))
            chn.link(v.tensor_copy(H0[:, :, :], AC[:, 4:6, :]))
            wide = [t[:, 0:1024].rearrange("p (g m) -> p g m", m=GCH) for t in (W1, W2)]
            coef = lambda r: AC[:, 2 + r, :].unsqueeze(2).to_broadcast([P, GROUPS, GCH])
            complex_mult(v, chn, BB[:, 0], BB[:, 1], BN[:, 0], BN[:, 1], coef(0), coef(1), *wide).then_inc(ssm_v, 1)
            v.tensor_tensor(DI[:, :, :], DB[:, :].rearrange("p (g n) -> p g n", n=GCH),
                            IDENT[0:GCH, 0:GCH].unsqueeze(1).to_broadcast([GCH, GROUPS, GCH]), ALU.mult).then_inc(ssm_v, 1)
            v.wait_ge(ssm_v, 6)
            v.wait_ge(ssm_a, 15)

        def pe_ssm_start(pe):
            pe.wait_ge(ssm_in, 16 * SSM_DMAS)
            pe.wait_ge(ssm_v, 3)
            for r in range(6):
                ins = nc.tensor.transpose(PS[:, 0, GROUPS * r:GROUPS * r + GROUPS], GM[:, r].rearrange("g d p -> g (d p)"),
                                          IDENT[0:GROUPS, 0:GROUPS])
            ins.then_inc(ssm_t, 1)
            for n in range(4):
                for T in range(4):
                    ins = nc.tensor.transpose(PS[:, 4 + n, P * T:P * T + P],
                                              CN[:, n // 2, 4 * (n % 2) + T].rearrange("q d p -> q (d p)"), IDENT[:, :])
                ins.then_inc(ssm_t, 1)

        POOL_GROUPS = 6

        def inputs_powers(T, slot, part, t1, t2):
            n = part.stop - part.start
            b = [BB[:, r, bass.ds(8 * T + part.start, n), :].unsqueeze(1).to_broadcast([P, 8, n, GCH]) for r in range(2)]
            pw = [POWB[:, r, :, bass.ds(8 * T + part.start, n)].unsqueeze(3).to_broadcast([P, 8, n, GCH]) for r in range(2)]
            out = [BP[:, slot, r, part, :].rearrange("p g (t m) -> p t g m", m=GCH) for r in range(2)]
            return (*out, *b, *pw, t1, t2)

        def dve_kernels(T, slot):
            v = nc.vector
            v.wait_ge(ks_copied, 3 * T + 3)
            mid = KS[:, slot, :, 7 * GCH:8 * GCH]
            v_link(v.tensor_tensor(mid, mid, KM[:, slot], ALU.add))
            v.tensor_tensor(mid, mid, DI[:, bass.ds(8 * T, 8), :], ALU.add).then_inc(ks_ready, 1)

        def dve_prep(i, slot, first):
            v = nc.vector
            T = 2 * i + slot
            w = lambda t, k, g: t[:, 0:k * g * GCH].rearrange("p (k g n) -> p k g n", k=k, g=g)
            c = lambda r: CT[:, r, bass.ds(T, 1), :].rearrange("p a (g n) -> p (a g) n", n=GCH).unsqueeze(1).to_broadcast([P, 9, 8, GCH])
            pw = lambda r: POWC[:, r, :, bass.ds(8 * T, 8)].unsqueeze(3).to_broadcast([P, 9, 8, GCH])
            out = lambda r: G[:, slot, r].rearrange("p g k n -> p k g n")
            if not first:
                v.wait_ge(kern_ps, 16 * T - 16)
                v.wait_ge(cp_out[slot], 32 * i)
            complex_mult(v, vchain, out(0), out(1), c(0), c(1), pw(0), pw(1), w(W1, 9, 8), w(W2, 9, 8),
                         minus_bi=pw(2)).then_inc(g_ready, 1)
            v.tensor_copy(BBS[:, slot], BB[:, :, bass.ds(8 * T, 8), :]).then_inc(g_ready, 1)
            if not first:
                v.wait_ge(bt_ps, 4 * T - 4)
            v.wait_ge(g_ready, 2 * T + 2)
            complex_mult(v, vchain, *inputs_powers(T, slot, slice(POOL_GROUPS, 8), w(W1, 8, 2), w(W2, 8, 2))).then_inc(bpv_ready, 1)
            v.wait_ge(bpv_ready, T + 1)
            if not first or slot:
                dve_kernels(T - 1, 1 - slot)

        def pool_prep(T):
            g = nc.gpsimd
            if T >= 2:
                g.wait_ge(bt_ps, 4 * T - 4)
                g.wait_ge(bp_ready, T)
            complex_mult(g, pchain, *inputs_powers(T, T % 2, slice(0, POOL_GROUPS), Q1[:, :, :, :], Q2[:, :, :, :])).then_inc(bp_ready, 1)
            g.wait_ge(bp_ready, T + 1)

        def store_kernels(T, slot):
            nc.scalar.wait_ge(ks_ready, T + 1)
            nc.scalar.dma_start(K_SCR[bass.ds(8 * T, 8)].rearrange("g m n -> m g n"), KS[:, slot]).then_inc(ks_out[slot], 16)

        def act_prep(i, slot, first):
            a = nc.scalar
            T = 2 * i + slot
            a.wait_ge(g_ready, 2 * T + 2)
            for d in range(2):
                rows = slice(64 * d, 64 * d + 64)
                a.dma_start(C_SCR[bass.ds(T, 1)][:, rows].rearrange("a p (g n) -> p (a g) n", n=P),
                            G[rows, slot, :, :, 1 - d:9 - d, :].rearrange("p r g k n -> p (r g) (k n)")).then_inc(cp_out[slot], 16)
            a.wait_ge(kern_ps, 16 * T + 16)
            if not first:
                a.wait_ge(ks_out[slot], 16 * i)
            bwd, fwd = [PS[0:GCH, b:b + 2, :].rearrange("m b (g n) -> m (b g) n", n=P) for b in (4, 6)]
            a.activation(KS[:, slot, :, 0:7 * GCH], bwd[:, :, 0:7 * GCH], ACT.Copy).then_inc(ks_copied, 1)
            a.activation(KS[:, slot, :, 7 * GCH:15 * GCH], fwd, ACT.Copy).then_inc(ks_copied, 1)
            a.activation(KM[:, slot], bwd[:, :, 7 * GCH:P], ACT.Copy).then_inc(ks_copied, 1)
            if not first:
                a.wait_ge(bt_out[slot], 16 * i)
            for n in range(4):
                a.wait_ge(bt_ps, 4 * T + n + 1)
                a.activation(BTS[:, slot, 2 * n:2 * n + 2, :, :].rearrange("p g r n -> p (g r n)"), PS[:, n, :], ACT.Copy).then_inc(bt_ready, 1)
            a.wait_ge(bt_ready, 4 * T + 4)
            a.dma_start(B_SCR[bass.ds(T, 1)].rearrange("a p n -> p (a n)"),
                        BTS[:, slot].rearrange("p g r n -> p (g r n)")).then_inc(bt_out[slot], 16)
            if not first or slot:
                store_kernels(T - 1, 1 - slot)

        def pe_prep(i, slot, first):
            pe = nc.tensor
            T = 2 * i + slot
            pe.wait_ge(g_ready, 2 * T + 2)
            if not first or slot:
                pe.wait_ge(ks_copied, 3 * T)
            for g in range(8):
                for d in range(2):
                    rows = FWD if d else BWD
                    for r in range(2):
                        c0 = P * (g % 4)
                        ins = nc.tensor.matmul(PS[0:GCH, 4 + 2 * d + g // 4, c0:c0 + P], BBS[rows, slot, r, g, :],
                                               G[rows, slot, r, g, 1 - d:9 - d, :].rearrange("p k n -> p (k n)"),
                                               start=(r == 0), stop=(r == 1))
                    ins.then_inc(kern_ps, 1)
            pe.wait_ge(bp_ready, T + 1)
            pe.wait_ge(bpv_ready, T + 1)
            if not first or slot:
                pe.wait_ge(bt_ready, 4 * T)
            for n in range(4):
                for g in range(2):
                    for r in range(2):
                        ins = nc.tensor.transpose(PS[:, n, P * (2 * g + r):P * (2 * g + r) + P], BP[:, slot, r, 2 * n + g, :], IDENT[:, :])
                ins.then_inc(bt_ps, 1)

        def over_batches(eng, body, chn=None, per=0):
            for slot in range(2):
                body(0, slot, True)
            with eng.Fori(1, NB // 2) as i:
                if chn is not None:
                    chn.enter(i - 1, per)
                for slot in range(2):
                    body(i, slot, False)
                if chn is not None:
                    chn.leave(NB // 2 - 1)


        def scan_views(T, r_major=False):
            return [(FWD, slice(0, CCH), slice(1, 1 + CCH)), (FWD, slice(CCH, NCHUNK), slice(CCH + 2, CCH + 2 + LCH)),
                    (BWD, slice(0, CCH), slice(CCH, 0, -1)), (BWD, slice(CCH, NCHUNK), slice(CCH + 1 + LCH, CCH + 1, -1))]

        def entering_views():
            return [(FWD, slice(0, CCH), slice(0, CCH)), (FWD, slice(CCH, NCHUNK), slice(CCH + 1, CCH + 1 + LCH)),
                    (BWD, slice(0, CCH), slice(CCH - 1, None, -1)), (BWD, slice(CCH, NCHUNK), slice(CCH + LCH, CCH, -1))]

        def sp_ssm(sp):
            def load_bt(T):
                sp.dma_start(BT[:, T % 2].rearrange("p g r n -> p (g r n)"), B_SCR[T]).then_inc(bt_in[T % 2], 16)

            sp.wait_ge(xl_ready, 3 * KT)
            for T in range(2):
                load_bt(T)
            for m in range(KT):
                sp.wait_ge(psum_free, BASE["win"] + m + 1)
                sp.dma_start(U_SCR[P * m:P * m + P, :], UT[:, m, :]).then_inc(u_out, 16)
            for T in range(2, NB):
                sp.wait_ge(inc_ps, T - 1)
                load_bt(T)
            pool_ada(3)
            for m in range(KT):
                sp.wait_ge(y_out[m], 16 * CHUNK)
                sp.dma_start(YIN[:, m, :], U_SCR[P * m:P * m + P, :]).then_inc(y_in[m], 16)
            sp.wait_ge(fin_ready, 1)
            for r, nm in enumerate(("new_re", "new_im")):
                sp.dma_start(O[nm][0, 0].rearrange("d g p -> g d p"), FIN[:, r, :].rearrange("g (d p) -> g d p", d=2)).then_inc(fin_out, 16)

        def load_outputs_matrices(sp):
            sp.wait_ge(inc_ps, NB)
            for T in range(NB):
                if T >= 2:
                    sp.wait_ge(y_ps, T - 1)
                sp.dma_start(CPL[:, T % 2].rearrange("p r g n -> p (r g n)"), C_SCR[T]).then_inc(cp_in[T % 2], 16)
                for t in range(CHUNK):
                    src = K_SCR[8 * T:8 * T + 8].rearrange("g m n -> m g n")[:, :, GCH * (7 - t):GCH * (7 - t) + P]
                    sp.dma_start(TOEP[GCH * t:GCH * t + GCH, T % 2, :, :], src).then_inc(cp_in[T % 2], 16)

        def pe_ssm(pe):
            pe.wait_ge(u_in, 16 * CHUNK)
            pe.wait_ge(psum_free, BASE["win"] + KT)
            for T in range(NB):
                pe.wait_ge(bt_in[T % 2], 16 * (T // 2 + 1))
                if T >= 2:
                    pe.wait_ge(inc_a, 2 * T - 2)
                    pe.wait_ge(inc_v, 2 * T - 2)
                for g in range(8):
                    for r in range(2):
                        c0 = 256 * (g % 2) + P * r
                        ins = nc.tensor.matmul(PS[:, 4 * (T % 2) + g // 2, c0:c0 + NCHUNK], BT[:, T % 2, g, r, :],
                                               U8[:, 8 * T + g, :], start=True, stop=True)
                ins.then_inc(inc_ps, 1)
            pe.wait_ge(inc_a, 2 * NB)
            pe.wait_ge(inc_v, 2 * NB)
            for group in range(GROUPS_IN[2], GROUPS_IN[3]):
                pe_ada(pe, group, 7)
            pe_mods(pe, 3)
            for T in range(NB):
                if T == 3:
                    pe.wait_ge(mods_read, 4)
                pe.wait_ge(cp_in[T % 2], 16 * 9 * (T // 2 + 1))
                pe.wait_ge(ent_a, 2 * T + 2)
                pe.wait_ge(ent_v, 2 * T + 2)
                if T >= 4:
                    pe.wait_ge(y_ready, T - 3)
                for g in range(8):
                    out = PS[:, 2 * (T % 4) + g // 4, P * (g % 4):P * (g % 4) + NCHUNK]
                    nc.tensor.matmul(out, TOEP[:, T % 2, g, :], U8[:, 8 * T + g, :], start=True, stop=False)
                    for r in range(2):
                        ins = nc.tensor.matmul(out, CPL[:, T % 2, r, g, :], ENT[:, r, 8 * T + g, :], start=False, stop=(r == 1))
                ins.then_inc(y_ps, 1)
            pe.wait_ge(y_ready, NB)
            for r in range(2):
                ins = nc.tensor.transpose(PS[0:GROUPS, 0, P * r:P * r + P], FINS[:, r, :], IDENT[:, :])
            ins.then_inc(fin_ps, 1)

        def scan_inputs(engine, T, parts, done):
            engine.wait_ge(inc_ps, T + 1)
            for rows, chunks, slots in parts:
                src = PS[rows, 4 * (T % 2):4 * (T % 2) + 4, :].rearrange("p b (g r c) -> p (b g) r c", g=2, r=2)[:, :, :, chunks]
                dst = ST[rows, slots, :, 8 * T:8 * T + 8].rearrange("p c r g -> p g r c")
                if engine is nc.scalar:
                    ins = engine.activation(dst, src, ACT.Copy)
                else:
                    ins = engine.tensor_copy(dst, src)
                ins.then_inc(done, 1)

        def entering(engine, T, parts, done):
            for rows, chunks, slots in parts:
                src = ST[rows, slots, :, 8 * T:8 * T + 8].rearrange("p c r g -> p r g c")
                dst = ENT[rows, :, 8 * T:8 * T + 8, chunks]
                if engine is nc.scalar:
                    ins = engine.activation(dst, src, ACT.Copy)
                else:
                    ins = engine.tensor_copy(dst, src)
                ins.then_inc(done, 1)

        def act_ssm():
            a = nc.scalar
            a.wait_ge(u_out, 16 * KT)
            for t in range(CHUNK):
                a.dma_start(U8[GCH * t:GCH * t + GCH, :, :], U_SCR.rearrange("(g c) n -> c g n", c=GCH)
                            [:, :, NCHUNK * t:NCHUNK * t + NCHUNK]).then_inc(u_in, 16)
            for T in range(NB):
                scan_inputs(a, T, scan_views(T)[0:2], inc_a)
            for group in range(GROUPS_IN[2], GROUPS_IN[3]):
                act_rows(group, 7)
            a.wait_ge(scan_done, 1)
            for T in range(NB):
                entering(a, T, entering_views()[0:2], ent_a)
            a.wait_ge(ent_a, 2 * NB)
            a.wait_ge(ent_v, 2 * NB)
            for T in range(NB):
                a.wait_ge(y_ps, T + 1)
                a.activation(Y8[:, 8 * T:8 * T + 8, :], PSF[:, 1024 * (T % 4):1024 * (T % 4) + 1024]
                             .rearrange("p (g c) -> p g c", g=8)[:, :, 0:NCHUNK], ACT.Copy).then_inc(y_ready, 1)
                a.wait_ge(y_ready, T + 1)
                for t in range(CHUNK):
                    a.dma_start(U_SCR[P * T:P * T + P, :].rearrange("(g c) n -> c g n", c=GCH)
                                [:, :, NCHUNK * t:NCHUNK * t + NCHUNK],
                                Y8[GCH * t:GCH * t + GCH, 8 * T:8 * T + 8, :]).then_inc(y_out[T], 16)
            a.wait_ge(fin_ps, 1)
            a.activation(FIN[:, :, :].rearrange("g r n -> g (r n)"), PS[0:GROUPS, 0, 0:2 * P], ACT.Copy).then_inc(fin_ready, 1)
            for m in range(KT):
                a.wait_ge(y_in[m], 16)
                a.activation(YIN[:, m, :], YIN[:, m, :], ACT.Gelu_apprx_tanh).then_inc(gelu_done, 1)
                a.wait_ge(gelu_done, m + 1)
                a.activation(XH[:, m, :], YIN[:, m, :], ACT.Copy).then_inc(gelu_hi, 1)

        def dve_ssm():
            v = nc.vector
            v.wait_ge(u_out, 16 * KT)
            v_link(v.memset(ST[:, 0, :, :], 0.0))
            v_link(v.tensor_copy(ST[:, CCH + 1, :, :], H0[:, :, :]))
            for T in range(NB):
                scan_inputs(v, T, scan_views(T)[2:4], inc_v)
            v.wait_ge(inc_a, 2 * NB)
            v.wait_ge(inc_v, 2 * NB)

            both = ST[:, 0:2 * (CCH + 1)].rearrange("p (a s) r g -> p a s (r g)", s=CCH + 1)

            def run(trips, first, n, count0):
                with v.Fori(0, trips) as i:
                    for u in range(UN):
                        c = count0 + 4 * UN * i + 4 * u
                        s = first + UN * i + u
                        if n == 2:
                            last = both[:, :, bass.ds(s - 1, 1), :].rearrange("p a s (r g) -> p (a s) r g", r=2)
                            now = both[:, :, bass.ds(s, 1), :].rearrange("p a s (r g) -> p (a s) r g", r=2)
                        else:
                            last, now = ST[:, bass.ds(s - 1, 1)], ST[:, bass.ds(s, 1)]
                        shape = [P, n, 2, GROUPS]
                        ar = AR[:, :, :].unsqueeze(1).to_broadcast(shape)
                        ai = AI[:, :, :].unsqueeze(1).to_broadcast(shape)
                        t1, t2 = SC1[:, 0:n], SC2[:, 0:n]
                        v.tensor_tensor(t1, last, ar, ALU.mult).then_inc(scan_t, 1)
                        v.tensor_tensor(t2[:, :, ::-1, :], last, ai, ALU.mult).then_inc(scan_t, 1)
                        v.wait_ge(scan_t, c + 1)
                        v.tensor_tensor(now, now, t1, ALU.add).then_inc(scan_t, 1)
                        v.wait_ge(scan_t, c + 3)
                        v.tensor_tensor(now, now, t2, ALU.add).then_inc(scan_t, 1)
                        v.wait_ge(scan_t, c + 4)
                return count0 + 4 * UN * trips

            UN = 4
            c = run(CCH // UN, 1, 2, 0)
            run((LCH - CCH) // UN, 2 * CCH + 2, 1, c)
            v.tensor_copy(FINS[:, :, :], ST[:, CCH, :, :]).then_inc(scan_done, 1)
            for T in range(NB):
                entering(v, T, entering_views()[2:4], ent_v)
            dve_mods(3)
            for m in range(KT):
                v.wait_ge(gelu_hi, m + 1)
                v.tensor_tensor(XL[:, m, :], YIN[:, m, :], XH[:, m, :].bitcast(F32), ALU.subtract).then_inc(gelu_lo, 1)

        def XBANK(k):
            return 4 + 2 * (k % 2)

        def act_out(a):
            for b in range(5):
                a.wait_ge(out_t, 2 * b + 1)
                if b >= 2:
                    a.wait_ge(out_dma[b % 2], 16 * (b // 2))
                a.activation(OUTN[:, b % 2, 0:512], PS[:, 2 * (b % 4), :], ACT.Copy).then_inc(out_a, 1)

        def dve_out(v):
            for b in range(5):
                v.wait_ge(out_t, 2 * b + 2)
                if b >= 2:
                    v.wait_ge(out_dma[b % 2], 16 * (b // 2))
                nc.vector.tensor_copy(OUTN[:, b % 2, 512:1024], PS[:, 2 * (b % 4) + 1, :]).then_inc(out_v, 1)

        def pe_out(pe, q):
            pe.wait_ge(ln_x, KT * q + KT)
            for b in range(5):
                if b >= 4:
                    pe.wait_ge(out_a, b - 3)
                    pe.wait_ge(out_v, b - 3)
                for k in range(KT):
                    ins = nc.tensor.transpose(PS[:, 2 * (b % 4) + k // 4, P * (k % 4):P * (k % 4) + P],
                                              X[:, k, P * b:P * b + P], IDENT[:, :])
                    if k % 4 == 3:
                        ins.then_inc(out_t, 1)

        block = ctx.enter_context(nc.Block())

        @block.sync
        def _(sp):
            rows = [(0, 0, I["b_ada"].rearrange("l (q p) -> (l q) p", p=P)),
                    (0, 96, I["ln_g"].rearrange("l i (k p) -> (l i k) p", p=P)),
                    (1, 0, I["ln_b"].rearrange("l i (k p) -> (l i k) p", p=P)),
                    (1, 32, I["c_ctx"].rearrange("(k p) -> k p", p=P)),
                    (1, 40, I["c"].rearrange("b (k p) -> (b k) p", p=P)),
                    (1, 48, I["ssm_d"].rearrange("b (k p) -> (b k) p", p=P))]
            for t, r, src in rows:
                sp.dma_start(SV[r:r + src.shape[0], t, :], src).then_inc(small_in, 16)
            sp.dma_start(IDENT[:, :], I["k_ident"]).then_inc(const_in, 16)
            load_ada(sp, 0, ADA_FIRST, dense=0)
            load_turn(sp, "qkv", 0, after_ada=ADA_FIRST)
            load_turn(sp, "qkv", 1)
            load_turn(sp, "qkv", 2)
            load_turn(sp, "wo", 0)
            load_ada(sp, ADA_FIRST, MODQ - ADA_FIRST, dense=ADA_SECOND_AT)
            load_ada(sp, MODQ, ADA_SECOND - MODQ)
            load_turn(sp, "wo", 1, after_ada=ADA_SECOND)
            for name, _n in STAGES[2:]:
                if name == "glu":
                    load_turn(sp, name, 0)
                    load_ada(sp, ADA_SECOND, ADA - ADA_SECOND, dense=ADA_THIRD_AT)
                    load_outputs_matrices(sp)
                    for i in range(1, COUNT[name] // SLOTS):
                        load_turn(sp, name, i, after_ada=ADA if i == 1 else 0)
                else:
                    load_stage(sp, name)
            for b in range(5):
                sp.wait_ge(out_a, b + 1)
                sp.wait_ge(out_v, b + 1)
                dst = O["y_prompt"][0] if b == 0 else O["y_sample"][0][P * (b - 1):P * b, :]
                sp.dma_start(dst, OUTN[:, b % 2, :]).then_inc(out_dma[b % 2], 16)
            sp.wait_ge(out_dma[0], 48)
            sp.wait_ge(out_dma[1], 32)
            sp.wait_ge(kv_out, 32)

        @block.scalar
        def _(a):
            for b in range(5):
                src = I["x_prompt"][0] if b == 0 else I["x_sample"][0][P * (b - 1):P * b, :]
                a.dma_start(XN[:, b, :], src).then_inc(x_in, 16)
            for n in range(4):
                a.dma_start(MASK[:, n, :], I["k_masks"][n]).then_inc(attn_in, 16)
            a.dma_start(ROPE[:, 0, :], I["k_rope"][0]).then_inc(attn_in, 16)
            a.dma_start(ROPE[:, 1, :], I["k_rope"][1]).then_inc(attn_in, 16)
            a.dma_start(CK[:, :], I["cache_k"][0, 0].rearrange("s h d -> s (h d)")).then_inc(attn_in, 16)
            a.dma_start(CV[:, :], I["cache_v"][0, 0].rearrange("s h d -> s (h d)")).then_inc(attn_in, 16)
            a.dma_start(SINK[:, :], I["attn_sink"][0:1, :].to_broadcast([P, HEADS])).then_inc(sink_in, 16)
            a.wait_ge(sv_t, 1)
            a.activation(PV1[:, :], PS[:, 0, 0:P], ACT.Copy).then_inc(pv_ready, 1)
            a.activation(PV2[:, :], PS[:, 1, 0:56], ACT.Copy).then_inc(pv_ready, 1)
            a.wait_ge(pv_ready, 2)
            a.activation(SC[:, :, :].rearrange("p k s -> p s k"), PV2[:, 32:48].rearrange("p (s k) -> p s k", s=2), ACT.Silu).then_inc(silu_c, 1)
            for k in range(KT):
                a.wait_ge(x_t, k + 1)
                a.activation(X[:, k, :], PSF[:, XBANK(k) * 512:XBANK(k) * 512 + TOK], ACT.Copy).then_inc(x_ready, 1)
            for group in range(GROUPS_IN[0]):
                act_rows(group, 3)
            for u in range(SLOTS):
                split_hi(u, u, first=True, ada=ADA_FIRST)
            for k in range(KT):
                act_high(0, k)
            act_split_only("qkv")
            act_attention_start()
            act_attention()
            act_split_only("wo")
            a.wait_ge(kv_out, 32)
            act_norm_modulate(0, 1)
            for ph in range(3):
                act_gated(f"up0{ph}", ACT.Silu, 0)
                act_split_only(f"down0{ph}")
            if LAYERS == 2:
                act_ssm_start()
                over_batches(a, act_prep)
                store_kernels(NB - 1, 1)
                act_norm_modulate(1, 2)
                act_split_only("win")
                act_ssm()
                act_gated("glu", ACT.Sigmoid, 0)
                act_split_only("wout")
                act_norm_modulate(2, 3)
                for ph in range(3):
                    act_gated(f"up1{ph}", ACT.Silu, 0)
                    act_split_only(f"down1{ph}")
            last = 2 * LAYERS - 1
            act_norm(last)
            for k in range(KT):
                act_norm_shift(last, k)
            act_out(a)

        @block.vector
        def _(v):
            nc.vector.memset(MEANW[:, :], 1.0 / D).then_inc(memset_done, 1)
            nc.vector.memset(EPS[:, :], LN_EPS / ALPHA ** 2).then_inc(memset_done, 1)
            v.wait_ge(pv_ready, 2)
            dve_mods(0)
            for u in range(SLOTS):
                split_lo(u, u)
            dve_modulate(0, 0, 0, lambda k: nc.vector.wait_ge(x_ready, k + 1))
            dve_store("qkv", QKVT)
            dve_attention_start()
            dve_attention()
            dve_mods(1)
            dve_mods(2)
            dve_residual("wo", 0, 2)
            v.wait_ge(kv_out, 32)
            dve_norm_modulate(0, 1, 0, 3)
            for ph in range(3):
                dve_gated(f"up0{ph}", PAIRS_BEFORE[f"up0{ph}"])
                dve_residual(f"down0{ph}", 0, 5)
            if LAYERS == 2:
                dve_ssm_start()
                over_batches(v, dve_prep, vchain, 22)
                dve_kernels(NB - 1, 1)
                for u in range(2):
                    v.wait_ge(cp_out[u], 16 * NB)
                    v.wait_ge(bt_out[u], 8 * NB)
                    v.wait_ge(ks_out[u], 8 * NB)
                dve_norm_modulate(1, 2, 1, 0)
                dve_store("win", UT)
                dve_ssm()
                dve_gated("glu", PAIRS_BEFORE["glu"])
                dve_residual("wout", 1, 2)
                dve_norm_modulate(2, 3, 1, 3)
                for ph in range(3):
                    dve_gated(f"up1{ph}", PAIRS_BEFORE[f"up1{ph}"])
                    dve_residual(f"down1{ph}", 1, 5)
            last = 2 * LAYERS - 1
            dve_norm(last)
            for k in range(KT):
                dve_norm_scale(last, k)
            dve_out(v)

        @block.gpsimd
        def _(g):
            pool_ada(0)
            g.wait_ge(att_kv, 4)
            g.dma_start(O["new_k"][0, 0].rearrange("s h d -> s (h d)"), KN[:, :]).then_inc(kv_out, 16)
            g.dma_start(O["new_v"][0, 0].rearrange("s h d -> s (h d)"), VN[:, 0, :]).then_inc(kv_out, 16)
            pool_ada(1)
            pool_ada(2)
            if LAYERS == 2:
                sp_ssm_start(g)
                g.wait_ge(ssm_v, 5)
                g.wait_ge(ssm_a, 11)
                g.wait_ge(ssm_t, 5)

                for T in range(NB):
                    pool_prep(T)
                sp_ssm(g)
                g.wait_ge(fin_out, 32)

        @block.tensor
        def _(pe):
            pe.wait_ge(small_in, 96)
            pe.wait_ge(const_in, 16)
            nc.tensor.transpose(PS[:, 0, 0:P], SV[:, 0, :], IDENT[:, :])
            nc.tensor.transpose(PS[:, 1, 0:56], SV[0:56, 1, :], IDENT[0:56, 0:56]).then_inc(sv_t, 1)
            pe.wait_ge(x_in, 80)
            for k in range(KT):
                if k >= 2:
                    pe.wait_ge(x_ready, k - 1)
                for b in range(5):
                    ins = nc.tensor.transpose(PSF[:, XBANK(k) * 512 + P * b:XBANK(k) * 512 + P * b + P],
                                              XN[:, b, P * k:P * k + P], IDENT[:, :])
                ins.then_inc(x_t, 1)
            pe.wait_ge(x_ready, KT)
            pe.wait_ge(silu_c, 1)
            for group in range(GROUPS_IN[0]):
                pe_ada(pe, group, 3)
            pe_mods(pe, 0)
            pe.wait_ge(xl_ready, KT)
            pe_stage(pe, "qkv", XH, XL)
            pe_attention_start(pe)
            pe_attention(pe)
            pe.wait_ge(att_ol, 20)
            pe_mods(pe, 1)
            pe_mods(pe, 2)
            pe.wait_ge(mods_read, 3)
            pe_stage(pe, "wo", XH, XL)
            pe_norm(pe, 0)
            pe.wait_ge(xl_ready, 2 * KT)
            for ph in range(3):
                pe_stage(pe, f"up0{ph}", XH, XL)
                pe.wait_ge(hid_lo, PAIRS_BEFORE[f"up0{ph}"] + PHASES[ph][1])
                pe_stage(pe, f"down0{ph}", HH, HL, PHASES[ph][1])
            if LAYERS == 2:
                pe_ssm_start(pe)
                for T in range(NB):
                    pe_prep(T // 2, T % 2, T < 2)
                pe_norm(pe, 1)
                pe.wait_ge(xl_ready, 3 * KT)
                pe_stage(pe, "win", XH, XL)
                pe_ssm(pe)
                pe.wait_ge(gelu_lo, KT)
                pe_stage(pe, "glu", XH, XL)
                pe.wait_ge(hid_lo, PAIRS_BEFORE["glu"] + 8)
                pe_stage(pe, "wout", HH, HL)
                pe_norm(pe, 2)
                pe.wait_ge(xl_ready, 4 * KT)
                for ph in range(3):
                    pe_stage(pe, f"up1{ph}", XH, XL)
                    pe.wait_ge(hid_lo, PAIRS_BEFORE[f"up1{ph}"] + PHASES[ph][1])
                    pe_stage(pe, f"down1{ph}", HH, HL, PHASES[ph][1])
            pe_norm(pe, 2 * LAYERS - 1)
            pe_out(pe, 2 * LAYERS - 1)


OUTPUTS = {"y_prompt": (1, CTX, D), "y_sample": (1, LAT, D), "new_k": (1, 1, CTX, KV_HEADS, HD),
           "new_v": (1, 1, CTX, KV_HEADS, HD), "new_re": (1, 1, 2, GROUPS, STATE), "new_im": (1, 1, 2, GROUPS, STATE)}


def kernel(**inputs):
    import concourse.bacc as bacc
    from concourse.bass_utils import run_bass_kernel_spmd

    nc = bacc.Bacc("TRN2", target_bir_lowering=False, num_devices=1)
    arrays = {n: np.ascontiguousarray(a) for n, a in inputs.items()}
    arrays.update(host_constants())
    handles = {n: nc.dram_tensor("in_" + n, a.shape, mybir.dt.from_np(a.dtype), kind="ExternalInput").ap()
               for n, a in arrays.items()}
    outs = {n: nc.dram_tensor("out_" + n, s, F32, kind="ExternalOutput").ap() for n, s in OUTPUTS.items()}
    hybrid_step(nc, handles, outs)
    r = run_bass_kernel_spmd(nc, [{"in_" + n: a for n, a in arrays.items()}], core_ids=[0])
    return tuple(r.results[0]["out_" + n] for n in OUTPUTS)
```

```python
from contextlib import ExitStack, nullcontext

import numpy as np

import concourse.bass as bass
from concourse import mybir

ACT = mybir.ActivationFunctionType
ALU = mybir.AluOpType
F32 = mybir.dt.float32
F32R = mybir.dt.float32r

P = 128
D = 1024
KT = D // P
CTX = 128
LAT = 512
TOK = CTX + LAT
HALF = TOK // 2
FF = 2816
HEADS = 16
KV_HEADS = 4
HD = 64
GROUPS = 64
GCH = 16
STATE = 64
CHUNK = 8
NCHUNK = TOK // CHUNK
CCH = CTX // CHUNK
LCH = LAT // CHUNK
ALPHA = 4.0 ** 0.25
LN_EPS = 1e-5
SCALE = HD ** -0.5
NEG = -1e30
SLOTS = 4
MODQ = 6 * KT

PHASES = [(0, 8), (8, 8), (16, 6)]
assert sum(_n for _, _n in PHASES) * P == FF
STAGES = [("qkv", 12), ("wo", 8)]
for _ph, (_f0, _n) in enumerate(PHASES):
    STAGES += [(f"up0{_ph}", 2 * _n), (f"down0{_ph}", 8)]
STAGES += [("win", 8), ("glu", 16), ("wout", 8)]
for _ph, (_f0, _n) in enumerate(PHASES):
    STAGES += [(f"up1{_ph}", 2 * _n), (f"down1{_ph}", 8)]
BASE, COUNT = {}, {}
_at = 0
for _name, _n in STAGES:
    BASE[_name], COUNT[_name] = _at, _n
    _at += _n
PANELS = _at
ADA = 2 * MODQ
ADA_FIRST, ADA_SECOND = 2 * KT, MODQ + 2 * KT
ADA_SECOND_AT, ADA_THIRD_AT = BASE["wo"] + SLOTS, BASE["glu"] + SLOTS


def ada_before(name):
    return ADA_FIRST if name == "qkv" else ADA_SECOND if BASE[name] < BASE["glu"] else ADA


PAIRS_BEFORE, _at = {}, 0
for _name, _n in STAGES:
    PAIRS_BEFORE[_name] = _at
    if _name.startswith("up") or _name == "glu":
        _at += _n // 2


def host_constants():
    ident = np.eye(P, dtype=np.float32)
    masks = np.zeros((4, P, 4 * P), np.float32)
    q = np.arange(P)[:, None]
    k = np.arange(P)[None, :]
    masks[:, :, P:2 * P] = np.where(k >= q, 0.0, NEG)
    masks[:, :, 3 * P:] = np.where(k <= q, 0.0, NEG)
    masks[0, :, P:2 * P] = NEG
    masks[3, :, 3 * P:] = NEG
    t = np.arange(LAT)
    nf = HD // 4
    inv = np.power(np.float32(10000.0), -np.arange(nf, dtype=np.float32) / np.float32(nf)).astype(np.float32)
    ang = np.stack([(t // 64).astype(np.float32)[:, None] * inv, (t % 64).astype(np.float32)[:, None] * inv])
    rope = np.zeros((2, P, LAT), np.float32)
    for p in range(P):
        axis, half, f = (p % HD) // 32, (p % 32) // 16, p % 16
        rope[0, p] = np.cos(ang[axis, :, f])
        rope[1, p] = np.sin(ang[axis, :, f]) * (1.0 if half else -1.0)
    return {"k_ident": ident, "k_masks": masks, "k_rope": rope}


class Chain:

    def __init__(self, eng, sem):
        self.eng, self.sem, self.n, self.i, self.per = eng, sem, 0, None, 0

    def value(self):
        return self.n if self.i is None else self.n + self.i * self.per

    def link(self, ins):
        self.n += 1
        ins.then_inc(self.sem, 1)
        self.eng.wait_ge(self.sem, self.value())

    def enter(self, i, per):
        self.i, self.per, self.start = i, per, self.n

    def leave(self, trips):
        assert self.n - self.start == self.per, (self.n - self.start, self.per)
        self.n, self.i = self.start + self.per * trips, None


def hybrid_step(nc, I, O):
    ctx = ExitStack()
    with ctx:
        def psum(name, shape):
            return ctx.enter_context(nc.psum_tensor(name, shape, F32))

        def sem(name):
            return ctx.enter_context(nc.semaphore(name))

        top = [((nc.sbuf_base + 63) // 64) * 64]

        def place(name, shape, dt=F32, at=None):
            size = int(np.prod(shape[1:])) * 4
            size = (size + 31) // 32 * 32
            where = top[0] if at is None else at
            t = nc.alloc_sbuf_tensor_at(name, shape, dt, offset=where)
            if at is None:
                top[0] += size
            return t, where + size

        def sb(name, shape, dt=F32):
            return place(name, shape, dt)[0]

        X = sb("X", [P, KT, TOK])
        RAW = sb("RAW", [P, SLOTS, KT, P])
        WH = sb("WH", [P, SLOTS, KT, P], F32R)
        WL = sb("WL", [P, SLOTS, KT, P], F32R)
        IDENT = sb("IDENT", [P, P])
        MEANW = sb("MEANW", [P, P])
        EPS = sb("EPS", [P, 1])
        PV1 = sb("PV1", [P, P])
        PV2 = sb("PV2", [P, 56])
        MODS = sb("MODS", [P, 2, MODQ, 2])
        SC = sb("SC", [P, KT, 2])
        ROWS = sb("ROWS", [2, 2, SLOTS * P])
        MT = sb("MT", [2 * MODQ, 2, P])
        XH = sb("XH", [P, KT, TOK], F32R)
        XL = sb("XL", [P, KT, TOK], F32R)
        AR, AI = sb("AR", [P, 2, GROUPS]), sb("AI", [P, 2, GROUPS])
        H0, FINS = sb("H0", [P, 2, GROUPS]), sb("FINS", [P, 2, GROUPS])
        common_end = top[0]
        HH, e = place("HH", [P, KT, TOK], F32R, at=common_end)
        HL, e = place("HL", [P, KT, TOK], F32R, at=e)
        GT, e = place("GT", [P, 2, TOK], at=e)
        HT, ffn_end = place("HT", [P, 2, TOK], at=e)
        ACC, _e = place("ACC", [P, TOK], at=nc.sbuf_usable_end // 32 * 32 - 4 * TOK)
        SQ, e = place("SQ", [P, 2, TOK], at=common_end)
        YT, e = place("YT", [P, 2, TOK], at=e)
        XM, e = place("XM", [P, 2, TOK], at=e)
        RSTD, e = place("RSTD", [P, TOK], at=e)
        RT, e = place("RT", [P, TOK], at=e)
        STD, ln_end = place("STD", [P, TOK], at=e)
        XN, e = place("XN", [P, 5, D], at=ln_end)
        SV, e = place("SV", [P, 2, P], at=e)
        QKVT, e = place("QKVT", [P, 12, TOK], at=common_end)
        VN, e = place("VN", [P, 7, 2 * P], at=e)
        KR, e = place("KR", [P, 2, LAT + 2 * P], at=e)
        KCT, e = place("KCT", [P, 2, P], at=e)
        QR, e = place("QR", [P, 2, 4, P], at=e)
        S, e = place("S", [P, 8, 4 * P], at=e)
        PT, e = place("PT", [P, 4, 4, P], at=e)
        MASK, e = place("MASK", [P, 4, 4 * P], at=e)
        ROPE, e = place("ROPE", [P, 2, LAT], at=e)
        SWAP, e = place("SWAP", [P, LAT], at=e)
        CK, e = place("CK", [P, 2 * P], at=e)
        CV, e = place("CV", [P, 2 * P], at=e)
        KN, e = place("KN", [P, 2 * P], at=e)
        SINK, e = place("SINK", [P, HEADS], at=e)
        STAT, e = place("STAT", [P, 8, 8], at=e)
        xh_at = common_end - 4 * 512 - 2 * KT * TOK * 4
        G, e = place("G", [P, 2, 2, 8, 9, GCH], at=xh_at)
        BTS, e = place("BTS", [P, 2, 8, 2, P], at=e)
        BBS, e = place("BBS", [P, 2, 2, 8, GCH], at=e)
        assert e <= common_end - 4 * 512
        Q1, e = place("Q1", [P, 8, 6, GCH], at=e)
        assert e <= common_end - 4 * 512
        acc_at = nc.sbuf_usable_end // 32 * 32 - 4 * TOK
        early = acc_at - 4 * (4 * GROUPS * GCH) - 4 * (4 * STATE + 8 * P + 12 * STATE + 8 + D)
        assert early >= ffn_end
        LAM, e = place("LAM", [GROUPS, 2, 2, STATE], at=early)
        ZR, e = place("ZR", [GROUPS, P], at=e)
        ZI, e = place("ZI", [GROUPS, P], at=e)
        MAG, e = place("MAG", [GROUPS, P], at=e)
        SIN, e = place("SIN", [GROUPS, P], at=e)
        SINH, e = place("SINH", [GROUPS, P], at=e)
        T1, e = place("T1", [GROUPS, P], at=e)
        T2, e = place("T2", [GROUPS, P], at=e)
        T3, scratch_end = place("T3", [GROUPS, P], at=e)
        GM, e = place("GM", [GROUPS, 6, 2, STATE], at=scratch_end)
        LDT, e = place("LDT", [GROUPS, 2], at=e)
        DB, e = place("DB", [GCH, D], at=e)
        BN, e = place("BN", [P, 2, GROUPS, GCH], at=e)
        CN, _e = place("CN", [P, 2, KT, 2, STATE], at=e)
        BP, e = place("BP", [P, 2, 2, 8, P], at=e - 4 * 2 * GROUPS * GCH)
        assert e <= acc_at
        KS, e = place("KS", [GCH, 2, 8, 15 * GCH], at=common_end)
        KM, e = place("KM", [GCH, 2, 8, GCH], at=e)
        Q2, e = place("Q2", [P, 8, 6, GCH], at=e)
        AC, e = place("AC", [P, 6, GROUPS], at=e)
        CT, e = place("CT", [P, 2, KT, P], at=e)
        POW, e = place("POW", [P, 2, 9, GROUPS], at=e)
        POWB, e = place("POWB", [P, 2, 8, GROUPS], at=e)
        POWC, e = place("POWC", [P, 3, 9, GROUPS], at=e)
        BB, e = place("BB", [P, 2, GROUPS, GCH], at=e)
        DI, e = place("DI", [GCH, GROUPS, GCH], at=e)
        W1, e = place("W1", [P, 9 * P], at=e)
        W2, e = place("W2", [P, 9 * P], at=e)
        assert e <= scratch_end, (e, scratch_end)
        SSM_DMAS = 15
        ENT, e = place("ENT", [P, 2, GROUPS, NCHUNK], at=xh_at)
        U8, e = place("U8", [P, GROUPS, NCHUNK], at=common_end)
        ST, st_end = place("ST", [P, TOK // CHUNK + 2, 2, GROUPS], at=common_end + 4 * KT * TOK)
        UT, _e = place("UT", [P, KT, TOK], at=common_end + 4 * KT * TOK)
        YC, e = place("YC", [NCHUNK, 2, CHUNK, P], at=common_end + 4 * KT * TOK)
        YIN, e = place("YIN", [P, KT, TOK], at=e)
        assert e <= st_end
        BT, _e = place("BT", [P, 2, 8, 2, P], at=st_end)
        CPL, e = place("CPL", [P, 2, 2, 8, P], at=st_end)
        TOEP, e = place("TOEP", [P, 2, 8, P], at=e)
        SC1, e = place("SC1", [P, 2, 2, GROUPS], at=e)
        SC2, e = place("SC2", [P, 2, 2, GROUPS], at=e)
        FIN, e = place("FIN", [GROUPS, 2, P], at=e)
        assert e <= nc.sbuf_usable_end, (e, nc.sbuf_usable_end)
        B_SCR = nc.dram_tensor("b_scratch", (KT, P, 16 * P), F32, kind="Internal").ap()
        C_SCR = nc.dram_tensor("c_scratch", (KT, P, 16 * P), F32, kind="Internal").ap()
        M_SCR = nc.dram_tensor("m_scratch", (2, 2, MODQ * P), F32, kind="Internal").ap()
        K_SCR = nc.dram_tensor("k_scratch", (GROUPS, GCH, 15 * GCH), F32, kind="Internal").ap()
        U_SCR = nc.dram_tensor("u_scratch", (D, TOK), F32, kind="Internal").ap()
        OUTN, _e = place("OUTN", [P, 2, D], at=common_end)
        assert e <= nc.sbuf_usable_end, (e, nc.sbuf_usable_end)

        PS = psum("PS", [P, 8, 512])
        PSF = PS[:, :, :].rearrange("p b n -> p (b n)")

        def halves(bank):
            return PS[:, bank:bank + 2, 0:HALF]

        def by_half(ap):
            return ap.rearrange("p (h t) -> p h t", h=2)

        raw_in = [sem(f"raw_in{u}") for u in range(SLOTS)]
        hi_ready = sem("hi_ready")
        lo_ready = sem("lo_ready")
        pe_done = sem("pe_done")
        psum_free = sem("psum_free")
        silu_done = sem("silu_done")
        hid_hi = sem("hid_hi")
        hid_lo = sem("hid_lo")
        dve_chain = sem("dve_chain")
        pool_chain = sem("pool_chain")
        sink_in = sem("sink_in")
        small_in = sem("small_in")
        const_in = sem("const_in")
        x_in = sem("x_in")
        attn_in = sem("attn_in")
        memset_done = sem("memset_done")
        sv_t = sem("sv_t")
        pv_ready = sem("pv_ready")
        silu_c = sem("silu_c")
        rows_read = sem("rows_read")
        rows_out = [sem(f"rows_out{u}") for u in range(2)]
        rows_t = sem("rows_t")
        mt_in = sem("mt_in")
        mods_ps = sem("mods_ps")
        mods_read = sem("mods_read")
        ada_done = sem("ada_done")
        x_t = sem("x_t")
        x_ready = sem("x_ready")
        xm_ready = sem("xm_ready")
        xh_ready = sem("xh_ready")
        xl_ready = sem("xl_ready")
        ln_sum, ln_mean, ln_cent = sem("ln_sum"), sem("ln_mean"), sem("ln_cent")
        ln_sq, ln_sqsum, ln_std = sem("ln_sq"), sem("ln_sqsum"), sem("ln_std")
        ln_y, ln_x = sem("ln_y"), sem("ln_x")
        out_t, out_a, out_v = sem("out_t"), sem("out_a"), sem("out_v")
        out_dma = [sem(f"out_dma{u}") for u in range(2)]
        kv_out = sem("kv_out")
        (att_t, att_kv, att_qrot, att_s, att_max, att_stat, att_exp, att_p, att_tr, att_pt,
         att_pv, att_oh, att_ol) = [sem("att_" + x) for x in (
             "t", "kv", "qrot", "s", "max", "stat", "exp", "p", "tr", "pt", "pv", "oh", "ol")]
        ATTN_DMAS = 8
        (ssm_in, ssm_a, ssm_v, ssm_t, g_ready, kern_ps, ks_copied, ks_ready, bp_ready, bpv_ready, bt_ps, bt_ready,
         inc_ps, inc_a, inc_v, scan_t, scan_done, ent_a, ent_v, y_ps, y_ready, yt_ps, fin_ps,
         fin_ready, fin_out, gelu_done, gelu_hi, gelu_lo) = [sem("s5_" + x) for x in (
             "in", "a", "v", "t", "g", "kern_ps", "ks_copied", "ks", "bp", "bpv", "bt_ps", "bt",
             "inc_ps", "inc_a", "inc_v", "scan_t", "scan", "ent_a", "ent_v", "y_ps", "y", "yt_ps",
             "fin_ps", "fin", "fin_out", "gelu", "gelu_hi", "gelu_lo")]
        cp_out, bt_out, ks_out = [[sem(f"s5_{x}_out{u}") for u in range(2)] for x in ("cp", "bt", "ks")]
        u_out, u_in = [[sem(f"s5_u_{x}{half}") for half in range(2)] for x in ("out", "in")]
        bt_in = [sem(f"s5_bt_in{u}") for u in range(2)]
        cp_in = [sem(f"s5_cp_in{u}") for u in range(2)]
        pchain = Chain(nc.gpsimd, pool_chain)

        def loop(eng, trips):
            return eng.Fori(0, trips) if trips > 1 else nullcontext(0)

        def panel_parts(name, i, u):
            full = RAW[:, u, :, :]
            if name == "qkv":
                w = I["w_qkv"][0].rearrange("(k p) n -> p k n", p=P)
                if isinstance(i, int) and i == 2:
                    return [(full, w[:, :, D + P * u:D + P * u + P])]
                return [(RAW[:, u, :, HD * h:HD * h + HD], w[:, :, bass.ds(512 * i + 256 * h + HD * u, HD)])
                        for h in range(2)]
            if name == "wo":
                w = I["w_o"][0].rearrange("(b h j d) n -> b h d j n", b=2, h=2, j=4)
                return [(RAW[HD * h:HD * h + HD, u, 4 * b:4 * b + 4, :], w[b, h][:, :, bass.ds(512 * i + P * u, P)])
                        for b in range(2) for h in range(2)]
            if name.startswith("up"):
                layer, ph = int(name[2]), int(name[3])
                w = I["ffn_w1" if u % 2 == 0 else "ffn_w3"][layer].rearrange("(k p) n -> p k n", p=P)
                return [(full, w[:, :, bass.ds(PHASES[ph][0] * P + 256 * i + P * (u // 2), P)])]
            if name.startswith("down"):
                layer, ph = int(name[4]), int(name[5])
                f0, n = PHASES[ph]
                w = I["ffn_w2"][layer].rearrange("(k p) n -> p k n", p=P)
                return [(RAW[:, u, 0:n, :], w[:, f0:f0 + n, bass.ds(512 * i + P * u, P)])]
            if name == "glu":
                w = I["ssm_w_glu"][0].rearrange("(k p) (v c n) -> p k v c n", p=P, v=2, n=P)
                src = w[:, :, 1 - u % 2, bass.ds(2 * i + u // 2, 1), :]
                return [(full, src.rearrange("p k a n -> p k (a n)"))]
            w = I["ssm_w_in" if name == "win" else "ssm_w_out"][0].rearrange("(k p) n -> p k n", p=P)
            return [(full, w[:, :, bass.ds(512 * i + P * u, P)])]

        def load_turn(sp, name, i, first=False, after_ada=0):
            for u in range(SLOTS):
                n = BASE[name] + SLOTS * i + u
                if after_ada:
                    sp.wait_ge(ada_done, after_ada - SLOTS + 1 + u)
                elif not first:
                    sp.wait_ge(hi_ready, n - SLOTS + 1)
                    sp.wait_ge(lo_ready, n - SLOTS + 1)
                parts = panel_parts(name, i, u)
                for dst, src in parts:
                    sp.dma_start(dst, src).then_inc(raw_in[u], 64 // len(parts))

        def load_stage(sp, name):
            with loop(sp, COUNT[name] // SLOTS) as i:
                load_turn(sp, name, i)

        def load_ada(sp, first, count, dense=None):
            layer, col = divmod(first, MODQ)
            w = I["w_ada"][layer].rearrange("(u k p) n -> u p k n", p=P, u=SLOTS)

            def body(i, peeled=False):
                for u in range(SLOTS):
                    if not peeled:
                        sp.wait_ge(ada_done, first + SLOTS * i + u - SLOTS + 1)
                    elif dense:
                        sp.wait_ge(hi_ready, dense - SLOTS + 1 + u)
                        sp.wait_ge(lo_ready, dense - SLOTS + 1 + u)
                    src = w[u][:, :, bass.ds(SLOTS * P * i + P * col, SLOTS * P)]
                    sp.dma_start(RAW[:, u].rearrange("p k m -> p (k m)").rearrange("p (k n) -> p k n", k=2), src
                                 ).then_inc(raw_in[u], 64)

            if dense is None:
                with sp.Fori(0, count // SLOTS) as i:
                    body(i)
            else:
                body(0, peeled=True)
                with sp.Fori(1, count // SLOTS) as i:
                    body(i)

        def split_hi(n, u, ada, first=False):
            nc.scalar.wait_ge(raw_in[u], (n - u) * 16 + 64 + ada * 16)
            if not first:
                nc.scalar.wait_ge(pe_done, n - SLOTS + 1)
            nc.scalar.activation(WH[:, u], RAW[:, u], ACT.Copy).then_inc(hi_ready, 1)

        def split_lo(n, u):
            nc.vector.wait_ge(hi_ready, n + 1)
            nc.vector.tensor_tensor(WL[:, u], RAW[:, u], WH[:, u].bitcast(F32), ALU.subtract).then_inc(lo_ready, 1)

        def stage_loop(eng, name, body):
            trips = COUNT[name] // SLOTS
            if BASE[name] + COUNT[name] == PANELS:
                with loop(eng, trips - 1) as i:
                    body(i, False)
                body(trips - 1, True)
            else:
                with loop(eng, trips) as i:
                    body(i, False)

        def pe_stage(pe, name, moving_h, moving_l, kt=KT, ready=None, count=0):
            base = BASE[name]

            def tile(u, k):
                for w, m, start, stop in ((WH, moving_h, k == 0, False), (WH, moving_l, False, False),
                                          (WL, moving_h, False, k == kt - 1)):
                    for h in range(2):
                        ins = nc.tensor.matmul(PS[:, 2 * u + h, 0:HALF], w[:, u, k, :],
                                               m[:, k, HALF * h:HALF * h + HALF], start=start, stop=stop)
                return ins

            def split_panel(n):
                if not isinstance(n, int) or n >= SLOTS:
                    pe.wait_ge(psum_free, n - SLOTS + 1)
                pe.wait_ge(hi_ready, n + 1)
                pe.wait_ge(lo_ready, n + 1)

            for u in range(SLOTS):
                split_panel(base + u)
            for k in range(kt):
                pe.wait_ge(ready, count + k + 1)
                for u in range(SLOTS):
                    ins = tile(u, k)
                    if k == kt - 1:
                        ins.then_inc(pe_done, 1)
            with loop(pe, COUNT[name] // SLOTS - 1) as i:
                for u in range(SLOTS):
                    split_panel(base + SLOTS * (i + 1) + u)
                    for k in range(kt):
                        ins = tile(u, k)
                    ins.then_inc(pe_done, 1)

        def pe_ada(pe, group, bank):
            a = SLOTS * group
            before = 0 if a < ADA_FIRST else ADA_SECOND_AT if a < ADA_SECOND else ADA_THIRD_AT
            if group:
                pe.wait_ge(rows_read, group)
            for u in range(SLOTS):
                pe.wait_ge(raw_in[u], 64 * (group + 1) + 16 * before)
                for k in range(2):
                    ins = nc.tensor.matmul(PS[0:2, bank, :], SC[:, 2 * u + k, :],
                                           RAW[:, u].rearrange("p k m -> p (k m)")[:, 512 * k:512 * k + 512],
                                           start=(u + k == 0), stop=(u == 3 and k == 1))
                ins.then_inc(ada_done, 1)

        ADA_PARTS = [(0, 0, 2, 3, 0), (0, 2, 6, 7, 0), (1, 0, 2, 7, P), (1, 2, 6, 7, 0)]
        GROUPS_IN = [4, 12, 16, 24]

        def act_rows(group, bank):
            a = nc.scalar
            a.wait_ge(ada_done, SLOTS * group + SLOTS)
            if group >= GROUPS_IN[0] + 2:
                a.wait_ge(rows_out[group % 2], 16 * ((group - GROUPS_IN[0]) // 2))
            elif group >= 2:
                a.wait_ge(rows_t, group - 1)
            a.activation(ROWS[:, group % 2, :], PS[0:2, bank, :], ACT.Copy).then_inc(rows_read, 1)

        def pool_ada(part):
            g = nc.gpsimd
            layer, first, end, bank, c0 = ADA_PARTS[part]
            for group in range(GROUPS_IN[part - 1], GROUPS_IN[part]):
                g.wait_ge(rows_read, group + 1)
                at = SLOTS * P * group - MODQ * P * layer
                g.dma_start(M_SCR[layer][:, at:at + SLOTS * P], ROWS[:, group % 2, :]).then_inc(rows_out[group % 2], 16)
            for u in range(2):
                g.wait_ge(rows_out[u], 8 * (GROUPS_IN[part] - GROUPS_IN[0]))
            if part == 3:
                g.wait_ge(mods_ps, 2)
            n = (end - first) * KT
            for s in range(2):
                g.dma_start(MT[n * s:n * s + n, part % 2, :], M_SCR[layer, s].rearrange("(q p) -> q p", p=P)
                            [first * KT:end * KT, :]).then_inc(mt_in, 16)

        def pe_first_mods(pe):
            def columns(group):
                pe.wait_ge(rows_read, group + 1)
                for q in range(SLOTS):
                    c = 2 * (SLOTS * group + q)
                    ins = nc.tensor.transpose(PS[:, 2, c:c + 2], ROWS[:, group % 2, P * q:P * q + P], IDENT[0:2, 0:2])
                ins.then_inc(rows_t, 1)

            for group in range(GROUPS_IN[0]):
                pe_ada(pe, group, 3)
                if group:
                    columns(group - 1)
            columns(GROUPS_IN[0] - 1)

        def pe_mods(pe, part):
            layer, first, end, bank, c0 = ADA_PARTS[part]
            n = 2 * (end - first) * KT
            pe.wait_ge(mt_in, 32 * part)
            pe.wait_ge(rows_read, GROUPS_IN[max(part, 2)])
            nc.tensor.transpose(PS[:, bank, c0:c0 + n], MT[0:n, part % 2, :], IDENT[0:n, 0:n]).then_inc(mods_ps, 1)

        def pe_ffn(pe, layer, r):
            for ph, (_first, n) in enumerate(PHASES):
                up, down = f"up{layer}{ph}", f"down{layer}{ph}"
                pe_stage(pe, up, XH, XL, ready=xl_ready, count=r * KT)
                pe_stage(pe, down, HH, HL, n, ready=hid_lo, count=PAIRS_BEFORE[up])

        def pe_norm(pe, q):
            pe.wait_ge(ln_sum, q + 1)
            for h in range(2):
                ins = nc.tensor.matmul(PS[:, h, 0:HALF], MEANW[:, :], ACC[:, HALF * h:HALF * h + HALF],
                                       start=True, stop=True)
            ins.then_inc(ln_mean, 1)
            for k in range(KT):
                pe.wait_ge(ln_sq, KT * q + k + 1)
                for h in range(2):
                    ins = nc.tensor.matmul(PS[:, 2 + h, 0:HALF], MEANW[:, :], SQ[:, k % 2, HALF * h:HALF * h + HALF],
                                           start=(k == 0), stop=(k == KT - 1))
                ins.then_inc(ln_sqsum, 1)

        vchain = Chain(nc.vector, dve_chain)
        v_link = vchain.link

        def act_gated(name, func):
            base = BASE[name]

            def body(i, last):
                for c in range(2):
                    n = base + SLOTS * i + 2 * c
                    nc.scalar.wait_ge(pe_done, n + 1)
                    nc.scalar.activation(by_half(GT[:, c, :]), halves(4 * c), func).then_inc(silu_done, 1)
                    if not last:
                        split_hi(n + SLOTS, 2 * c, ada=ada_before(name))
                        split_hi(n + SLOTS + 1, 2 * c + 1, ada=ada_before(name))
                    nc.scalar.wait_ge(psum_free, n + 2)
                    nc.scalar.activation(HH[:, bass.ds(2 * i + c, 1), :].rearrange("p a t -> p (a t)"),
                                         HT[:, c, :], ACT.Copy).then_inc(hid_hi, 1)

            stage_loop(nc.scalar, name, body)

        def dve_gated(name, pairs_before):
            base = BASE[name]

            def body(i, last):
                for c in range(2):
                    n = base + SLOTS * i + 2 * c
                    pair = pairs_before + 2 * i + c
                    nc.vector.wait_ge(silu_done, pair + 1)
                    nc.vector.wait_ge(pe_done, n + 2)
                    if pairs_before:
                        nc.vector.wait_ge(hid_lo, pair - 1)
                    nc.vector.tensor_tensor(by_half(HT[:, c, :]), halves(4 * c + 2), by_half(GT[:, c, :]),
                                            ALU.mult).then_inc(psum_free, 2)
                    if not last:
                        split_lo(n + SLOTS, 2 * c)
                        split_lo(n + SLOTS + 1, 2 * c + 1)
                    nc.vector.wait_ge(hid_hi, pair + 1)
                    one = bass.ds(2 * i + c, 1)
                    nc.vector.tensor_tensor(HL[:, one, :].rearrange("p a t -> p (a t)"), HT[:, c, :],
                                            HH[:, one, :].rearrange("p a t -> p (a t)").bitcast(F32),
                                            ALU.subtract).then_inc(hid_lo, 1)

            stage_loop(nc.vector, name, body)

        def act_split_only(name):
            base = BASE[name]

            def body(i, last):
                for u in range(SLOTS):
                    if not last:
                        split_hi(base + SLOTS * i + u + SLOTS, u, ada=ada_before(name))

            stage_loop(nc.scalar, name, body)

        def stream_parts(permuted):
            if not permuted:
                return [(0, 0, slice(0, CTX), slice(0, CTX)), (1, 0, slice(CTX, HALF), slice(CTX, HALF)),
                        (1, 1, slice(0, HALF), slice(HALF, TOK))]
            return [(s, h, cs, h) for h in range(2) for s, cs in ((0, slice(0, CCH)), (1, slice(CCH, NCHUNK)))]

        norm_after = [BASE["wo"] + 8, BASE["down02"] + 8, BASE["wout"] + 8, BASE["down12"] + 8]

        def dve_residual(name, layer, gate):
            base = BASE[name]
            v = nc.vector

            def add_to_sum(k):
                v.wait_ge(psum_free, base + k + 1)
                if k == 0:
                    return v.tensor_copy(ACC[:, :], X[:, 0, :])
                return v.tensor_tensor(ACC[:, :], ACC[:, :], X[:, k, :], ALU.add)

            def body(i, last):
                for u in range(SLOTS):
                    n = base + SLOTS * i + u
                    nc.vector.wait_ge(pe_done, n + 1)
                    tile = X[:, bass.ds(SLOTS * i + u, 1), :].rearrange("p a t -> p (a t)")
                    col = MODS[:, layer, bass.ds(gate * KT + SLOTS * i + u, 1), :].rearrange("p a s -> p (a s)")
                    for s, b, cols, where in stream_parts(layer == 1):
                        if layer == 0:
                            src, dst = PS[:, 2 * u + b, cols], tile[:, where]
                        else:
                            src = PS[:, 2 * u + b, 0:HALF].rearrange("p (t c) -> p t c", c=NCHUNK)[:, :, cols]
                            dst = tile[:, HALF * b:HALF * b + HALF].rearrange("p (t c) -> p t c", c=NCHUNK)[:, :, cols]
                        ins = nc.vector.scalar_tensor_tensor(out=dst, in0=src, scalar=col[:, s:s + 1], in1=dst,
                                                             op0=ALU.mult, op1=ALU.add)
                    ins.then_inc(psum_free, 1)
                    if sums:
                        k = SLOTS * i + u
                        if k:
                            v_link(add_to_sum(k - 1))
                        if k == KT - 1:
                            add_to_sum(k).then_inc(ln_sum, 1)
                    if not last:
                        split_lo(n + SLOTS, u)

            sums = base + COUNT[name] in norm_after
            if sums:
                for i in range(2):
                    body(i, i == 1 and base + COUNT[name] == PANELS)
            else:
                stage_loop(nc.vector, name, body)

        def dve_store(name, dest):
            base = BASE[name]

            def body(i, last):
                for u in range(SLOTS):
                    n = base + SLOTS * i + u
                    nc.vector.wait_ge(pe_done, n + 1)
                    nc.vector.tensor_copy(by_half(dest[:, bass.ds(SLOTS * i + u, 1), :].rearrange("p a t -> p (a t)")),
                                          halves(2 * u)).then_inc(psum_free, 1)
                    if not last:
                        split_lo(n + SLOTS, u)

            stage_loop(nc.vector, name, body)


        def dve_mods(part):
            v = nc.vector
            layer, first, end, bank, c0 = ADA_PARTS[part]
            q = slice(first * KT, end * KT)
            n = (end - first) * KT
            if part:
                v.wait_ge(mods_ps, max(part, 2))
                src = PS[:, bank, c0:c0 + 2 * n].rearrange("p (s q) -> p q s", s=2)
            else:
                v.wait_ge(rows_t, GROUPS_IN[0])
                src = PS[:, 2, 0:2 * n].rearrange("p (q s) -> p q s", s=2)
            bias = PV1[:, MODQ * layer:MODQ * (layer + 1)][:, q].unsqueeze(2).to_broadcast([P, n, 2])
            v.tensor_tensor(MODS[:, layer, q], src, bias,
                            ALU.add).then_inc(mods_read, 1)
            v.wait_ge(mods_read, part + 1)
            for sixth in range(first, end):
                cols = MODS[:, layer, sixth * KT:(sixth + 1) * KT, :]
                if sixth % 3 == 1:
                    v_link(v.tensor_scalar(cols, cols, 1.0, None, ALU.add))
                if sixth % 3 == 2:
                    v_link(v.tensor_scalar(cols, cols, 1.0 / ALPHA, None, ALU.mult))

        def perm_view(tile):
            return tile.rearrange("p (t c) -> p t c", c=NCHUNK)


        def dve_norm(q):
            v = nc.vector
            v.wait_ge(ln_mean, q + 1)
            for k in range(KT):
                v.tensor_tensor(by_half(X[:, k, :]), by_half(X[:, k, :]), halves(0), ALU.subtract).then_inc(ln_cent, 1)
            v.wait_ge(ln_std, 2 * q + 2)
            v_link(v.tensor_tensor(RT[:, :], RSTD[:, :], RSTD[:, :], ALU.mult))
            v_link(v.scalar_tensor_tensor(out=by_half(RT[:, :]), in0=halves(2), scalar=LN_EPS / ALPHA ** 2,
                                          in1=by_half(RT[:, :]), op0=ALU.add, op1=ALU.mult))
            v_link(v.tensor_scalar(RT[:, :], RT[:, :], -0.5, 1.5, ALU.mult, ALU.add))
            v_link(v.tensor_tensor(RSTD[:, :], RSTD[:, :], RT[:, :], ALU.mult))

        def dve_norm_scale(q, k):
            v = nc.vector
            if k >= 2:
                v.wait_ge(ln_x, KT * q + k - 1)
            v.wait_ge(ln_cent, KT * q + k + 1)
            v.scalar_tensor_tensor(out=YT[:, k % 2, :], in0=X[:, k, :], scalar=PV1[:, 2 * MODQ + KT * q + k:2 * MODQ + KT * q + k + 1],
                                   in1=RSTD[:, :], op0=ALU.mult, op1=ALU.mult).then_inc(ln_y, 1)

        def act_norm(q):
            a = nc.scalar
            for k in range(KT):
                a.wait_ge(ln_cent, KT * q + k + 1)
                if k >= 2:
                    a.wait_ge(ln_sqsum, KT * q + k - 1)
                a.activation(SQ[:, k % 2, :], X[:, k, :], ACT.Square).then_inc(ln_sq, 1)
            a.wait_ge(ln_sqsum, KT * q + KT)
            a.activation(by_half(STD[:, :]), halves(2), ACT.Ln, bias=EPS[:, :]).then_inc(ln_std, 1)
            a.wait_ge(ln_std, 2 * q + 1)
            a.activation(RSTD[:, :], STD[:, :], ACT.Exp, scale=-0.5).then_inc(ln_std, 1)

        def act_norm_shift(q, k):
            a = nc.scalar
            a.wait_ge(ln_y, KT * q + k + 1)
            src, dst = YT[:, k % 2, :], X[:, k, :]
            if q == 1:
                src, dst = src.rearrange("p (c t) -> p t c", t=CHUNK), perm_view(dst)
            if q == 3:
                src, dst = perm_view(src), dst.rearrange("p (c t) -> p t c", t=CHUNK)
            a.activation(dst, src, ACT.Identity, bias=PV2[:, KT * q + k:KT * q + k + 1]).then_inc(ln_x, 1)

        def dve_modulate(r, layer, shift, before):
            v = nc.vector

            def low(k):
                v.wait_ge(xh_ready, KT * r + k + 1)
                v.tensor_tensor(XL[:, k, :], XM[:, k % 2, :], XH[:, k, :].bitcast(F32), ALU.subtract).then_inc(xl_ready, 1)

            for k in range(KT):
                before(k)
                if k >= 2:
                    v.wait_ge(xl_ready, KT * r + k - 1)
                sc = MODS[:, layer, (shift + 1) * KT + k, :]
                sh = MODS[:, layer, shift * KT + k, :]
                for s in range(2):
                    if r < 2:
                        cols = slice(0, CTX) if s == 0 else slice(CTX, TOK)
                        src, dst = X[:, k, cols], XM[:, k % 2, cols]
                    else:
                        cols = slice(0, CCH) if s == 0 else slice(CCH, NCHUNK)
                        src = perm_view(X[:, k, :])[:, :, cols]
                        dst = perm_view(XM[:, k % 2, :])[:, :, cols]
                    ins = v.tensor_scalar(dst, src, sc[:, s:s + 1], sh[:, s:s + 1], ALU.mult, ALU.add)
                ins.then_inc(xm_ready, 1)
                if k:
                    low(k - 1)
            low(KT - 1)

        def act_high(r, k):
            a = nc.scalar
            a.wait_ge(xm_ready, KT * r + k + 1)
            a.activation(XH[:, k, :], XM[:, k % 2, :], ACT.Copy).then_inc(xh_ready, 1)

        def dve_norm_modulate(q, r, layer, shift):
            dve_norm(q)

            def before(k):
                if k == 0:
                    dve_norm_scale(q, 0)
                if k < KT - 1:
                    dve_norm_scale(q, k + 1)
                nc.vector.wait_ge(ln_x, KT * q + k + 1)

            dve_modulate(r, layer, shift, before)

        def act_norm_modulate(q, r):
            act_norm(q)
            act_norm_shift(q, 0)
            for k in range(KT):
                if k < KT - 1:
                    act_norm_shift(q, k + 1)
                act_high(r, k)

        qkv_end = BASE["wo"]

        STEPS = [(block, B, h) for block in (None, 0, 1, 2, 3) for B in range(2) for h in range(2)]

        ADA_STEPS = [0, 1, 2, 3] + list(range(4, 20, 2))
        assert len(ADA_STEPS) == GROUPS_IN[2] - GROUPS_IN[0]

        def key_tiles(block):
            return 1 if block is None else 4

        def pe_attention_start(pe):
            pe.wait_ge(psum_free, qkv_end)
            pe.wait_ge(attn_in, 16 * ATTN_DMAS)
            t = lambda bank, col, src: nc.tensor.transpose(PS[:, bank, P * col:P * col + P], src, IDENT[:, :])
            for bank in range(2):
                for b in range(2):
                    for d in range(2):
                        c0 = CTX + P * (2 * bank + b)
                        ins = t(bank, 2 * b + d, QKVT[:, 10 + d, c0:c0 + P])
                ins.then_inc(att_t, 1)
            for d in range(2):
                t(2, d, QKVT[:, 10 + d, 0:CTX])
                ins = t(2, 2 + d, QKVT[:, 8 + d, 0:CTX])
            ins.then_inc(att_t, 1)
            for d in range(2):
                ins = t(3, d, CK[:, P * d:P * d + P])
            ins.then_inc(att_t, 1)

        def act_attention_start():
            a = nc.scalar
            for bank in range(2):
                a.wait_ge(att_t, bank + 1)
                a.activation(VN[:, 2 + 2 * bank:4 + 2 * bank, :].rearrange("p b d -> p (b d)"), PS[:, bank, :],
                             ACT.Copy).then_inc(att_kv, 1)
            a.wait_ge(att_t, 3)
            a.activation(VN[:, 0, :], PS[:, 2, 0:2 * P], ACT.Copy).then_inc(att_kv, 1)
            a.activation(KN[:, :], PS[:, 2, 2 * P:4 * P], ACT.Copy).then_inc(att_kv, 1)
            a.wait_ge(att_t, 4)
            a.activation(KCT[:, :, :].rearrange("p b d -> p (b d)"), PS[:, 3, 0:2 * P], ACT.Copy).then_inc(att_kv, 1)

        SWAP_HALVES = [(p + 16) % 32 for p in range(32)]

        def dve_rotate(out, src, cos, sin, swap):
            v = nc.vector
            v_link(v.stream_shuffle(swap, src, SWAP_HALVES))
            v_link(v.tensor_tensor(swap, swap, sin, ALU.mult))
            v_link(v.tensor_tensor(out, src, cos, ALU.mult))
            return v.tensor_tensor(out, out, swap, ALU.add)

        def dve_attention_start():
            v = nc.vector
            v.wait_ge(psum_free, qkv_end)
            v.wait_ge(attn_in, 16 * ATTN_DMAS)
            v.wait_ge(sink_in, 16)

        def dve_keys(B):
            v = nc.vector
            v_link(v.memset(VN[:, 1 + 5 * B, :], 0.0))
            v_link(v.memset(KR[:, B, 0:P], 0.0))
            v_link(v.memset(KR[:, B, P + LAT:], 0.0))
            v_link(dve_rotate(KR[:, B, P:P + LAT], QKVT[:, 8 + B, CTX:TOK], ROPE[:, 0, :], ROPE[:, 1, :], SWAP[:, :]))

        def queries(block, B):
            first = 0 if block is None else block * P + CTX
            return QKVT[:, 4 * B:4 * B + 4, bass.ds(first, P)]

        def attended(T, block, B, rows):
            first = 0 if block is None else block * P + CTX
            return T[rows, 4 * B:4 * B + 4, first:first + P]

        def pv_out(h):
            return PS[HD * h:HD * h + HD, 6, :].rearrange("p (j q) -> p j q", j=4)

        def dve_queries(t):
            block, B, h = STEPS[t]
            v, turn = nc.vector, t // 2
            tok = slice(block * P, block * P + P)
            cos = ROPE[:, 0, tok].unsqueeze(1).to_broadcast([P, 4, P])
            sin = ROPE[:, 1, tok].unsqueeze(1).to_broadcast([P, 4, P])
            if turn >= 4:
                v.wait_ge(att_s, 8 * (turn - 2) + 8)
            dve_rotate(QR[:, turn % 2, :, :], queries(block, B), cos, sin,
                       SWAP[:, :].rearrange("p (a t) -> p a t", a=4)).then_inc(att_qrot, 1)

        def dve_mask(t):
            block, B, h = STEPS[t]
            v, width, c = nc.vector, P * key_tiles(block), 4 * (t % 2)
            if t >= 2:
                v.wait_ge(att_tr, 4 * (t - 2) + 4)
            for j in range(4):
                v.wait_ge(att_s, 4 * t + j + 1)
                v.tensor_tensor_reduce(out=S[:, c + j, 0:width], in0=PS[:, j, 0:width], in1=MASK[:, block or 0, 0:width],
                                       scale=1.0, scalar=-3.0e38, op0=ALU.add, op1=ALU.max,
                                       accum_out=STAT[:, 0, c + j:c + j + 1]).then_inc(att_max, 1)
            v.wait_ge(att_max, 4 * t + 4)
            row = lambda r: STAT[:, r, c:c + 4]
            sink = SINK[:, 8 * B + 4 * h:8 * B + 4 * h + 4]
            v_link(v.scalar_tensor_tensor(out=row(1), in0=row(0), scalar=SCALE, in1=sink, op0=ALU.mult, op1=ALU.max))
            v_link(v.tensor_scalar(row(2), row(1), -1.0, None, ALU.mult))
            v.tensor_tensor(row(3), sink, row(1), ALU.subtract).then_inc(att_stat, 1)

        def dve_normalize(t):
            block, B, h = STEPS[t]
            v, width, c = nc.vector, P * key_tiles(block), 4 * (t % 2)
            v.wait_ge(att_exp, 5 * t + 5)
            v_link(v.tensor_tensor(STAT[:, 6, c:c + 4], STAT[:, 4, c:c + 4], STAT[:, 5, c:c + 4], ALU.add))
            v_link(v.reciprocal(STAT[:, 7, c:c + 4], STAT[:, 6, c:c + 4]))
            for j in range(4):
                v.tensor_scalar(S[:, c + j, 0:width], S[:, c + j, 0:width], STAT[:, 7, c + j:c + j + 1], None,
                                ALU.mult).then_inc(att_p, 1)

        def dve_attended(t):
            block, B, h = STEPS[t]
            rows = slice(HD * h, HD * h + HD)
            nc.vector.wait_ge(att_oh, t + 1)
            nc.vector.tensor_tensor(attended(XL, block, B, rows), pv_out(h), attended(XH, block, B, rows).bitcast(F32),
                                    ALU.subtract).then_inc(att_ol, 1)

        def dve_attention():
            dve_mask(0)
            for t in range(len(STEPS)):
                dve_normalize(t)
                if t + 1 < len(STEPS):
                    dve_mask(t + 1)
                if t < 2:
                    dve_keys(t)
                if t + 2 < len(STEPS) and t % 2 == 0 and STEPS[t + 2][0] is not None:
                    dve_queries(t + 2)
                if t:
                    dve_attended(t - 1)
            dve_attended(len(STEPS) - 1)

        def act_exp(t):
            block, B, h = STEPS[t]
            a, width, c = nc.scalar, P * key_tiles(block), 4 * (t % 2)
            a.wait_ge(att_stat, t + 1)
            a.activation(STAT[:, 5, c:c + 4], STAT[:, 3, c:c + 4], ACT.Exp).then_inc(att_exp, 1)
            for j in range(4):
                a.activation(S[:, c + j, 0:width], S[:, c + j, 0:width], ACT.Exp, bias=STAT[:, 2, c + j:c + j + 1],
                             scale=SCALE, accum_out=STAT[:, 4, c + j:c + j + 1]).then_inc(att_exp, 1)

        def act_attention():
            a = nc.scalar
            act_exp(0)
            for t, (block, B, h) in enumerate(STEPS):
                kt = key_tiles(block)
                if t:
                    a.wait_ge(att_pv, t)
                for j in range(4):
                    a.wait_ge(att_tr, 4 * t + j + 1)
                    a.activation(PT[:, 0:kt, j, :], PS[:, 4 + j % 2, 0:P * kt].rearrange("p (k q) -> p k q", k=kt),
                                 ACT.Copy).then_inc(att_pt, 1)
                if t + 1 < len(STEPS):
                    act_exp(t + 1)
                if t in ADA_STEPS:
                    act_rows(GROUPS_IN[0] + ADA_STEPS.index(t), 7)
                a.wait_ge(att_pv, t + 1)
                a.activation(attended(XH, block, B, slice(HD * h, HD * h + HD)), pv_out(h), ACT.Copy).then_inc(att_oh, 1)

        def pe_scores(pe, t):
            block, B, h = STEPS[t]
            rows = slice(HD * h, HD * h + HD)
            if h == 0 and block is not None:
                pe.wait_ge(att_qrot, 2 * block + B + 1)
            for j in range(4):
                if t:
                    pe.wait_ge(att_max, 4 * (t - 1) + j + 1)
                keys = QKVT[rows, 8 + B, 0:CTX] if block is None else KCT[rows, B, :]
                ins = nc.tensor.matmul(PS[:, j, 0:P], queries(block, B)[rows, j, :], keys, start=True, stop=True)
                if block is not None:
                    ins = nc.tensor.matmul(PS[:, j, P:4 * P], QR[rows, (t // 2) % 2, j, :],
                                           KR[rows, B, P * block:P * block + 3 * P], start=True, stop=True)
                ins.then_inc(att_s, 1)

        def pe_attention(pe):
            pe.wait_ge(att_kv, 5)
            pe_scores(pe, 0)
            for t, (block, B, h) in enumerate(STEPS):
                if t + 1 < len(STEPS):
                    pe_scores(pe, t + 1)
                kt = key_tiles(block)
                for j in range(4):
                    pe.wait_ge(att_p, 4 * t + j + 1)
                    if 4 * t + j >= 2:
                        pe.wait_ge(att_pt, 4 * t + j - 1)
                    for k in range(kt):
                        ins = nc.tensor.transpose(PS[:, 4 + j % 2, P * k:P * k + P],
                                                  S[:, 4 * (t % 2) + j, P * k:P * k + P], IDENT[:, :])
                    ins.then_inc(att_tr, 1)
                if t in ADA_STEPS:
                    pe_ada(pe, GROUPS_IN[0] + ADA_STEPS.index(t), 7)
                pe.wait_ge(att_pt, 4 * t + 4)
                if t >= 2:
                    pe.wait_ge(att_ol, t - 1)
                c0 = P * B + HD * h
                for k in range(kt):
                    val = VN[:, 0, :] if block is None else CV[:, :] if k == 0 else VN[:, block + k, :]
                    ins = nc.tensor.matmul(PS[HD * h:HD * h + HD, 6, :], val[:, c0:c0 + HD],
                                           PT[:, k, :, :].rearrange("p j q -> p (j q)"), start=(k == 0), stop=(k == kt - 1))
                ins.then_inc(att_pv, 1)

        NB = GROUPS // 8
        FWD, BWD = slice(0, STATE), slice(STATE, P)

        def complex_mult(eng, chn, out_re, out_im, ar, ai, br, bi, t1, t2, minus_bi=None):
            chn.link(eng.tensor_tensor(t1, ar, br, ALU.mult))
            chn.link(eng.tensor_tensor(t2, ai, bi, ALU.mult))
            chn.link(eng.tensor_tensor(out_re, t1, t2, ALU.subtract))
            chn.link(eng.tensor_tensor(t1, ar, bi if minus_bi is None else minus_bi, ALU.mult))
            chn.link(eng.tensor_tensor(t2, ai, br, ALU.mult))
            return eng.tensor_tensor(out_im, t1, t2, ALU.add if minus_bi is None else ALU.subtract)

        def pool_ssm_start(g):
            g.wait_ge(att_ol, len(STEPS))
            by_group = lambda a: a.rearrange("d g p -> g d p")
            g.dma_start(LAM[:, 0], by_group(I["ssm_lam_re"][0])).then_inc(ssm_in, 16)
            g.dma_start(LAM[:, 1], by_group(I["ssm_lam_im"][0])).then_inc(ssm_in, 16)
            g.dma_start(GM[:, 4], by_group(I["state_ssm_re"][0, 0])).then_inc(ssm_in, 16)
            g.dma_start(GM[:, 5], by_group(I["state_ssm_im"][0, 0])).then_inc(ssm_in, 16)
            for d in range(2):
                g.dma_start(LDT[:, d:d + 1], I["ssm_log_dt"][0, d].rearrange("(g a) -> g a", a=1)).then_inc(ssm_in, 16)
            for r, nm in enumerate(("re", "im")):
                for d in range(2):
                    rows = slice(STATE * d, STATE * d + STATE)
                    g.dma_start(BN[rows, r], I["ssm_b_" + nm][0, d].rearrange("g p m -> p g m")).then_inc(ssm_in, 16)
                    g.dma_start(CN[:, r, :, d, :], I["ssm_c_" + nm][0, d].rearrange("g n p -> (g n) p")
                                 .rearrange("(T q) p -> q T p", q=P)).then_inc(ssm_in, 16)
            g.dma_start(DB[:, :], I["ssm_d"][0:1, :].to_broadcast([GCH, D])).then_inc(ssm_in, 16)

        TWO_PI = (6.28125, 0.0019350051879882812, 3.0199161e-07)
        ROUND = 12582912.0

        def act_discretise():
            a = nc.scalar
            a.wait_ge(ssm_in, 16 * SSM_DMAS)
            a.activation(LDT[:, :], LDT[:, :], ACT.Exp).then_inc(ssm_a, 1)
            a.wait_ge(ssm_v, 1)
            a.activation(MAG[:, :], ZR[:, :], ACT.Exp).then_inc(ssm_a, 1)
            a.wait_ge(ssm_v, 2)
            a.activation(SINH[:, :], ZI[:, :], ACT.Sin, scale=0.5).then_inc(ssm_a, 1)
            a.activation(SIN[:, :], ZI[:, :], ACT.Sin).then_inc(ssm_a, 1)

        def act_ssm_start():
            a = nc.scalar
            a.wait_ge(ssm_t, 1)
            a.activation(AC[:, :, :], PS[:, 0, 0:6 * GROUPS].rearrange("p (a g) -> p a g", g=GROUPS), ACT.Copy).then_inc(ssm_a, 1)
            for n in range(4):
                a.wait_ge(ssm_t, 2 + n)
                a.activation(CT[:, n // 2, 4 * (n % 2):4 * (n % 2) + 4, :].rearrange("p a n -> p (a n)"),
                             PS[:, 4 + n, :], ACT.Copy).then_inc(ssm_a, 1)
            a.wait_ge(ssm_v, 4)
            a.activation(POWB[0:64], POW[0:64, :, 0:8, :][:, :, ::-1, :], ACT.Copy).then_inc(ssm_a, 1)
            a.activation(POWB[64:P], POW[64:P, :, 0:8, :], ACT.Copy).then_inc(ssm_a, 1)
            a.activation(POWC[0:64, 0:2], POW[0:64], ACT.Copy).then_inc(ssm_a, 1)
            a.activation(POWC[0:64, 2], POW[0:64, 1], ACT.Copy, scale=-1.0).then_inc(ssm_a, 1)
            a.activation(POWC[64:P, 0:2], POW[64:P][:, :, ::-1, :], ACT.Copy).then_inc(ssm_a, 1)
            a.activation(POWC[64:P, 2], POW[64:P, 1][:, ::-1, :], ACT.Copy, scale=-1.0).then_inc(ssm_a, 1)

        def dve_discretise():
            v = nc.vector
            chn = vchain
            tt, ts = v.tensor_tensor, v.tensor_scalar
            v.wait_ge(ssm_in, 16 * SSM_DMAS)
            v.wait_ge(ssm_a, 1)
            dp = lambda t: t[:, :].rearrange("g (d p) -> g d p", d=2)
            dt = LDT[:, :].unsqueeze(2).to_broadcast([GROUPS, 2, STATE])
            tt(dp(ZR), LAM[:, 0], dt, ALU.mult).then_inc(ssm_v, 1)
            chn.link(tt(dp(ZI), LAM[:, 1], dt, ALU.mult))
            chn.link(ts(T1[:, :], ZI[:, :], 1.0 / (2 * np.pi), None, ALU.mult))
            chn.link(ts(T1[:, :], T1[:, :], ROUND, None, ALU.add))
            chn.link(ts(T1[:, :], T1[:, :], -ROUND, None, ALU.add))
            for part in TWO_PI:
                chn.link(v.scalar_tensor_tensor(out=ZI[:, :], in0=T1[:, :], scalar=-part, in1=ZI[:, :], op0=ALU.mult, op1=ALU.add))
            ts(ZI[:, :], ZI[:, :], 3.1415925, -3.1415925, ALU.min, ALU.max).then_inc(ssm_v, 1)
            v.wait_ge(ssm_a, 4)
            chn.link(tt(T1[:, :], SINH[:, :], SINH[:, :], ALU.mult))
            chn.link(ts(T1[:, :], T1[:, :], -2.0, 1.0, ALU.mult, ALU.add))
            gm = lambda r: GM[:, r].rearrange("g d p -> g (d p)")
            lam = lambda r: LAM[:, r].rearrange("g d p -> g (d p)")
            chn.link(tt(gm(0), MAG[:, :], T1[:, :], ALU.mult))
            chn.link(tt(gm(1), MAG[:, :], SIN[:, :], ALU.mult))
            chn.link(ts(T1[:, :], gm(0), -1.0, None, ALU.add))
            chn.link(tt(T2[:, :], lam(0), lam(0), ALU.mult))
            chn.link(tt(T3[:, :], lam(1), lam(1), ALU.mult))
            chn.link(tt(T2[:, :], T2[:, :], T3[:, :], ALU.add))
            chn.link(v.reciprocal(T2[:, :], T2[:, :]))
            chn.link(tt(gm(2), T1[:, :], lam(0), ALU.mult))
            chn.link(tt(T3[:, :], gm(1), lam(1), ALU.mult))
            chn.link(tt(gm(2), gm(2), T3[:, :], ALU.add))
            chn.link(tt(gm(2), gm(2), T2[:, :], ALU.mult))
            chn.link(tt(gm(3), gm(1), lam(0), ALU.mult))
            chn.link(tt(T3[:, :], T1[:, :], lam(1), ALU.mult))
            chn.link(tt(gm(3), gm(3), T3[:, :], ALU.subtract))
            tt(gm(3), gm(3), T2[:, :], ALU.mult).then_inc(ssm_v, 1)

        def dve_ssm_start():
            v = nc.vector
            chn, ts = vchain, nc.vector.tensor_scalar
            v.wait_ge(ssm_a, 5)
            chn.link(v.memset(POW[:, 0, 0, :], 1.0))
            chn.link(v.memset(POW[:, 1, 0, :], 0.0))
            chn.link(v.tensor_copy(POW[:, :, 1, :], AC[:, 0:2, :]))
            for have in (1, 2, 4):
                pw = lambda r: POW[:, r, 1:have + 1, :]
                by = lambda r: POW[:, r, have:have + 1, :].to_broadcast([P, have, GROUPS])
                tmp = [W1[:, 0:have * GROUPS].rearrange("p (k g) -> p k g", g=GROUPS),
                       W2[:, 0:have * GROUPS].rearrange("p (k g) -> p k g", g=GROUPS)]
                out = lambda r: POW[:, r, have + 1:2 * have + 1, :]
                ins = complex_mult(v, chn, out(0), out(1), pw(0), pw(1), by(0), by(1), *tmp)
                if have < 4:
                    chn.link(ins)
                else:
                    ins.then_inc(ssm_v, 1)
            v.wait_ge(ssm_v, 4)
            for r in range(2):
                chn.link(v.tensor_copy(AR[:, r, :], POW[:, 0, 8, :]))
            chn.link(v.tensor_copy(AI[:, 0, :], POW[:, 1, 8, :]))
            chn.link(ts(AI[:, 1, :], POW[:, 1, 8, :], -1.0, None, ALU.mult))
            chn.link(v.tensor_copy(H0[:, :, :], AC[:, 4:6, :]))
            wide = [t[:, 0:1024].rearrange("p (g m) -> p g m", m=GCH) for t in (W1, W2)]
            coef = lambda r: AC[:, 2 + r, :].unsqueeze(2).to_broadcast([P, GROUPS, GCH])
            complex_mult(v, chn, BB[:, 0], BB[:, 1], BN[:, 0], BN[:, 1], coef(0), coef(1), *wide).then_inc(ssm_v, 1)
            v.tensor_tensor(DI[:, :, :], DB[:, :].rearrange("p (g n) -> p g n", n=GCH),
                            IDENT[0:GCH, 0:GCH].unsqueeze(1).to_broadcast([GCH, GROUPS, GCH]), ALU.mult).then_inc(ssm_v, 1)
            v.wait_ge(ssm_v, 6)
            v.wait_ge(ssm_a, 15)

        def pe_ssm_start(pe):
            pe.wait_ge(psum_free, BASE["win"])
            pe.wait_ge(ssm_in, 16 * SSM_DMAS)
            pe.wait_ge(ssm_v, 3)
            for r in range(6):
                ins = nc.tensor.transpose(PS[:, 0, GROUPS * r:GROUPS * r + GROUPS], GM[:, r].rearrange("g d p -> g (d p)"),
                                          IDENT[0:GROUPS, 0:GROUPS])
            ins.then_inc(ssm_t, 1)
            for n in range(4):
                for T in range(4):
                    ins = nc.tensor.transpose(PS[:, 4 + n, P * T:P * T + P],
                                              CN[:, n // 2, 4 * (n % 2) + T].rearrange("q d p -> q (d p)"), IDENT[:, :])
                ins.then_inc(ssm_t, 1)

        POOL_GROUPS = 6

        def inputs_powers(T, slot, part, t1, t2):
            n = part.stop - part.start
            b = [BB[:, r, bass.ds(8 * T + part.start, n), :].unsqueeze(1).to_broadcast([P, 8, n, GCH]) for r in range(2)]
            pw = [POWB[:, r, :, bass.ds(8 * T + part.start, n)].unsqueeze(3).to_broadcast([P, 8, n, GCH]) for r in range(2)]
            out = [BP[:, slot, r, part, :].rearrange("p g (t m) -> p t g m", m=GCH) for r in range(2)]
            return (*out, *b, *pw, t1, t2)

        def dve_kernels(T, slot):
            v = nc.vector
            v.wait_ge(ks_copied, 3 * T + 3)
            mid = KS[:, slot, :, 7 * GCH:8 * GCH]
            v_link(v.tensor_tensor(mid, mid, KM[:, slot], ALU.add))
            v.tensor_tensor(mid, mid, DI[:, bass.ds(8 * T, 8), :], ALU.add).then_inc(ks_ready, 1)

        def dve_prep(i, slot, first):
            v = nc.vector
            T = 2 * i + slot
            w = lambda t, k, g: t[:, 0:k * g * GCH].rearrange("p (k g n) -> p k g n", k=k, g=g)
            c = lambda r: CT[:, r, bass.ds(T, 1), :].rearrange("p a (g n) -> p (a g) n", n=GCH).unsqueeze(1).to_broadcast([P, 9, 8, GCH])
            pw = lambda r: POWC[:, r, :, bass.ds(8 * T, 8)].unsqueeze(3).to_broadcast([P, 9, 8, GCH])
            out = lambda r: G[:, slot, r].rearrange("p g k n -> p k g n")
            if not first:
                v.wait_ge(kern_ps, 16 * T - 16)
                v.wait_ge(cp_out[slot], 32 * i)
            complex_mult(v, vchain, out(0), out(1), c(0), c(1), pw(0), pw(1), w(W1, 9, 8), w(W2, 9, 8),
                         minus_bi=pw(2)).then_inc(g_ready, 1)
            v.tensor_copy(BBS[:, slot], BB[:, :, bass.ds(8 * T, 8), :]).then_inc(g_ready, 1)
            if not first:
                v.wait_ge(bt_ps, 4 * T - 4)
            v.wait_ge(g_ready, 2 * T + 2)
            complex_mult(v, vchain, *inputs_powers(T, slot, slice(POOL_GROUPS, 8), w(W1, 8, 2), w(W2, 8, 2))).then_inc(bpv_ready, 1)
            v.wait_ge(bpv_ready, T + 1)
            if not first or slot:
                dve_kernels(T - 1, 1 - slot)

        def pool_prep(T):
            g = nc.gpsimd
            if T >= 2:
                g.wait_ge(bt_ps, 4 * T - 4)
                g.wait_ge(bp_ready, T)
            complex_mult(g, pchain, *inputs_powers(T, T % 2, slice(0, POOL_GROUPS), Q1[:, :, :, :], Q2[:, :, :, :])).then_inc(bp_ready, 1)
            g.wait_ge(bp_ready, T + 1)

        def store_kernels(T, slot):
            nc.scalar.wait_ge(ks_ready, T + 1)
            nc.scalar.dma_start(K_SCR[bass.ds(8 * T, 8)].rearrange("g m n -> m g n"), KS[:, slot]).then_inc(ks_out[slot], 16)

        def act_prep(i, slot, first):
            a = nc.scalar
            T = 2 * i + slot
            a.wait_ge(g_ready, 2 * T + 2)
            for d in range(2):
                rows = slice(64 * d, 64 * d + 64)
                a.dma_start(C_SCR[bass.ds(T, 1)][:, rows].rearrange("a p (g n) -> p (a g) n", n=P),
                            G[rows, slot, :, :, 1 - d:9 - d, :].rearrange("p r g k n -> p (r g) (k n)")).then_inc(cp_out[slot], 16)
            a.wait_ge(kern_ps, 16 * T + 16)
            if not first:
                a.wait_ge(ks_out[slot], 16 * i)
            bwd, fwd = [PS[0:GCH, b:b + 2, :].rearrange("m b (g n) -> m (b g) n", n=P) for b in (4, 6)]
            a.activation(KS[:, slot, :, 0:7 * GCH], bwd[:, :, 0:7 * GCH], ACT.Copy).then_inc(ks_copied, 1)
            a.activation(KS[:, slot, :, 7 * GCH:15 * GCH], fwd, ACT.Copy).then_inc(ks_copied, 1)
            a.activation(KM[:, slot], bwd[:, :, 7 * GCH:P], ACT.Copy).then_inc(ks_copied, 1)
            if not first:
                a.wait_ge(bt_out[slot], 16 * i)
            for n in range(4):
                a.wait_ge(bt_ps, 4 * T + n + 1)
                a.activation(BTS[:, slot, 2 * n:2 * n + 2, :, :].rearrange("p g r n -> p (g r n)"), PS[:, n, :], ACT.Copy).then_inc(bt_ready, 1)
            a.wait_ge(bt_ready, 4 * T + 4)
            a.dma_start(B_SCR[bass.ds(T, 1)].rearrange("a p n -> p (a n)"),
                        BTS[:, slot].rearrange("p g r n -> p (g r n)")).then_inc(bt_out[slot], 16)
            if not first or slot:
                store_kernels(T - 1, 1 - slot)

        def pe_prep(i, slot, first):
            pe = nc.tensor
            T = 2 * i + slot
            pe.wait_ge(g_ready, 2 * T + 2)
            if not first or slot:
                pe.wait_ge(ks_copied, 3 * T)
            for g in range(8):
                for d in range(2):
                    rows = FWD if d else BWD
                    for r in range(2):
                        c0 = P * (g % 4)
                        ins = nc.tensor.matmul(PS[0:GCH, 4 + 2 * d + g // 4, c0:c0 + P], BBS[rows, slot, r, g, :],
                                               G[rows, slot, r, g, 1 - d:9 - d, :].rearrange("p k n -> p (k n)"),
                                               start=(r == 0), stop=(r == 1))
                    ins.then_inc(kern_ps, 1)
            pe.wait_ge(bp_ready, T + 1)
            pe.wait_ge(bpv_ready, T + 1)
            if not first or slot:
                pe.wait_ge(bt_ready, 4 * T)
            for n in range(4):
                for g in range(2):
                    for r in range(2):
                        ins = nc.tensor.transpose(PS[:, n, P * (2 * g + r):P * (2 * g + r) + P], BP[:, slot, r, 2 * n + g, :], IDENT[:, :])
                ins.then_inc(bt_ps, 1)

        def over_batches(eng, body, chn=None, per=0):
            for slot in range(2):
                body(0, slot, True)
            with eng.Fori(1, NB // 2) as i:
                if chn is not None:
                    chn.enter(i - 1, per)
                for slot in range(2):
                    body(i, slot, False)
                if chn is not None:
                    chn.leave(NB // 2 - 1)


        def scan_views():
            return [(FWD, slice(0, CCH), slice(1, 1 + CCH)), (FWD, slice(CCH, NCHUNK), slice(CCH + 2, CCH + 2 + LCH)),
                    (BWD, slice(0, CCH), slice(CCH, 0, -1)), (BWD, slice(CCH, NCHUNK), slice(CCH + 1 + LCH, CCH + 1, -1))]

        def entering_views():
            return [(FWD, slice(0, CCH), slice(0, CCH)), (FWD, slice(CCH, NCHUNK), slice(CCH + 1, CCH + 1 + LCH)),
                    (BWD, slice(0, CCH), slice(CCH - 1, None, -1)), (BWD, slice(CCH, NCHUNK), slice(CCH + LCH, CCH, -1))]

        def load_u8(eng, half):
            eng.wait_ge(u_out[half], 16 * 4)
            gs = slice(32 * half, 32 * half + 32)
            for t in range(CHUNK):
                eng.dma_start(U8[GCH * t:GCH * t + GCH, gs, :], U_SCR.rearrange("(g c) n -> c g n", c=GCH)
                              [:, gs, NCHUNK * t:NCHUNK * t + NCHUNK]).then_inc(u_in[half], 16)

        def pool_ssm(g):
            def load_bt(T):
                g.dma_start(BT[:, T % 2].rearrange("p g r n -> p (g r n)"), B_SCR[T]).then_inc(bt_in[T % 2], 16)

            g.wait_ge(xl_ready, 3 * KT)
            for T in range(2):
                load_bt(T)
            for m in range(KT):
                g.wait_ge(psum_free, BASE["win"] + m + 1)
                g.dma_start(U_SCR[P * m:P * m + P, :], UT[:, m, :]).then_inc(u_out[m // 4], 16)
                if m == 3:
                    load_u8(g, 0)
            for T in range(2, NB):
                g.wait_ge(inc_ps, T - 1)
                load_bt(T)
            pool_ada(3)
            g.wait_ge(fin_ready, 1)
            for r, nm in enumerate(("new_re", "new_im")):
                g.dma_start(O[nm][0, 0].rearrange("d g p -> g d p"), FIN[:, r, :].rearrange("g (d p) -> g d p", d=2)).then_inc(fin_out, 16)

        def load_outputs_matrices(sp):
            sp.wait_ge(inc_ps, NB)
            for T in range(NB):
                if T >= 2:
                    sp.wait_ge(y_ps, T - 1)
                sp.dma_start(CPL[:, T % 2].rearrange("p r g n -> p (r g n)"), C_SCR[T]).then_inc(cp_in[T % 2], 16)
                for t in range(CHUNK):
                    src = K_SCR[8 * T:8 * T + 8].rearrange("g m n -> m g n")[:, :, GCH * (7 - t):GCH * (7 - t) + P]
                    sp.dma_start(TOEP[GCH * t:GCH * t + GCH, T % 2, :, :], src).then_inc(cp_in[T % 2], 16)

        def pe_ssm(pe):
            pe.wait_ge(psum_free, BASE["win"] + KT)
            for T in range(NB):
                pe.wait_ge(u_in[T // 4], 16 * CHUNK)
                pe.wait_ge(bt_in[T % 2], 16 * (T // 2 + 1))
                if T >= 2:
                    pe.wait_ge(inc_a, 2 * T - 2)
                    pe.wait_ge(inc_v, 2 * T - 2)
                for g in range(8):
                    for r in range(2):
                        c0 = 256 * (g % 2) + P * r
                        ins = nc.tensor.matmul(PS[:, 4 * (T % 2) + g // 2, c0:c0 + NCHUNK], BT[:, T % 2, g, r, :],
                                               U8[:, 8 * T + g, :], start=True, stop=True)
                ins.then_inc(inc_ps, 1)
            pe.wait_ge(inc_a, 2 * NB)
            pe.wait_ge(inc_v, 2 * NB)
            for group in range(GROUPS_IN[2], GROUPS_IN[3]):
                pe_ada(pe, group, 7)
            pe_mods(pe, 3)
            for T in range(NB + 1):
                if T < NB:
                    pe.wait_ge(cp_in[T % 2], 16 * 9 * (T // 2 + 1))
                    pe.wait_ge(ent_a, 2 * T + 2)
                    pe.wait_ge(ent_v, 2 * T + 2)
                    if T >= 2:
                        pe.wait_ge(y_ready, T - 1)
                    for g in range(8):
                        out = PS[0:NCHUNK, 2 * (T % 2) + g // 4, P * (g % 4):P * (g % 4) + P]
                        nc.tensor.matmul(out, U8[:, 8 * T + g, :], TOEP[:, T % 2, g, :], start=True, stop=False)
                        for r in range(2):
                            ins = nc.tensor.matmul(out, ENT[:, r, 8 * T + g, :], CPL[:, T % 2, r, g, :], start=False, stop=(r == 1))
                    ins.then_inc(y_ps, 1)
                if T:
                    b = T - 1
                    pe.wait_ge(y_ready, b + 1)
                    pe.wait_ge(mods_read, 4)
                    if b >= 2:
                        pe.wait_ge(gelu_done, b - 1)
                    for t in range(CHUNK):
                        ins = nc.tensor.transpose(PS[:, 4 + 2 * (b % 2) + t // 4, NCHUNK * (t % 4):NCHUNK * (t % 4) + NCHUNK],
                                                  YC[:, b % 2, t, :], IDENT[0:NCHUNK, 0:NCHUNK])
                    ins.then_inc(yt_ps, 1)
            pe.wait_ge(y_ready, NB)
            for r in range(2):
                ins = nc.tensor.transpose(PS[0:GROUPS, 0, P * r:P * r + P], FINS[:, r, :], IDENT[:, :])
            ins.then_inc(fin_ps, 1)

        def scan_inputs(engine, T, parts, done):
            engine.wait_ge(inc_ps, T + 1)
            for rows, chunks, slots in parts:
                src = PS[rows, 4 * (T % 2):4 * (T % 2) + 4, :].rearrange("p b (g r c) -> p (b g) r c", g=2, r=2)[:, :, :, chunks]
                dst = ST[rows, slots, :, 8 * T:8 * T + 8].rearrange("p c r g -> p g r c")
                if engine is nc.scalar:
                    ins = engine.activation(dst, src, ACT.Copy)
                else:
                    ins = engine.tensor_copy(dst, src)
                ins.then_inc(done, 1)

        def entering(engine, T, parts, done):
            for rows, chunks, slots in parts:
                src = ST[rows, slots, :, 8 * T:8 * T + 8].rearrange("p c r g -> p r g c")
                dst = ENT[rows, :, 8 * T:8 * T + 8, chunks]
                if engine is nc.scalar:
                    ins = engine.activation(dst, src, ACT.Copy)
                else:
                    ins = engine.tensor_copy(dst, src)
                ins.then_inc(done, 1)

        def act_ssm():
            a = nc.scalar
            load_u8(a, 1)
            for T in range(NB):
                scan_inputs(a, T, scan_views()[0:2], inc_a)
            for group in range(GROUPS_IN[2], GROUPS_IN[3]):
                act_rows(group, 7)
            a.wait_ge(scan_done, 1)
            for T in range(NB):
                entering(a, T, entering_views()[0:2], ent_a)
            a.wait_ge(ent_a, 2 * NB)
            a.wait_ge(ent_v, 2 * NB)
            for T in range(NB + 1):
                if T < NB:
                    a.wait_ge(y_ps, T + 1)
                    if T >= 2:
                        a.wait_ge(yt_ps, T - 1)
                    a.activation(YC[:, T % 2].rearrange("c t (g n) -> c g t n", n=GCH),
                                 PSF[0:NCHUNK, 1024 * (T % 2):1024 * (T % 2) + 1024].rearrange("c (g t n) -> c g t n", g=8, n=GCH),
                                 ACT.Copy).then_inc(y_ready, 1)
                if T:
                    a.wait_ge(yt_ps, T)
                    a.activation(by_half(YIN[:, T - 1, :]), halves(4 + 2 * ((T - 1) % 2)), ACT.Gelu_apprx_tanh).then_inc(gelu_done, 1)
            a.wait_ge(fin_ps, 1)
            a.activation(FIN[:, :, :].rearrange("g r n -> g (r n)"), PS[0:GROUPS, 0, 0:2 * P], ACT.Copy).then_inc(fin_ready, 1)
            a.wait_ge(y_ps, NB)
            for m in range(KT):
                a.wait_ge(gelu_done, m + 1)
                a.activation(XH[:, m, :], YIN[:, m, :], ACT.Copy).then_inc(gelu_hi, 1)

        def dve_ssm():
            v = nc.vector
            v.wait_ge(u_out[0], 16 * 4)
            v.wait_ge(u_out[1], 16 * 4)
            v_link(v.memset(ST[:, 0, :, :], 0.0))
            v_link(v.tensor_copy(ST[:, CCH + 1, :, :], H0[:, :, :]))
            for T in range(NB):
                scan_inputs(v, T, scan_views()[2:4], inc_v)
            v.wait_ge(inc_a, 2 * NB)
            v.wait_ge(inc_v, 2 * NB)

            both = ST[:, 0:2 * (CCH + 1)].rearrange("p (a s) r g -> p a s (r g)", s=CCH + 1)

            def run(trips, first, n, count0):
                with loop(v, trips) as i:
                    for u in range(UN):
                        c = count0 + 4 * UN * i + 4 * u
                        s = first + UN * i + u
                        if n == 2:
                            last = both[:, :, bass.ds(s - 1, 1), :].rearrange("p a s (r g) -> p (a s) r g", r=2)
                            now = both[:, :, bass.ds(s, 1), :].rearrange("p a s (r g) -> p (a s) r g", r=2)
                        else:
                            last, now = ST[:, bass.ds(s - 1, 1)], ST[:, bass.ds(s, 1)]
                        shape = [P, n, 2, GROUPS]
                        ar = AR[:, :, :].unsqueeze(1).to_broadcast(shape)
                        ai = AI[:, :, :].unsqueeze(1).to_broadcast(shape)
                        t1, t2 = SC1[:, 0:n], SC2[:, 0:n]
                        v.tensor_tensor(t1, last, ar, ALU.mult).then_inc(scan_t, 1)
                        v.tensor_tensor(t2[:, :, ::-1, :], last, ai, ALU.mult).then_inc(scan_t, 1)
                        v.wait_ge(scan_t, c + 1)
                        v.tensor_tensor(now, now, t1, ALU.add).then_inc(scan_t, 1)
                        v.wait_ge(scan_t, c + 3)
                        v.tensor_tensor(now, now, t2, ALU.add).then_inc(scan_t, 1)
                        v.wait_ge(scan_t, c + 4)
                return count0 + 4 * UN * trips

            UN = 16
            c = run(CCH // UN, 1, 2, 0)
            run((LCH - CCH) // UN, 2 * CCH + 2, 1, c)
            v.tensor_copy(FINS[:, :, :], ST[:, CCH, :, :]).then_inc(scan_done, 1)
            for T in range(NB):
                entering(v, T, entering_views()[2:4], ent_v)
            dve_mods(3)
            for m in range(KT):
                v.wait_ge(gelu_hi, m + 1)
                v.tensor_tensor(XL[:, m, :], YIN[:, m, :], XH[:, m, :].bitcast(F32), ALU.subtract).then_inc(gelu_lo, 1)

        def XBANK(k):
            return 4 + 2 * (k % 2)

        def act_out(a):
            for b in range(5):
                a.wait_ge(out_t, 2 * b + 1)
                if b >= 2:
                    a.wait_ge(out_dma[b % 2], 16 * (b // 2))
                a.activation(OUTN[:, b % 2, 0:512], PS[:, 2 * (b % 4), :], ACT.Copy).then_inc(out_a, 1)

        def dve_out(v):
            for b in range(5):
                v.wait_ge(out_t, 2 * b + 2)
                if b >= 2:
                    v.wait_ge(out_dma[b % 2], 16 * (b // 2))
                nc.vector.tensor_copy(OUTN[:, b % 2, 512:1024], PS[:, 2 * (b % 4) + 1, :]).then_inc(out_v, 1)

        def pe_out(pe, q):
            pe.wait_ge(ln_x, KT * q + KT)
            for b in range(5):
                if b >= 4:
                    pe.wait_ge(out_a, b - 3)
                    pe.wait_ge(out_v, b - 3)
                for k in range(KT):
                    ins = nc.tensor.transpose(PS[:, 2 * (b % 4) + k // 4, P * (k % 4):P * (k % 4) + P],
                                              X[:, k, P * b:P * b + P], IDENT[:, :])
                    if k % 4 == 3:
                        ins.then_inc(out_t, 1)

        block = ctx.enter_context(nc.Block())

        @block.sync
        def _(sp):
            rows = [(0, 0, I["b_ada"].rearrange("l (q p) -> (l q) p", p=P)),
                    (0, 96, I["ln_g"].rearrange("l i (k p) -> (l i k) p", p=P)),
                    (1, 0, I["ln_b"].rearrange("l i (k p) -> (l i k) p", p=P)),
                    (1, 32, I["c_ctx"].rearrange("(k p) -> k p", p=P)),
                    (1, 40, I["c"].rearrange("b (k p) -> (b k) p", p=P)),
                    (1, 48, I["ssm_d"].rearrange("b (k p) -> (b k) p", p=P))]
            for t, r, src in rows:
                sp.dma_start(SV[r:r + src.shape[0], t, :], src).then_inc(small_in, 16)
            sp.dma_start(IDENT[:, :], I["k_ident"]).then_inc(const_in, 16)
            load_ada(sp, 0, ADA_FIRST, dense=0)
            load_turn(sp, "qkv", 0, after_ada=ADA_FIRST)
            load_turn(sp, "qkv", 1)
            load_turn(sp, "qkv", 2)
            load_turn(sp, "wo", 0)
            load_ada(sp, ADA_FIRST, MODQ - ADA_FIRST, dense=ADA_SECOND_AT)
            load_ada(sp, MODQ, ADA_SECOND - MODQ)
            load_turn(sp, "wo", 1, after_ada=ADA_SECOND)
            for name, _n in STAGES[2:]:
                if name == "glu":
                    load_turn(sp, name, 0)
                    load_ada(sp, ADA_SECOND, ADA - ADA_SECOND, dense=ADA_THIRD_AT)
                    load_outputs_matrices(sp)
                    for i in range(1, COUNT[name] // SLOTS):
                        load_turn(sp, name, i, after_ada=ADA if i == 1 else 0)
                else:
                    load_stage(sp, name)
            for b in range(5):
                sp.wait_ge(out_a, b + 1)
                sp.wait_ge(out_v, b + 1)
                dst = O["y_prompt"][0] if b == 0 else O["y_sample"][0][P * (b - 1):P * b, :]
                sp.dma_start(dst, OUTN[:, b % 2, :]).then_inc(out_dma[b % 2], 16)
            sp.wait_ge(out_dma[0], 48)
            sp.wait_ge(out_dma[1], 32)
            sp.wait_ge(kv_out, 32)

        @block.scalar
        def _(a):
            for b in range(5):
                src = I["x_prompt"][0] if b == 0 else I["x_sample"][0][P * (b - 1):P * b, :]
                a.dma_start(XN[:, b, :], src).then_inc(x_in, 16)
            for n in range(4):
                a.dma_start(MASK[:, n, :], I["k_masks"][n]).then_inc(attn_in, 16)
            a.dma_start(ROPE[:, 0, :], I["k_rope"][0]).then_inc(attn_in, 16)
            a.dma_start(ROPE[:, 1, :], I["k_rope"][1]).then_inc(attn_in, 16)
            a.dma_start(CK[:, :], I["cache_k"][0, 0].rearrange("s h d -> s (h d)")).then_inc(attn_in, 16)
            a.dma_start(CV[:, :], I["cache_v"][0, 0].rearrange("s h d -> s (h d)")).then_inc(attn_in, 16)
            a.dma_start(SINK[:, :], I["attn_sink"][0:1, :].to_broadcast([P, HEADS])).then_inc(sink_in, 16)
            a.wait_ge(sv_t, 1)
            a.activation(PV1[:, :], PS[:, 0, 0:P], ACT.Copy).then_inc(pv_ready, 1)
            a.activation(PV2[:, :], PS[:, 1, 0:56], ACT.Copy).then_inc(pv_ready, 1)
            a.wait_ge(pv_ready, 2)
            a.activation(SC[:, :, :].rearrange("p k s -> p s k"), PV2[:, 32:48].rearrange("p (s k) -> p s k", s=2), ACT.Silu).then_inc(silu_c, 1)
            for k in range(KT):
                a.wait_ge(x_t, k + 1)
                a.activation(X[:, k, :], PSF[:, XBANK(k) * 512:XBANK(k) * 512 + TOK], ACT.Copy).then_inc(x_ready, 1)
            for group in range(GROUPS_IN[0]):
                act_rows(group, 3)
            for u in range(SLOTS):
                split_hi(u, u, first=True, ada=ADA_FIRST)
            for k in range(KT):
                act_high(0, k)
            act_split_only("qkv")
            act_attention_start()
            act_attention()
            act_split_only("wo")
            a.wait_ge(kv_out, 32)
            act_norm_modulate(0, 1)
            for ph in range(3):
                act_gated(f"up0{ph}", ACT.Silu)
                act_split_only(f"down0{ph}")
                if ph == 1:
                    act_discretise()
            act_ssm_start()
            over_batches(a, act_prep)
            store_kernels(NB - 1, 1)
            act_norm_modulate(1, 2)
            act_split_only("win")
            act_ssm()
            act_gated("glu", ACT.Sigmoid)
            act_split_only("wout")
            act_norm_modulate(2, 3)
            for ph in range(3):
                act_gated(f"up1{ph}", ACT.Silu)
                act_split_only(f"down1{ph}")
            last = 3
            act_norm(last)
            for k in range(KT):
                act_norm_shift(last, k)
            act_out(a)

        @block.vector
        def _(v):
            nc.vector.memset(MEANW[:, :], 1.0 / D).then_inc(memset_done, 1)
            nc.vector.memset(EPS[:, :], LN_EPS / ALPHA ** 2).then_inc(memset_done, 1)
            v.wait_ge(pv_ready, 2)
            dve_mods(0)
            for u in range(SLOTS):
                split_lo(u, u)
            dve_modulate(0, 0, 0, lambda k: nc.vector.wait_ge(x_ready, k + 1))
            dve_store("qkv", QKVT)
            dve_attention_start()
            dve_attention()
            dve_mods(1)
            dve_mods(2)
            v.wait_ge(kv_out, 32)
            dve_residual("wo", 0, 2)
            dve_norm_modulate(0, 1, 0, 3)
            for ph in range(3):
                dve_gated(f"up0{ph}", PAIRS_BEFORE[f"up0{ph}"])
                dve_residual(f"down0{ph}", 0, 5)
                if ph == 1:
                    dve_discretise()
            dve_ssm_start()
            over_batches(v, dve_prep, vchain, 22)
            dve_kernels(NB - 1, 1)
            for u in range(2):
                v.wait_ge(cp_out[u], 16 * NB)
                v.wait_ge(bt_out[u], 8 * NB)
                v.wait_ge(ks_out[u], 8 * NB)
            dve_norm_modulate(1, 2, 1, 0)
            dve_store("win", UT)
            dve_ssm()
            dve_gated("glu", PAIRS_BEFORE["glu"])
            v.wait_ge(fin_out, 32)
            dve_residual("wout", 1, 2)
            dve_norm_modulate(2, 3, 1, 3)
            for ph in range(3):
                dve_gated(f"up1{ph}", PAIRS_BEFORE[f"up1{ph}"])
                dve_residual(f"down1{ph}", 1, 5)
            last = 3
            dve_norm(last)
            for k in range(KT):
                dve_norm_scale(last, k)
            dve_out(v)

        @block.gpsimd
        def _(g):
            g.wait_ge(att_kv, 4)
            g.dma_start(O["new_k"][0, 0].rearrange("s h d -> s (h d)"), KN[:, :]).then_inc(kv_out, 16)
            g.dma_start(O["new_v"][0, 0].rearrange("s h d -> s (h d)"), VN[:, 0, :]).then_inc(kv_out, 16)
            pool_ada(1)
            pool_ada(2)
            pool_ssm_start(g)
            g.wait_ge(ssm_v, 5)
            g.wait_ge(ssm_a, 11)
            g.wait_ge(ssm_t, 5)

            for T in range(NB):
                pool_prep(T)
            pool_ssm(g)
            g.wait_ge(fin_out, 32)

        @block.tensor
        def _(pe):
            pe.wait_ge(small_in, 96)
            pe.wait_ge(const_in, 16)
            nc.tensor.transpose(PS[:, 0, 0:P], SV[:, 0, :], IDENT[:, :])
            nc.tensor.transpose(PS[:, 1, 0:56], SV[0:56, 1, :], IDENT[0:56, 0:56]).then_inc(sv_t, 1)
            pe.wait_ge(x_in, 80)
            for k in range(KT):
                if k >= 2:
                    pe.wait_ge(x_ready, k - 1)
                for b in range(5):
                    ins = nc.tensor.transpose(PSF[:, XBANK(k) * 512 + P * b:XBANK(k) * 512 + P * b + P],
                                              XN[:, b, P * k:P * k + P], IDENT[:, :])
                ins.then_inc(x_t, 1)
            pe.wait_ge(x_ready, KT)
            pe.wait_ge(silu_c, 1)
            pe_first_mods(pe)
            pe_stage(pe, "qkv", XH, XL, ready=xl_ready)
            pe_attention_start(pe)
            pe_attention(pe)
            pe_mods(pe, 1)
            pe_mods(pe, 2)
            pe.wait_ge(mods_read, 3)
            pe.wait_ge(att_ol, len(STEPS))
            pe_stage(pe, "wo", XH, XL, ready=xl_ready)
            pe_norm(pe, 0)
            pe_ffn(pe, 0, 1)
            pe_ssm_start(pe)
            for T in range(NB):
                pe_prep(T // 2, T % 2, T < 2)
            pe.wait_ge(bt_ready, 4 * NB)
            pe_norm(pe, 1)
            pe_stage(pe, "win", XH, XL, ready=xl_ready, count=2 * KT)
            pe_ssm(pe)
            pe_stage(pe, "glu", XH, XL, ready=gelu_lo)
            pe_stage(pe, "wout", HH, HL, ready=hid_lo, count=PAIRS_BEFORE["glu"])
            pe_norm(pe, 2)
            pe_ffn(pe, 1, 3)
            pe_norm(pe, 3)
            pe_out(pe, 3)


OUTPUTS = {"y_prompt": (1, CTX, D), "y_sample": (1, LAT, D), "new_k": (1, 1, CTX, KV_HEADS, HD),
           "new_v": (1, 1, CTX, KV_HEADS, HD), "new_re": (1, 1, 2, GROUPS, STATE), "new_im": (1, 1, 2, GROUPS, STATE)}


def kernel(**inputs):
    import concourse.bacc as bacc
    from concourse.bass_utils import run_bass_kernel_spmd

    nc = bacc.Bacc("TRN2", target_bir_lowering=False, num_devices=1)
    arrays = {n: np.ascontiguousarray(a) for n, a in inputs.items()}
    arrays.update(host_constants())
    handles = {n: nc.dram_tensor("in_" + n, a.shape, mybir.dt.from_np(a.dtype), kind="ExternalInput").ap()
               for n, a in arrays.items()}
    outs = {n: nc.dram_tensor("out_" + n, s, F32, kind="ExternalOutput").ap() for n, s in OUTPUTS.items()}
    hybrid_step(nc, handles, outs)
    r = run_bass_kernel_spmd(nc, [{"in_" + n: a for n, a in arrays.items()}], core_ids=[0])
    return tuple(r.results[0]["out_" + n] for n in OUTPUTS)
```
